# Optimizing a Trainium2 kernel written in Bass

```python
import math
import jax, jax.numpy as jnp
from jax import lax
import numpy as np

D_MODEL = 1024
BATCH = 1
SEQ = 256
DEPTH = 2

N_MIXERS = 2
N_RWKV_LAYERS = (DEPTH + 1) // 2
N_ATTN_LAYERS = DEPTH // 2
RMS_EPS = 1e-6
N_MOD = 6

RWKV_HEAD = 64
RWKV_HEADS = D_MODEL // RWKV_HEAD
D_DECAY_LORA = 64
D_AAA_LORA = 64
D_GATE_LORA = 128
RWKV_GN_EPS = 64e-5
N_DIRS = 2
N_SHIFT_MIX = 6

ATTN_GROUPS = ((128, 1), (512, 4), (2048, 16))
N_GROUPS = len(ATTN_GROUPS)
ATTN_HEADS = 8
ATTN_HEAD_DIM = D_MODEL // ATTN_HEADS
QKV_WIDTH = N_GROUPS * 3 * ATTN_HEADS * ATTN_HEAD_DIM
Q_BLOCK = 64
NEG_INF = -1e30

N_EXPERT_GROUPS = 4
EXPERTS_PER_GROUP = 8
TOP_K_INNER = 2
D_EXPERT = D_MODEL // 4


def rms_norm(x, g):
    x32 = x.astype(jnp.float32)
    y = x32 * lax.rsqrt(jnp.mean(x32 * x32, axis=-1, keepdims=True) + RMS_EPS)
    return (y * g.astype(jnp.float32)).astype(x.dtype)

def modulate(h, shift, scale):
    return h * (1.0 + scale[:, None, :]) + shift[:, None, :]

def _wkv7_scan(r, w, k, v, a, b, reverse):
    bsz, _, h, n = r.shape

    def step(state, inp):
        r_t, w_t, k_t, v_t, a_t, b_t = inp
        sa = jnp.einsum('bhvk,bhk->bhv', state, a_t)
        state = (state * w_t[:, :, None, :]
                 + sa[:, :, :, None] * b_t[:, :, None, :]
                 + v_t[:, :, :, None] * k_t[:, :, None, :])
        y_t = jnp.einsum('bhvk,bhk->bhv', state, r_t)
        return state, y_t

    s0 = jnp.zeros((bsz, h, n, n), jnp.float32)
    xs = tuple(jnp.moveaxis(t, 1, 0) for t in (r, w, k, v, a, b))
    _, ys = lax.scan(step, s0, xs, reverse=reverse)
    return jnp.moveaxis(ys, 0, 1)

def rwkv7_mix(h, mu, w_rkv, w0, w1, w2, a0, a1, a2, g1, g2, k_k, k_a, r_k, ln_w, ln_b, w_o):
    bsz, s, d = h.shape
    f32 = jnp.float32
    x_prev = jnp.pad(h, ((0, 0), (1, 0), (0, 0)))[:, :-1]
    x_next = jnp.pad(h, ((0, 0), (0, 1), (0, 0)))[:, 1:]
    xx = 0.5 * (x_prev + x_next) - h
    xs = h[:, :, None, :] + xx[:, :, None, :] * mu
    rkv = jnp.einsum('bsjd,jde->bsje', xs[:, :, :3], w_rkv)
    r, k, v = rkv[:, :, 0], rkv[:, :, 1], rkv[:, :, 2]
    xw, xa, xg = xs[:, :, 3], xs[:, :, 4], xs[:, :, 5]

    def lora(xin, A, Bm, act):
        return jnp.einsum('zbsr,zre->zbse', act(jnp.einsum('bsd,zdr->zbsr', xin, A)), Bm)

    w_log = -jax.nn.softplus(-(w0[:, None, None, :] + lora(xw, w1, w2, jnp.tanh)).astype(f32)) - 0.5
    decay = jnp.exp(-jnp.exp(w_log))
    a = jax.nn.sigmoid((a0[:, None, None, :] + lora(xa, a1, a2, lambda t: t)).astype(f32))
    g = lora(xg, g1, g2, jax.nn.sigmoid).astype(f32)

    def heads(t):
        return t.reshape(t.shape[:-1] + (RWKV_HEADS, RWKV_HEAD))

    r32, k32, v32 = (heads(t.astype(f32)) for t in (r, k, v))
    kk = k32 * heads(k_k.astype(f32))
    kk = kk / jnp.maximum(jnp.sqrt(jnp.sum(kk * kk, axis=-1, keepdims=True)), 1e-12)
    a_h, decay_h = heads(a), heads(decay)
    k_dir = k32[None] * (1.0 + (a_h - 1.0) * heads(k_a.astype(f32)))
    b_dir = kk[None] * a_h
    y_f = _wkv7_scan(r32, decay_h[0], k_dir[0], v32, -kk, b_dir[0], reverse=False)
    y_b = _wkv7_scan(r32, decay_h[1], k_dir[1], v32, -kk, b_dir[1], reverse=True)
    y = jnp.stack([y_f, y_b])
    mean = jnp.mean(y, axis=-1, keepdims=True)
    var = jnp.mean(jnp.square(y - mean), axis=-1, keepdims=True)
    y = (y - mean) * lax.rsqrt(var + RWKV_GN_EPS) * heads(ln_w.astype(f32)) + heads(ln_b.astype(f32))
    bonus = jnp.sum(r32[None] * k_dir * r_k.astype(f32), axis=-1, keepdims=True) * v32[None]
    o = jnp.sum(heads(g) * (y + bonus), axis=0).reshape(bsz, s, d)
    return jnp.einsum('bsd,de->bse', o.astype(h.dtype), w_o)

def alibi_slopes(n):
    return 2.0 ** (-8.0 * jnp.arange(1, n + 1, dtype=jnp.float32) / n)

def _dilated_group(q, k, v, slopes, window, dilation):
    bsz, s, h, dh = q.shape
    half = window // (2 * dilation)
    L = s // dilation
    nb = -(-L // Q_BLOCK)
    lp = nb * Q_BLOCK
    kb_len = Q_BLOCK + 2 * half

    def strided(t):
        return t.reshape(bsz, L, dilation, h, dh).transpose(0, 2, 3, 1, 4)

    qd = jnp.pad(strided(q), ((0, 0), (0, 0), (0, 0), (0, lp - L), (0, 0)))
    qd = qd.reshape(bsz, dilation, h, nb, Q_BLOCK, dh)
    pad_kv = ((0, 0), (0, 0), (0, 0), (half, lp - L + half), (0, 0))
    kd = jnp.pad(strided(k), pad_kv)
    vd = jnp.pad(strided(v), pad_kv)
    key_idx = jnp.arange(nb)[:, None] * Q_BLOCK + jnp.arange(kb_len)[None, :]
    kblk = kd[:, :, :, key_idx]
    vblk = vd[:, :, :, key_idx]
    scores = jnp.einsum('brhnqd,brhnkd->brhnqk', qd, kblk) * (dh ** -0.5)
    q_pos = jnp.arange(lp).reshape(nb, Q_BLOCK)
    k_pos = key_idx - half
    rel = jnp.abs(k_pos[:, None, :] - q_pos[:, :, None])
    valid = (rel <= half) & (k_pos[:, None, :] >= 0) & (k_pos[:, None, :] < L)
    alibi = -slopes[:, None, None, None] * (rel * dilation).astype(jnp.float32)
    scores = jnp.where(valid, scores + alibi[None, None], NEG_INF)
    m = jnp.max(scores, axis=-1, keepdims=True)
    e = jnp.exp(scores - m)
    den = jnp.sum(e, axis=-1, keepdims=True)
    o = jnp.einsum('brhnqk,brhnkd->brhnqd', e, vblk) / den
    lse = (m + jnp.log(den))[..., 0]

    def unstride(t):
        t = t.reshape((bsz, dilation, h, lp) + t.shape[5:])[:, :, :, :L]
        t = jnp.moveaxis(t, 3, 1)
        return t.reshape((bsz, s, h) + t.shape[4:])

    return unstride(o), unstride(lse)

def dilated_attention_mix(h, w_qkv, w_o):
    bsz, s, d = h.shape
    qkv = jnp.einsum('bsd,de->bse', h, w_qkv).astype(jnp.float32)
    qkv = qkv.reshape(bsz, s, N_GROUPS, 3, ATTN_HEADS, ATTN_HEAD_DIM)
    slopes = alibi_slopes(N_GROUPS * ATTN_HEADS).reshape(N_GROUPS, ATTN_HEADS)
    outs, lses = [], []
    for gi, (window, dil) in enumerate(ATTN_GROUPS):
        o, lse = _dilated_group(qkv[:, :, gi, 0], qkv[:, :, gi, 1], qkv[:, :, gi, 2], slopes[gi], window, dil)
        outs.append(o)
        lses.append(lse)
    o = jnp.stack(outs)
    alpha = jax.nn.softmax(jnp.stack(lses), axis=0)
    merged = jnp.sum(alpha[..., None] * o, axis=0).reshape(bsz, s, d)
    return jnp.einsum('bsd,de->bse', merged.astype(h.dtype), w_o)

def hier_moe(h, router_g, router_g_b, router_e, router_e_b, w_gate, w_up, w_down):
    bsz, s, d = h.shape
    xt = h.reshape(-1, d)
    f32 = jnp.float32
    g_logits = (xt @ router_g + router_g_b).astype(f32)
    g_prob = jax.nn.softmax(g_logits, axis=-1)
    _, g_top = lax.top_k(g_logits, 1)
    p_group = jnp.take_along_axis(g_prob, g_top, axis=-1)
    e_logits = (jnp.einsum('td,gde->tge', xt, router_e) + router_e_b).astype(f32)
    e_sel = jnp.take_along_axis(e_logits, g_top[:, :, None], axis=1)[:, 0]
    top_v, top_i = lax.top_k(e_sel, TOP_K_INNER)
    top_w = jax.nn.softmax(top_v, axis=-1) * p_group
    inner = jnp.sum(jax.nn.one_hot(top_i, EXPERTS_PER_GROUP, dtype=f32) * top_w[..., None], axis=1)
    gates = jax.nn.one_hot(g_top[:, 0], N_EXPERT_GROUPS, dtype=f32)[:, :, None] * inner[:, None, :]
    out = jnp.zeros((xt.shape[0], d), f32)
    for gi in range(N_EXPERT_GROUPS):
        hid = jax.nn.silu(jnp.einsum('td,edf->tef', xt, w_gate[gi])) * jnp.einsum('td,edf->tef', xt, w_up[gi])
        hid = hid * gates[:, gi, :, None].astype(hid.dtype)
        out = out + jnp.einsum('tef,efd->td', hid, w_down[gi]).astype(f32)
    return out.reshape(bsz, s, d).astype(h.dtype)

def first_inputs(seed: int = 0) -> dict:
    key = jax.random.key(seed)
    ks = iter(jax.random.split(key, 48))
    f32 = jnp.float32
    D, NR, NA = D_MODEL, N_RWKV_LAYERS, N_ATTN_LAYERS
    G, E, F = N_EXPERT_GROUPS, EXPERTS_PER_GROUP, D_EXPERT

    def nrm(shape, scale):
        return jax.random.normal(next(ks), shape, f32) * scale

    def uni(shape, lo, hi):
        return jax.random.uniform(next(ks), shape, f32, minval=lo, maxval=hi)

    return {
        "x": nrm((BATCH, SEQ, D), 1.0),
        "c": nrm((BATCH, D), 1.0),
        "ada_w": nrm((DEPTH, D, N_MOD * D), 0.5 * D ** -0.5),
        "ada_b": nrm((DEPTH, N_MOD * D), 0.01),
        "norm_tm_g": 1.0 + nrm((DEPTH, D), 0.02),
        "norm_cm_g": 1.0 + nrm((DEPTH, D), 0.02),
        "rw_mu": uni((NR, N_SHIFT_MIX, D), 0.0, 1.0),
        "rw_w_rkv": nrm((NR, 3, D, D), D ** -0.5),
        "rw_w0": uni((NR, N_DIRS, D), -4.5, -0.5),
        "rw_w1": nrm((NR, N_DIRS, D, D_DECAY_LORA), D ** -0.5),
        "rw_w2": nrm((NR, N_DIRS, D_DECAY_LORA, D), 0.5 * D_DECAY_LORA ** -0.5),
        "rw_a0": nrm((NR, N_DIRS, D), 0.5),
        "rw_a1": nrm((NR, N_DIRS, D, D_AAA_LORA), D ** -0.5),
        "rw_a2": nrm((NR, N_DIRS, D_AAA_LORA, D), 0.5 * D_AAA_LORA ** -0.5),
        "rw_g1": nrm((NR, N_DIRS, D, D_GATE_LORA), D ** -0.5),
        "rw_g2": nrm((NR, N_DIRS, D_GATE_LORA, D), D_GATE_LORA ** -0.5),
        "rw_k_k": 0.85 + nrm((NR, D), 0.05),
        "rw_k_a": 1.0 + nrm((NR, D), 0.05),
        "rw_r_k": nrm((NR, RWKV_HEADS, RWKV_HEAD), 0.1),
        "rw_ln_w": 1.0 + nrm((NR, D), 0.02),
        "rw_ln_b": nrm((NR, D), 0.01),
        "rw_w_o": nrm((NR, D, D), D ** -0.5),
        "at_w_qkv": nrm((NA, D, QKV_WIDTH), D ** -0.5),
        "at_w_o": nrm((NA, D, D), D ** -0.5),
        "moe_router_g": nrm((DEPTH, D, G), D ** -0.5),
        "moe_router_g_b": nrm((DEPTH, G), 0.01),
        "moe_router_e": nrm((DEPTH, G, D, E), D ** -0.5),
        "moe_router_e_b": nrm((DEPTH, G, E), 0.01),
        "moe_w_gate": nrm((DEPTH, G, E, D, F), D ** -0.5),
        "moe_w_up": nrm((DEPTH, G, E, D, F), D ** -0.5),
        "moe_w_down": nrm((DEPTH, G, E, F, D), F ** -0.5),
        "final_g": 1.0 + nrm((D,), 0.02),
    }

def first_block(x, c, ada_w, ada_b, norm_tm_g, norm_cm_g,
              rw_mu, rw_w_rkv, rw_w0, rw_w1, rw_w2, rw_a0, rw_a1, rw_a2, rw_g1, rw_g2,
              rw_k_k, rw_k_a, rw_r_k, rw_ln_w, rw_ln_b, rw_w_o,
              at_w_qkv, at_w_o,
              moe_router_g, moe_router_g_b, moe_router_e, moe_router_e_b,
              moe_w_gate, moe_w_up, moe_w_down, final_g):
    silu_c = jax.nn.silu(c)
    for i in range(DEPTH):
        mod = silu_c @ ada_w[i] + ada_b[i]
        sh_t, sc_t, ga_t, sh_c, sc_c, ga_c = jnp.split(mod, N_MOD, axis=-1)
        hn = modulate(rms_norm(x, norm_tm_g[i]), sh_t, sc_t)
        j = i // N_MIXERS
        if i % N_MIXERS == 0:
            tm = rwkv7_mix(hn, rw_mu[j], rw_w_rkv[j], rw_w0[j], rw_w1[j], rw_w2[j],
                           rw_a0[j], rw_a1[j], rw_a2[j], rw_g1[j], rw_g2[j],
                           rw_k_k[j], rw_k_a[j], rw_r_k[j], rw_ln_w[j], rw_ln_b[j], rw_w_o[j])
        else:
            tm = dilated_attention_mix(hn, at_w_qkv[j], at_w_o[j])
        x = x + ga_t[:, None, :] * tm
        hn = modulate(rms_norm(x, norm_cm_g[i]), sh_c, sc_c)
        cm = hier_moe(hn, moe_router_g[i], moe_router_g_b[i], moe_router_e[i], moe_router_e_b[i],
                      moe_w_gate[i], moe_w_up[i], moe_w_down[i])
        x = x + ga_c[:, None, :] * cm
    return rms_norm(x, final_g)


PLE_DIM = 256
HEAD_DIM = 64
DIFF_HEADS = 4
DSA_HEADS = 8
IDX_HEADS = 8
IDX_DIM = 64
TOPK_MAX = 256
N_GROUPS_2 = 4
TOP_K_IN_GROUP = 2
D_EXPERT_2 = 256
ROPE_THETA = 500000.0
ROT_DIM = HEAD_DIM // 4
Q_BLOCK_2 = 128
LN_EPS = 1e-5
NEG_INF_2 = -1e30
ALPHA = (2 * DEPTH) ** 0.25
BETA = (8 * DEPTH) ** -0.25
DIFF_WIDTH = DIFF_HEADS * 2 * HEAD_DIM
DSA_WIDTH = DSA_HEADS * HEAD_DIM
SPLIT_SIZES = (DIFF_WIDTH, DIFF_WIDTH, DIFF_WIDTH, DSA_WIDTH, DSA_WIDTH, DSA_WIDTH,
               IDX_HEADS * IDX_DIM, IDX_DIM, IDX_HEADS, D_MODEL, D_MODEL)
W_IN_COLS = sum(SPLIT_SIZES)


def layer_norm(x, g, b):
    xf = x.astype(jnp.float32)
    mu = jnp.mean(xf, axis=-1, keepdims=True)
    var = jnp.mean(jnp.square(xf - mu), axis=-1, keepdims=True)
    y = (xf - mu) * lax.rsqrt(var + LN_EPS)
    return (y * g.astype(jnp.float32) + b.astype(jnp.float32)).astype(x.dtype)

def rms_norm_2(x, g):
    xf = x.astype(jnp.float32)
    y = xf * lax.rsqrt(jnp.mean(jnp.square(xf), axis=-1, keepdims=True) + LN_EPS)
    return (y * g.astype(jnp.float32)).astype(x.dtype)

def rope_tables(positions):
    inv_freq = 1.0 / (ROPE_THETA ** (jnp.arange(0, ROT_DIM, 2, dtype=jnp.float32) / ROT_DIM))
    ang = positions.astype(jnp.float32)[..., None] * inv_freq
    return jnp.cos(ang), jnp.sin(ang)

def partial_rope(t, cos, sin):
    half = ROT_DIM // 2
    shp = cos.shape[:2] + (1,) * (t.ndim - 3) + (half,)
    c = cos.reshape(shp).astype(t.dtype)
    s = sin.reshape(shp).astype(t.dtype)
    x1 = t[..., :half]
    x2 = t[..., half:ROT_DIM]
    return jnp.concatenate([x1 * c - x2 * s, x2 * c + x1 * s, t[..., ROT_DIM:]], axis=-1)

def diff_attention(q, k, v, lam):
    B, S, H, _, dk = q.shape
    nb = S // Q_BLOCK_2
    scale = dk ** -0.5
    qb = q.reshape(B, nb, Q_BLOCK_2, H, 2, dk).swapaxes(0, 1)
    key_pos = jnp.arange(S)

    def one_block(args):
        q_i, b_i = args
        q_pos = b_i * Q_BLOCK_2 + jnp.arange(Q_BLOCK_2)
        s = jnp.einsum('bqhcd,bkhcd->bhcqk', q_i, k).astype(jnp.float32) * scale
        s = jnp.where(key_pos[None, :] <= q_pos[:, None], s, NEG_INF_2)
        pr = jax.nn.softmax(s, axis=-1)
        a = pr[:, :, 0] - lam * pr[:, :, 1]
        return jnp.einsum('bhqk,bkhe->bqhe', a.astype(v.dtype), v)

    o = lax.map(one_block, (qb, jnp.arange(nb)))
    return o.swapaxes(0, 1).reshape(B, S, H, v.shape[-1])

def dsa_attention(q, k, v, q_idx, k_idx, w_idx, topk):
    B, S, H, dh = q.shape
    nb = S // Q_BLOCK_2
    scale = dh ** -0.5
    to_blocks = lambda t: t.reshape((B, nb, Q_BLOCK_2) + t.shape[2:]).swapaxes(0, 1)
    key_pos = jnp.arange(S)

    def one_block(args):
        q_b, qi_b, wi_b, b_i = args
        q_pos = b_i * Q_BLOCK_2 + jnp.arange(Q_BLOCK_2)
        dots = jnp.einsum('bqhd,bsd->bqhs', qi_b, k_idx).astype(jnp.float32) * (IDX_DIM ** -0.5)
        score = jnp.einsum('bqhs,bqh->bqs', jax.nn.relu(dots), wi_b.astype(jnp.float32))
        score = jnp.where(key_pos[None, None, :] <= q_pos[None, :, None], score, NEG_INF_2)
        _, sel = lax.top_k(score, topk)
        valid = sel <= q_pos[None, :, None]
        kg = jax.vmap(lambda kb, ib: kb[ib])(k, sel)
        vg = jax.vmap(lambda vb, ib: vb[ib])(v, sel)
        s = jnp.einsum('bqhd,bqkhd->bhqk', q_b, kg).astype(jnp.float32) * scale
        s = jnp.where(valid[:, None], s, NEG_INF_2)
        pr = jax.nn.softmax(s, axis=-1)
        return jnp.einsum('bhqk,bqkhd->bqhd', pr.astype(v.dtype), vg)

    o = lax.map(one_block, (to_blocks(q), to_blocks(q_idx), to_blocks(w_idx), jnp.arange(nb)))
    return o.swapaxes(0, 1).reshape(B, S, H * dh)

def token_mixers(x, cos, sin, w_in, lam_params, subln_g, w_bd, w_bs, w_o, lam_init):
    B, S, _ = x.shape
    h = x @ w_in
    points = [int(c) for c in np.cumsum(SPLIT_SIZES)[:-1]]
    dq, dkk, dv, sq, sk, sv, iq, ik, iw, ga, gb = jnp.split(h, points, axis=-1)

    dq = partial_rope(dq.reshape(B, S, DIFF_HEADS, 2, HEAD_DIM), cos, sin)
    dkk = partial_rope(dkk.reshape(B, S, DIFF_HEADS, 2, HEAD_DIM), cos, sin)
    dv = dv.reshape(B, S, DIFF_HEADS, 2 * HEAD_DIM)
    lp = lam_params.astype(jnp.float32)
    lam = jnp.exp(jnp.sum(lp[0] * lp[1])) - jnp.exp(jnp.sum(lp[2] * lp[3])) + lam_init
    ya = diff_attention(dq, dkk, dv, lam)
    ya = (rms_norm_2(ya, subln_g) * (1.0 - lam_init)).reshape(B, S, DIFF_WIDTH)

    sq = partial_rope(sq.reshape(B, S, DSA_HEADS, HEAD_DIM), cos, sin)
    sk = partial_rope(sk.reshape(B, S, DSA_HEADS, HEAD_DIM), cos, sin)
    sv = sv.reshape(B, S, DSA_HEADS, HEAD_DIM)
    iq = partial_rope(iq.reshape(B, S, IDX_HEADS, IDX_DIM), cos, sin)
    ik = partial_rope(ik, cos, sin)
    iw = iw * (IDX_HEADS ** -0.5)
    topk = min(TOPK_MAX, S // 4)
    yb = dsa_attention(sq, sk, sv, iq, ik, iw, topk)

    merged = jax.nn.sigmoid(ga) * (ya @ w_bd) + jax.nn.sigmoid(gb) * (yb @ w_bs)
    return merged @ w_o

def hierarchical_moe(x, w_rg, b_rg, w_re, b_re, w_g, w_u, w_d):
    B, S, D = x.shape
    xt = x.reshape(-1, D)
    n = xt.shape[0]
    g_prob = jax.nn.softmax((xt @ w_rg).astype(jnp.float32) + b_rg.astype(jnp.float32), axis=-1)
    g_val, g_idx = lax.top_k(g_prob, 1)
    e_logit = ((xt @ w_re).astype(jnp.float32) + b_re.astype(jnp.float32)).reshape(n, N_GROUPS_2, EXPERTS_PER_GROUP)
    e_logit = jnp.take_along_axis(e_logit, g_idx[:, :, None], axis=1)[:, 0]
    e_prob = jax.nn.softmax(e_logit, axis=-1)
    e_val, e_idx = lax.top_k(e_prob, TOP_K_IN_GROUP)
    e_val = e_val / jnp.sum(e_val, axis=-1, keepdims=True)
    within = jnp.sum(jax.nn.one_hot(e_idx, EXPERTS_PER_GROUP, dtype=jnp.float32) * e_val[..., None], axis=1)
    comb = jax.nn.one_hot(g_idx[:, 0], N_GROUPS_2, dtype=jnp.float32)[:, :, None] * (g_val * within)[:, None, :]
    y = jnp.zeros_like(xt)
    for g in range(N_GROUPS_2):
        hg = jax.nn.silu(jnp.einsum('nd,edf->nef', xt, w_g[g])) * jnp.einsum('nd,edf->nef', xt, w_u[g])
        y = y + jnp.einsum('nef,efd->nd', hg * comb[:, g, :, None].astype(hg.dtype), w_d[g])
    return y.reshape(B, S, D)

def second_inputs(seed: int = 0) -> dict:
    key = jax.random.key(seed)
    ks = jax.random.split(key, 24)
    L, D = DEPTH, D_MODEL
    G, E, F = N_GROUPS_2, EXPERTS_PER_GROUP, D_EXPERT_2
    nrm = lambda k, shape, scale: jax.random.normal(k, shape, jnp.float32) * scale
    return {
        'x': nrm(ks[0], (BATCH, SEQ, D), 1.0),
        'p': nrm(ks[1], (L, BATCH, SEQ, PLE_DIM), 1.0),
        'positions': jnp.broadcast_to(jnp.arange(SEQ, dtype=jnp.int32), (BATCH, SEQ)),
        'w_in': nrm(ks[2], (L, D, W_IN_COLS), D ** -0.5),
        'diff_lambda': nrm(ks[3], (L, 4, HEAD_DIM), 0.1),
        'diff_subln_g': 1.0 + nrm(ks[4], (L, 2 * HEAD_DIM), 0.01),
        'w_branch_diff': nrm(ks[5], (L, DIFF_WIDTH, D), DIFF_WIDTH ** -0.5),
        'w_branch_dsa': nrm(ks[6], (L, DSA_WIDTH, D), DSA_WIDTH ** -0.5),
        'w_out': nrm(ks[7], (L, D, D), BETA * D ** -0.5),
        'ln1_g': 1.0 + nrm(ks[8], (L, D), 0.01),
        'ln1_b': nrm(ks[9], (L, D), 0.01),
        'w_route_group': nrm(ks[10], (L, D, G), D ** -0.5),
        'b_route_group': nrm(ks[11], (L, G), 0.01),
        'w_route_expert': nrm(ks[12], (L, D, G * E), D ** -0.5),
        'b_route_expert': nrm(ks[13], (L, G * E), 0.01),
        'w_exp_gate': nrm(ks[14], (L, G, E, D, F), D ** -0.5),
        'w_exp_up': nrm(ks[15], (L, G, E, D, F), D ** -0.5),
        'w_exp_down': nrm(ks[16], (L, G, E, F, D), BETA * F ** -0.5),
        'w_ple': nrm(ks[17], (L, PLE_DIM, D), BETA * PLE_DIM ** -0.5),
        'w_ple_gate': nrm(ks[18], (L, D, D), D ** -0.5),
        'ln2_g': 1.0 + nrm(ks[19], (L, D), 0.01),
        'ln2_b': nrm(ks[20], (L, D), 0.01),
    }

def second_block(x, p, positions, w_in, diff_lambda, diff_subln_g, w_branch_diff, w_branch_dsa,
              w_out, ln1_g, ln1_b, w_route_group, b_route_group, w_route_expert, b_route_expert,
              w_exp_gate, w_exp_up, w_exp_down, w_ple, w_ple_gate, ln2_g, ln2_b):
    cos, sin = rope_tables(positions)
    for i in range(DEPTH):
        lam_init = 0.8 - 0.6 * math.exp(-0.3 * i)
        mix = token_mixers(x, cos, sin, w_in[i], diff_lambda[i], diff_subln_g[i],
                           w_branch_diff[i], w_branch_dsa[i], w_out[i], lam_init)
        x = layer_norm(ALPHA * x + mix, ln1_g[i], ln1_b[i])
        ffn = hierarchical_moe(x, w_route_group[i], b_route_group[i], w_route_expert[i],
                               b_route_expert[i], w_exp_gate[i], w_exp_up[i], w_exp_down[i])
        ple = jax.nn.sigmoid(x @ w_ple_gate[i]) * (p[i] @ w_ple[i])
        x = layer_norm(ALPHA * x + ffn + ple, ln2_g[i], ln2_b[i])
    return x


def setup_inputs(seed=0):
    out = dict(first_inputs(seed))
    for name, value in second_inputs(seed + 1).items():
        if name != "x":
            out[name + "_2"] = value
    return out


def reference(
    x, c, ada_w, ada_b, norm_tm_g, norm_cm_g, rw_mu, rw_w_rkv, rw_w0, rw_w1, rw_w2, rw_a0,
    rw_a1, rw_a2, rw_g1, rw_g2, rw_k_k, rw_k_a, rw_r_k, rw_ln_w, rw_ln_b, rw_w_o, at_w_qkv,
    at_w_o, moe_router_g, moe_router_g_b, moe_router_e, moe_router_e_b, moe_w_gate, moe_w_up,
    moe_w_down, final_g, p_2, positions_2, w_in_2, diff_lambda_2, diff_subln_g_2,
    w_branch_diff_2, w_branch_dsa_2, w_out_2, ln1_g_2, ln1_b_2, w_route_group_2,
    b_route_group_2, w_route_expert_2, b_route_expert_2, w_exp_gate_2, w_exp_up_2, w_exp_down_2,
    w_ple_2, w_ple_gate_2, ln2_g_2, ln2_b_2,
):
    x = first_block(
        x, c, ada_w, ada_b, norm_tm_g, norm_cm_g, rw_mu, rw_w_rkv, rw_w0, rw_w1, rw_w2, rw_a0,
        rw_a1, rw_a2, rw_g1, rw_g2, rw_k_k, rw_k_a, rw_r_k, rw_ln_w, rw_ln_b, rw_w_o, at_w_qkv,
        at_w_o, moe_router_g, moe_router_g_b, moe_router_e, moe_router_e_b, moe_w_gate,
        moe_w_up, moe_w_down, final_g,
    )
    return second_block(
        x, p_2, positions_2, w_in_2, diff_lambda_2, diff_subln_g_2, w_branch_diff_2,
        w_branch_dsa_2, w_out_2, ln1_g_2, ln1_b_2, w_route_group_2, b_route_group_2,
        w_route_expert_2, b_route_expert_2, w_exp_gate_2, w_exp_up_2, w_exp_down_2, w_ple_2,
        w_ple_gate_2, ln2_g_2, ln2_b_2,
    )


_drawn_inputs = setup_inputs


def setup_inputs(seed=0):
    import zlib

    import numpy as np

    out = dict(_drawn_inputs(seed))
    spreads = {}
    factors = {'norm_tm_g': 3.221,
     'rw_ln_w': 4.915,
     'rw_ln_b': 5.738,
     'moe_router_g_b': 4.126,
     'moe_router_e_b': 4.551,
     'diff_subln_g_2': 8.0,
     'ln1_g_2': 3.022,
     'ln1_b_2': 2.935,
     'b_route_group_2': 8.0,
     'b_route_expert_2': 6.328,
     'ln2_g_2': 3.303,
     'ln2_b_2': 3.112}
    for name, (base, spread) in spreads.items():
        noise = np.random.default_rng([zlib.crc32(name.encode()), seed]).standard_normal(out[name].shape)
        drawn = base * np.exp(spread * noise) if base else spread * noise
        out[name] = __import__('jax').numpy.asarray(drawn.astype(out[name].dtype))
    for name, factor in factors.items():
        out[name] = (out[name] * factor).astype(out[name].dtype)
    return out
```

```python
import math
from contextlib import ExitStack

import numpy as np
import concourse.bass as bass
from concourse import mybir

F32 = mybir.dt.float32
I32 = mybir.dt.int32
ALU = mybir.AluOpType
ACT = mybir.ActivationFunctionType
X = mybir.AxisListType.X
MUL, ADD, SUB, MAX = ALU.mult, ALU.add, ALU.subtract, ALU.max

P = 128
T, D = 256, 1024
TILES = T // P
K8 = D // P
DEPTH = 2
SLOTS, SLOT = 12, 2048
HALF = 512

HEADS, HN = 16, 64
CH = 64
RMS_EPS, GN_EPS, LN_EPS = 1e-6, 64e-5, 1e-5

GROUPS = ((128, 1), (512, 4), (2048, 16))
AH, ADH = 8, 128

N_GROUPS, PER_GROUP = 4, 8
EXPERTS = N_GROUPS * PER_GROUP
F = 256
UNROLL = 4

SEG = dict(dq=0, dk=512, dv=1024, sq=1536, sk=2048, sv=2560, iq=3072, ik=3584, iw=3648, ga=3656, gb=4680)
W_IN = 5704
DH, SH = 4, 8
TOPK = min(256, T // 4)
ROT = 16
THETA = 500000.0
ALPHA = (2 * DEPTH) ** 0.25
BIG = 1e30


class Signal:

    def __init__(self, sem):
        self.sem, self.base = sem, 0

    def at(self, n):
        return self.base + n

    def close(self, n):
        self.base += n


class Chain:

    def __init__(self, sem):
        self.sem, self.n = sem, 0

    def mark(self, ins):
        self.n += 1
        ins.then_inc(self.sem, 1)

    def link(self, eng, ins):
        self.mark(ins)
        eng.wait_ge(self.sem, self.n)


class Carver:

    def __init__(self, buf, width, start=0):
        self.buf, self.width, self.at = buf, width, start

    def take(self, n):
        assert self.at + n <= self.width, (self.at + n, self.width)
        v = self.buf[:, self.at:self.at + n]
        self.at += n
        return v


class Core:
    pass


def plan_streams(a):

    def jobs(w, spans):
        rows = w.shape[0] // P
        v = w.rearrange("(p k) n -> p k n", k=rows)
        return [v[:, 2 * u:2 * u + 2, c0:c0 + n] for c0, n in spans for u in range(rows // 2)]

    def wide(n):
        return [(c, min(D, n - c)) for c in range(0, n, D)]

    def moe(i, gate, up, down):
        g = gate[i].rearrange("g e (p k) f -> (g e) p (k f)", k=K8)
        u = up[i].rearrange("g e (p k) f -> (g e) p (k f)", k=K8)
        d = down[i].rearrange("g e (p j) n -> (g e) p (j n)", j=2)
        order = [g[0], u[0]]
        for e in range(EXPERTS - 1):
            order += [g[e + 1], u[e + 1], d[e]]
        return order + [d[EXPERTS - 1]]

    plan = []
    for i in range(DEPTH):
        plan.append((f"ada{i}", jobs(a["ada_w"][i], wide(6 * D))))
        if i == 0:
            for j in range(3):
                plan.append((f"rkv{j}", jobs(a["rw_w_rkv"][0, j], wide(D))))
            plan.append(("scratch", []))
            plan.append(("rwo", jobs(a["rw_w_o"][0], wide(D))))
        else:
            plan.append(("qkv", jobs(a["at_w_qkv"][0], wide(9 * D))))
            plan.append(("scratch", []))
            plan.append(("awo", jobs(a["at_w_o"][0], wide(D))))
        plan.append((f"moe{i}", moe(i, a["moe_w_gate"], a["moe_w_up"], a["moe_w_down"])))
    for i in range(DEPTH):
        spans = [(0, D), (D, D), (2 * D, D), (3 * D, SEG["ga"] - 3 * D), (SEG["ga"], D), (SEG["gb"], D)]
        plan.append((f"win{i}", jobs(a["w_in_2"][i], spans)))
        plan.append(("scratch", []))
        plan.append((f"wbd{i}", jobs(a["w_branch_diff_2"][i], wide(D))))
        plan.append((f"wbs{i}", jobs(a["w_branch_dsa_2"][i], wide(D))))
        plan.append((f"wout{i}", jobs(a["w_out_2"][i], wide(D))))
        plan.append((f"pleg{i}", jobs(a["w_ple_gate_2"][i], wide(D))))
        plan.append((f"ple{i}", jobs(a["w_ple_2"][i], wide(D))))
        plan.append((f"moe{DEPTH + i}", moe(i, a["w_exp_gate_2"], a["w_exp_up_2"], a["w_exp_down_2"])))
    return plan


def make_core(nc, ctx, a):
    k = Core()
    k.nc, k.a = nc, a

    def sb(name, shape, dt=F32):
        return ctx.enter_context(nc.sbuf_tensor(name, shape, dt))

    k.arena = sb("arena", [P, SLOTS * SLOT])
    k.region_w = 21248
    k.region = sb("region", [P, k.region_w])
    k.x = sb("x_tokens", [P, TILES, D])
    k.xT = sb("x_features", [P, K8, T])
    k.gate_row = sb("gate_rows", [P, 2, D])
    k.mod = sb("mod_columns", [P, 6, K8])
    k.scale_col = sb("scale_columns", [P, 2, K8])
    k.ident = sb("identity", [P, P])
    k.desc = sb("descending", [P, PER_GROUP])
    k.stat = sb("statistics", [P, 64])
    k.cos = sb("cos", [P, TILES, ROT // 2])
    k.sin = sb("sin", [P, TILES, ROT // 2])
    k.ps = ctx.enter_context(nc.psum_tensor("ps", [P, 8, HALF], F32))

    def sem(name):
        return ctx.enter_context(nc.semaphore(name))

    k.landed = [sem(f"slot_landed{s}") for s in range(SLOTS)]
    k.used = sem("units_used")
    k.vec_chain = Chain(sem("vector_chain"))
    k.act_chain = Chain(sem("scalar_chain"))
    k.pool_chain = Chain(sem("gpsimd_chain"))
    k.small_landed, k.stored = Signal(sem("small_landed")), Signal(sem("stored"))
    k.pe_done, k.vec_done = Signal(sem("pe_done")), Signal(sem("vec_done"))
    k.act_done, k.pool_done = Signal(sem("act_done")), Signal(sem("pool_done"))
    k.pass_mid = Signal(sem("product_done"))
    k.turn_joint, k.turn_tile0, k.turn_tile1 = (Signal(sem(f"turn_{n}")) for n in ("joint", "tile0", "tile1"))
    k.plan, k.starts, k.stops, n = [], {}, [], 0
    for name, units in plan_streams(a):
        if name == "scratch":
            k.stops.append(n)
            continue
        k.starts[name] = n
        k.plan += units
        n += len(units)
    k.issued = 0
    return k


def issue(k, sp, upto):
    for n in range(k.issued, min(upto, len(k.plan))):
        src = k.plan[n]
        size = int(np.prod(src.shape[1:]))
        at = (n % SLOTS) * SLOT
        dst = k.arena[:, at:at + size]
        if len(src.shape) == 3:
            dst = dst.rearrange("p (k n) -> p k n", k=src.shape[1])
        if n >= SLOTS:
            sp.wait_ge(k.used, n - SLOTS + 1)
        sp.dma_start(dst, src).then_inc(k.landed[n % SLOTS], 16)
    k.issued = max(k.issued, min(upto, len(k.plan)))


def ahead(k, sp, end):
    stop = min([s for s in k.stops if s >= end], default=len(k.plan))
    issue(k, sp, end)
    issue(k, sp, min(end + SLOTS, stop))


def landed(k, pe, n):
    pe.wait_ge(k.landed[n % SLOTS], 16 * (n // SLOTS + 1))


def used_up(k, eng, n):
    eng.wait_ge(k.used, n)


def unit(k, n, width):
    at = (n % SLOTS) * SLOT
    return k.arena[:, at:at + 2 * width].rearrange("p (k n) -> p k n", k=2)


def bank(k, b, n=1):
    return k.ps[:, b:b + n, :].rearrange("p b n -> p (b n)")


def project_tokens(k, pe, n0, xT, rows, width, set_):
    halves = [(0, min(HALF, width))] + ([(HALF, width - HALF)] if width > HALF else [])
    for u in range(rows // 2):
        landed(k, pe, n0 + u)
        w = unit(k, n0 + u, width)
        for kk in range(2):
            s = 2 * u + kk
            for tile in range(TILES):
                for h, (c0, n) in enumerate(halves):
                    mm = pe.matmul(k.ps[:, set_ * 4 + tile * 2 + h, 0:n], xT[:, s, tile * P:(tile + 1) * P],
                                   w[:, kk, c0:c0 + n], start=(s == 0), stop=(s == rows - 1))
        mm.then_inc(k.used, 1)


def project_features(k, pe, n0, xT, rows, set_):
    for u in range(rows // 2):
        landed(k, pe, n0 + u)
        w = unit(k, n0 + u, D)
        for kk in range(2):
            s = 2 * u + kk
            for m in range(K8):
                mm = pe.matmul(k.ps[:, set_ * 4 + m // 2, (m % 2) * T:(m % 2 + 1) * T],
                               w[:, kk, m * P:(m + 1) * P], xT[:, s, :],
                               start=(s == 0 and m % 2 == 0), stop=(s == rows - 1), skip_group_check=True)
        mm.then_inc(k.used, 1)


def setup_phase(k):
    a = k.a
    c = Carver(k.region, k.region_w)
    pos = c.take(TILES).bitcast(I32)
    posf = c.take(TILES)
    freq = c.take(ROT // 2)
    ang, turns, red = (c.take(TILES * ROT // 2).rearrange("p (t r) -> p t r", t=TILES) for _ in range(3))
    inv = (np.float32(1.0) / np.float32(THETA) ** (np.arange(0, ROT, 2, dtype=np.float32) / np.float32(ROT)))
    two_pi = 2 * math.pi
    hi = float(np.float32(6.28125))
    mid = float(np.float32(np.round((two_pi - hi) * 2 ** 18) / 2 ** 18))
    lo = float(np.float32(two_pi - hi - mid))
    ROUND = float(np.float32(1.5 * 2 ** 23))

    with k.nc.Block() as block:
        @block.sync
        def _(sp):
            sp.dma_start(k.x[:, :, :], a["x"].rearrange("b (t p) d -> p (b t) d", p=P)).then_inc(k.small_landed.sem, 16)
            sp.dma_start(pos, a["positions_2"].rearrange("b (t p) -> p (b t)", p=P),
                         allow_slow_non_contiguous=True).then_inc(k.small_landed.sem, 16)
            ahead(k, sp, 0)

        @block.gpsimd
        def _(pool):
            link = lambda ins: k.pool_chain.link(pool, ins)
            link(pool.memset(k.ident[:, :], 0.0))
            link(pool.affine_select(out=k.ident[:, :], in_=k.ident[:, :], pattern=[[-1, P]], compare_op=ALU.not_equal,
                                    fill=1.0, base=0, channel_multiplier=1))

        @block.vector
        def _(vec):
            link = lambda ins: k.vec_chain.link(vec, ins)
            for j in range(PER_GROUP):
                k.vec_chain.mark(vec.memset(k.desc[:, j:j + 1], float(PER_GROUP - j)))
            for j in range(ROT // 2):
                k.vec_chain.mark(vec.memset(freq[:, j:j + 1], float(inv[j])))
            vec.wait_ge(k.small_landed.sem, k.small_landed.at(32))
            link(vec.tensor_copy(posf, pos))
            f3 = freq.rearrange("p (a r) -> p a r", a=1).to_broadcast([P, TILES, ROT // 2])
            p3 = posf.rearrange("p (t a) -> p t a", a=1).to_broadcast([P, TILES, ROT // 2])
            link(vec.tensor_tensor(ang, p3, f3, MUL))
            link(vec.tensor_scalar(turns, ang, 1.0 / two_pi, None, MUL))
            link(vec.tensor_scalar(turns, turns, ROUND, -ROUND, ADD, ADD))
            link(vec.scalar_tensor_tensor(out=red, in0=turns, scalar=-hi, in1=ang, op0=MUL, op1=ADD))
            link(vec.scalar_tensor_tensor(out=red, in0=turns, scalar=-mid, in1=red, op0=MUL, op1=ADD))
            link(vec.scalar_tensor_tensor(out=red, in0=turns, scalar=-lo, in1=red, op0=MUL, op1=ADD))
            vec.sem_inc(k.vec_done.sem, 1)
            vec.wait_ge(k.act_done.sem, k.act_done.at(1))
            link(vec.tensor_tensor(k.cos[:, :, :], ang, ang, MUL))
            link(vec.tensor_scalar(k.cos[:, :, :], k.cos[:, :, :], -2.0, 1.0, MUL, ADD))

        @block.scalar
        def _(act):
            link = lambda ins: k.act_chain.link(act, ins)
            act.wait_ge(k.vec_done.sem, k.vec_done.at(1))
            link(act.activation(k.sin[:, :, :], red, ACT.Sin))
            link(act.activation(ang, red, ACT.Sin, scale=0.5))
            act.sem_inc(k.act_done.sem, 1)
    k.small_landed.close(32)
    k.vec_done.close(1)
    k.act_done.close(1)


def ada_phase(k, i):
    a = k.a
    n0 = k.starts[f"ada{i}"]
    c = Carver(k.region, k.region_w)
    ccol, silu = c.take(K8), c.take(K8)
    bias = c.take(6 * K8).rearrange("p (j k) -> p j k", j=6)
    gain = c.take(2 * K8).rearrange("p (j k) -> p j k", j=2)
    diag = c.take(2 * D).rearrange("p (g k m) -> p g k m", g=2, k=K8)
    ones = c.take(P)
    small = (
        (ccol, a["c"].rearrange("b (p k) -> p (b k)", k=K8)),
        (bias, a["ada_b"][i].rearrange("(j p k) -> p j k", p=P, k=K8)),
        (gain[:, 0, :], a["norm_tm_g"][i].rearrange("(p k) -> p k", k=K8)),
        (gain[:, 1, :], a["norm_cm_g"][i].rearrange("(p k) -> p k", k=K8)),
    )
    with k.nc.Block() as block:
        @block.sync
        def _(sp):
            ahead(k, sp, n0 + 24)

        @block.scalar
        def _(act):
            for dst, src in small:
                act.dma_start(dst, src).then_inc(k.small_landed.sem, 16)
            act.wait_ge(k.small_landed.sem, k.small_landed.at(64))
            act.activation(silu, ccol, ACT.Silu).then_inc(k.act_done.sem, 1)
            act.wait_ge(k.pe_done.sem, k.pe_done.at(1))
            act.activation(k.gate_row[:, :, :], k.ps[:, 1:5, :].rearrange("p (g h) n -> p g (h n)", g=2),
                           ACT.Copy).then_inc(k.act_done.sem, 1)

        @block.tensor
        def _(pe):
            pe.wait_ge(k.act_done.sem, k.act_done.at(1))
            for j in range(6):
                for u in range(4):
                    landed(k, pe, n0 + 4 * j + u)
                    w = unit(k, n0 + 4 * j + u, D)
                    for kk in range(2):
                        s = 2 * u + kk
                        for f in range(K8):
                            mm = pe.matmul(k.ps[:, 0, j * K8 + f:j * K8 + f + 1], w[:, kk, f:D:K8], silu[:, s:s + 1],
                                           start=(j == 0 and s == 0 and f == 0), stop=(s == K8 - 1),
                                           skip_group_check=True)
                    mm.then_inc(k.used, 1)
            pe.wait_ge(k.vec_done.sem, k.vec_done.at(1))
            for g in range(2):
                for h in range(2):
                    mm = pe.matmul(k.ps[:, 1 + 2 * g + h, :], ones,
                                   diag[:, g, :, h * 64:(h + 1) * 64].rearrange("p k m -> p m k"),
                                   start=True, stop=True)
            mm.then_inc(k.pe_done.sem, 1)

        @block.vector
        def _(vec):
            link = lambda ins: k.vec_chain.link(vec, ins)
            k.vec_chain.mark(vec.memset(ones, 1.0))
            vec.wait_ge(k.small_landed.sem, k.small_landed.at(64))
            used_up(k, vec, n0 + 24)
            link(vec.tensor_tensor(k.mod[:, :, :], k.ps[:, 0, 0:6 * K8].rearrange("p (j k) -> p j k", j=6), bias, ADD))
            for g in range(2):
                k.vec_chain.mark(vec.tensor_tensor(
                    diag[:, g], k.ident[:, :].rearrange("p (a m) -> p a m", a=1).to_broadcast([P, K8, P]),
                    k.mod[:, 3 * g + 2, :].rearrange("p (k a) -> p k a", a=1).to_broadcast([P, K8, P]), MUL))
                link(vec.scalar_tensor_tensor(out=k.scale_col[:, g, :], in0=k.mod[:, 3 * g + 1, :], scalar=1.0,
                                              in1=gain[:, g, :], op0=ADD, op1=MUL))
            vec.sem_inc(k.vec_done.sem, 1)
    k.small_landed.close(64)
    k.act_done.close(2)
    k.pe_done.close(1)
    k.vec_done.close(1)


def transposes(k, pe, src, rows, bank0, cols=None):
    for s in range(rows):
        for tile in range(TILES):
            mm = pe.transpose(k.ps[:, bank0 + s // 2, (s % 2) * T + tile * P:(s % 2) * T + (tile + 1) * P],
                              src[:, tile, s:rows * P:rows], k.ident[:, :])
    return mm


def to_features_phase(k, src, dst, rows, end, norm=None, copy_out=None):
    c = Carver(k.region, k.region_w, k.region_w - TILES * D)
    xn = c.take(TILES * D).rearrange("p (t d) -> p t d", t=TILES)
    ss = k.stat[:, 0:TILES]
    rms = k.stat[:, TILES:2 * TILES]
    with k.nc.Block() as block:
        @block.sync
        def _(sp):
            ahead(k, sp, end)

        if norm is not None:
            @block.scalar
            def _(act):
                act.wait_ge(k.vec_done.sem, k.vec_done.at(1))
                act.activation(rms, rms, ACT.Sqrt).then_inc(k.act_done.sem, 1)

        @block.tensor
        def _(pe):
            if norm is not None:
                pe.wait_ge(k.vec_done.sem, k.vec_done.at(2))
            transposes(k, pe, src if norm is None else xn, rows, 0).then_inc(k.pe_done.sem, 1)

        @block.vector
        def _(vec):
            link = lambda ins: k.vec_chain.link(vec, ins)
            if norm is not None:
                for tile in range(TILES):
                    k.vec_chain.mark(vec.tensor_tensor_reduce(xn[:, tile], src[:, tile], src[:, tile], 1.0, 0.0, MUL,
                                                              ADD, ss[:, tile:tile + 1]))
                vec.wait_ge(k.vec_chain.sem, k.vec_chain.n)
                link(vec.tensor_scalar(rms, ss, 1.0 / D, RMS_EPS, MUL, ADD))
                vec.sem_inc(k.vec_done.sem, 1)
                vec.wait_ge(k.act_done.sem, k.act_done.at(1))
                link(vec.reciprocal(rms, rms))
                for tile in range(TILES):
                    link(vec.tensor_scalar(xn[:, tile], src[:, tile], rms[:, tile:tile + 1], None, MUL))
                vec.sem_inc(k.vec_done.sem, 1)
            vec.wait_ge(k.pe_done.sem, k.pe_done.at(1))
            for s in range(rows):
                t = k.ps[:, s // 2, (s % 2) * T:(s % 2 + 1) * T]
                if norm is None:
                    k.vec_chain.mark(vec.tensor_copy(dst[:, s, :], t))
                else:
                    k.vec_chain.mark(vec.tensor_scalar(dst[:, s, :], t, k.scale_col[:, norm, s:s + 1],
                                                       k.mod[:, 3 * norm, s:s + 1], MUL, ADD))
            vec.wait_ge(k.vec_chain.sem, k.vec_chain.n)
    k.pe_done.close(1)
    if norm is not None:
        k.vec_done.close(2)
        k.act_done.close(1)


def residual_phase(k, name, xT, which):
    n0 = k.starts[name]
    with k.nc.Block() as block:
        @block.sync
        def _(sp):
            ahead(k, sp, n0 + 4)

        @block.tensor
        def _(pe):
            project_tokens(k, pe, n0, xT, K8, D, 0)

        @block.vector
        def _(vec):
            link = lambda ins: k.vec_chain.link(vec, ins)
            used_up(k, vec, n0 + 4)
            add_gated(k, vec, link, which, k.region[:, 0:TILES * D])


def add_gated(k, vec, link, which, scratch):
    tmp = scratch.rearrange("p (t d) -> p t d", t=TILES)
    link(vec.tensor_tensor(tmp, bank(k, 0, 4).rearrange("p (t d) -> p t d", t=TILES),
                           k.gate_row[:, which:which + 1, :].to_broadcast([P, TILES, D]), MUL))
    link(vec.tensor_tensor(k.x[:, :, :], k.x[:, :, :], tmp, ADD))


def v3(ap, a, n):
    return ap.rearrange("p (a n) -> p a n", a=a)


def rwkv_buffers(k):
    c = Carver(k.region, k.region_w)
    b = Core()
    b.r, b.k, b.v = (v3(c.take(TILES * D), TILES, D) for _ in range(3))
    b.tw, b.ta = c.take(T), c.take(T)
    b.tg = v3(c.take(2 * T), 2, T)
    b.end = c.at
    return b


def rwkv_project_phase(k, b):
    a = k.a
    n0 = k.starts["rkv0"]
    c = Carver(k.region, k.region_w, b.end)
    xx = v3(c.take(K8 * T), K8, T)
    xs = c.take(2 * K8 * T).rearrange("p (b k t) -> p b k t", b=2, k=K8)
    mu = v3(c.take(6 * K8), 6, K8)
    w1 = c.take(K8 * P).rearrange("p (k z r) -> p k z r", k=K8, z=2)
    a1 = c.take(K8 * P).rearrange("p (k z r) -> p k z r", k=K8, z=2)
    g1 = c.take(K8 * 2 * P).rearrange("p (k z r) -> p k z r", k=K8, z=2)
    small = [(mu, a["rw_mu"][0].rearrange("j (p k) -> p j k", k=K8))]
    for z in range(2):
        small += [(w1[:, :, z, :], a["rw_w1"][0, z].rearrange("(p k) r -> p k r", k=K8)),
                  (a1[:, :, z, :], a["rw_a1"][0, z].rearrange("(p k) r -> p k r", k=K8)),
                  (g1[:, :, z, :], a["rw_g1"][0, z].rearrange("(p k) r -> p k r", k=K8))]
    n_small = 16 * len(small)
    with k.nc.Block() as block:
        @block.sync
        def _(sp):
            ahead(k, sp, n0 + 12)

        @block.scalar
        def _(act):
            for dst, src in small:
                act.dma_start(dst, src).then_inc(k.small_landed.sem, 16)
            for j, dst in enumerate((b.r, b.k, b.v)):
                used_up(k, act, n0 + 4 * (j + 1))
                act.activation(dst, bank(k, 4 * (j % 2), 4).rearrange("p (t d) -> p t d", t=TILES),
                               ACT.Copy).then_inc(k.act_done.sem, 1)
            act.wait_ge(k.pe_done.sem, k.pe_done.at(1))
            act.activation(b.tw, k.ps[:, 4, 0:T], ACT.Tanh).then_inc(k.act_done.sem, 1)
            act.wait_ge(k.pe_done.sem, k.pe_done.at(2))
            act.activation(b.ta, k.ps[:, 5, 0:T], ACT.Copy).then_inc(k.act_done.sem, 1)
            act.wait_ge(k.pe_done.sem, k.pe_done.at(3))
            act.activation(b.tg, v3(k.ps[:, 6, :], 2, T), ACT.Sigmoid).then_inc(k.act_done.sem, 1)

        @block.vector
        def _(vec):
            link = lambda ins: k.vec_chain.link(vec, ins)
            mark = k.vec_chain.mark
            h = k.xT
            mark(vec.tensor_copy(xx[:, :, 0:1], h[:, :, 1:2]))
            mark(vec.tensor_copy(xx[:, :, T - 1:T], h[:, :, T - 2:T - 1]))
            link(vec.tensor_tensor(xx[:, :, 1:T - 1], h[:, :, 0:T - 2], h[:, :, 2:T], ADD))
            link(vec.scalar_tensor_tensor(out=xx, in0=xx, scalar=0.5, in1=h[:, :, :], op0=MUL, op1=SUB))
            vec.wait_ge(k.small_landed.sem, k.small_landed.at(n_small))
            for j in range(6):
                if 2 <= j < 5:
                    used_up(k, vec, n0 + 4 * (j - 1))
                elif j == 5:
                    vec.wait_ge(k.pe_done.sem, k.pe_done.at(1))
                for s in range(K8):
                    mark(vec.scalar_tensor_tensor(out=xs[:, j % 2, s], in0=xx[:, s], scalar=mu[:, j, s:s + 1],
                                                  in1=h[:, s], op0=MUL, op1=ADD))
                vec.wait_ge(k.vec_chain.sem, k.vec_chain.n)
                vec.sem_inc(k.vec_done.sem, 1)

        @block.tensor
        def _(pe):
            for j in range(3):
                pe.wait_ge(k.vec_done.sem, k.vec_done.at(j + 1))
                if j == 2:
                    pe.wait_ge(k.act_done.sem, k.act_done.at(1))
                project_tokens(k, pe, n0 + 4 * j, xs[:, j % 2], K8, D, j % 2)
            pe.wait_ge(k.act_done.sem, k.act_done.at(2))
            pe.wait_ge(k.small_landed.sem, k.small_landed.at(n_small))
            for j, w in ((3, w1), (4, a1)):
                pe.wait_ge(k.vec_done.sem, k.vec_done.at(j + 1))
                for s in range(K8):
                    mm = pe.matmul(k.ps[:, 1 + j, 0:T], w[:, s].rearrange("p z r -> p (z r)"), xs[:, j % 2, s],
                                   start=(s == 0), stop=(s == K8 - 1))
                mm.then_inc(k.pe_done.sem, 1)
            pe.wait_ge(k.vec_done.sem, k.vec_done.at(6))
            for z in range(2):
                for s in range(K8):
                    mm = pe.matmul(k.ps[:, 6, z * T:(z + 1) * T], g1[:, s, z], xs[:, 1, s],
                                   start=(s == 0), stop=(s == K8 - 1))
            mm.then_inc(k.pe_done.sem, 1)
    k.small_landed.close(n_small)
    k.act_done.close(6)
    k.vec_done.close(6)
    k.pe_done.close(3)


STAGES = tuple(2 ** s for s in range(1, int(math.log2(CH)) + 1))
FS = 256
ORDER = [(par, hp) for par in range(2) for hp in range(2)]


def rwkv_mix_phase(k, b):
    a = k.a
    c = Carver(k.region, k.region_w, b.end)
    vecs = c.take(9 * D).rearrange("p (j d) -> p j d", j=9)
    w2, a2 = c.take(D), c.take(D)
    g2 = v3(c.take(2 * D), 2, D)
    s = Carver(k.arena, SLOTS * SLOT)
    full = lambda: v3(s.take(TILES * FS), TILES, FS)
    cum, ein, eneg, ex, eh, lw, ar, kd, bd, kk, rt, bt, kt, bh, kh = (full() for _ in range(15))
    at_ = full()
    wv = s.take(TILES * 4 * HN).rearrange("p (t o n) -> p t o n", t=TILES, o=4)
    art = s.take(8 * P).rearrange("p (h t w n) -> p h t w n", h=2, t=TILES, w=2)
    btT = s.take(4 * P).rearrange("p (h t n) -> p h t n", h=2, t=TILES)
    ktT = s.take(4 * P).rearrange("p (h t n) -> p h t n", h=2, t=TILES)
    lq = s.take(TILES * 12 * P).rearrange("p (t o w n) -> p t o w n", t=TILES, o=4, w=3)
    mq = s.take(TILES * 8 * P).rearrange("p (t o w n) -> p t o w n", t=TILES, o=4, w=2)
    inv = s.take(TILES * 8 * P).rearrange("p (t o w n) -> p t o w n", t=TILES, o=4, w=2)
    xb = s.take(TILES * 4 * P).rearrange("p (t o n) -> p t o n", t=TILES, o=4)
    gu = s.take(TILES * 4 * P).rearrange("p (t o n) -> p t o n", t=TILES, o=4)
    ght = s.take(TILES * 4 * P).rearrange("p (t w h n) -> p t w h n", t=TILES, w=2, h=2)
    us = v3(s.take(4 * HN), 4, HN)
    st = v3(s.take(2 * HN), 2, HN)
    yb = full()
    pc = s.take(8)
    sm = s.take(4 * 8)
    stage = s.take(2 * len(STAGES) * P).rearrange("p (z s n) -> p z s n", z=2, s=len(STAGES))
    tri = s.take(2 * 2 * P).rearrange("p (z w n) -> p z w n", z=2, w=2)
    blk = s.take(P)
    blkcol = s.take(2)
    og = v3(k.xT[:, :, :].rearrange("p k t -> p (k t)"), TILES, D)
    rows = [a["rw_w0"][0, 0], a["rw_a0"][0, 0], a["rw_w0"][0, 1], a["rw_a0"][0, 1], a["rw_k_k"][0], a["rw_k_a"][0],
            a["rw_r_k"][0].rearrange("h n -> (h n)"), a["rw_ln_w"][0], a["rw_ln_b"][0]]
    small = [(vecs[:, j, :], r.partition_broadcast(P)) for j, r in enumerate(rows)]
    small += [(w2, a["rw_w2"][0].rearrange("z r d -> (z r) d")), (a2, a["rw_a2"][0].rearrange("z r d -> (z r) d")),
              (g2, a["rw_g2"][0].rearrange("z r d -> r z d"))]
    n_small = 16 * len(small)

    batches = [(q, z) for q in range(HEADS // 4) for z in range(2)]
    chunks = T // CH
    PREP, TILE_STEPS = 12, 4 + 4 * (len(STAGES) - 1) + 6
    FINISH = PREP + 2 + 4 * (chunks - 2) + 2
    JOINT = FINISH + 4
    turn_tile = (k.turn_tile0, k.turn_tile1)

    def joint(eng, n, done):
        eng.wait_ge(k.turn_joint.sem, k.turn_joint.at(n * JOINT + done))

    def joint_end(eng):
        eng.sem_inc(k.turn_joint.sem, 1)

    def tile_turn(eng, n, tile, done):
        eng.wait_ge(turn_tile[tile].sem, turn_tile[tile].at(n * TILE_STEPS + done))

    def tile_end(eng, tile):
        eng.sem_inc(turn_tile[tile].sem, 1)

    def by_parity(ap):
        return ap.rearrange("p (h q n) -> p q h n", h=2, q=2)

    with k.nc.Block() as block:
        @block.sync
        def _(sp):
            for dst, src in small:
                sp.dma_start(dst, src).then_inc(k.small_landed.sem, 16)

        @block.gpsimd
        def _(pool):
            link = lambda ins: k.pool_chain.link(pool, ins)

            def keep(v, pattern, base, mult):
                link(pool.affine_select(out=v, in_=v, pattern=pattern, compare_op=ALU.is_ge, fill=0.0, base=base,
                                        channel_multiplier=mult))

            link(pool.memset(blk, 1.0))
            v = blk.rearrange("p (b m) -> p b m", m=CH)
            keep(v, [[-CH, P // CH], [0, CH]], 0, 1)
            keep(v, [[CH, P // CH], [0, CH]], CH - 1, -1)
            link(pool.tensor_copy(blkcol, v[:, :, 0]))
            link(pool.memset(stage, 1.0))
            for z in range(2):
                for w in range(2):
                    link(pool.tensor_copy(tri[:, z, w], blk))
                    keep(tri[:, z, w], [[1 - 2 * z, P]], w - 1, 2 * z - 1)
                for i, m in enumerate(STAGES):
                    v = stage[:, z, i].rearrange("p (b q m) -> p b q m", q=2, m=m // 2)
                    if z == 0:
                        keep(v, [[-m, P // m], [-1000, 2], [0, m // 2]], -(m // 2), 1)
                        keep(v, [[m, P // m], [0, 2], [0, m // 2]], m - 1, -1)
                    else:
                        keep(v, [[-m, P // m], [1000, 2], [0, m // 2]], -1000, 1)
                        keep(v, [[m, P // m], [0, 2], [0, m // 2]], m // 2 - 1, -1)
            pool.sem_inc(k.pool_done.sem, 1)

        @block.tensor
        def _(pe):
            pe.wait_ge(k.small_landed.sem, k.small_landed.at(n_small))
            pe.wait_ge(k.pool_done.sem, k.pool_done.at(1))
            for n, (q, z) in enumerate(batches):
                fs = slice(q * FS, (q + 1) * FS)
                joint(pe, n, 1)
                for m, (t1, t2) in enumerate(((b.tw, w2), (b.ta, a2))):
                    for tile in range(TILES):
                        mm = pe.matmul(k.ps[:, m, tile * FS:(tile + 1) * FS],
                                       t1[z * 64:(z + 1) * 64, tile * P:(tile + 1) * P],
                                       t2[z * 64:(z + 1) * 64, fs], start=True, stop=True)
                mm.then_inc(k.turn_joint.sem, 1)
                joint(pe, n, 5)
                for tile in range(TILES):
                    pe.matmul(k.ps[:, 0, tile * FS:(tile + 1) * FS], tri[:, z, 1], lw[:, tile], start=True, stop=True)
                    pe.matmul(k.ps[:, 1, tile * FS:(tile + 1) * FS], blk, lw[:, tile], start=True, stop=True)
                    for hp in range(2):
                        at = hp * 4 + tile * 2
                        mm = pe.matmul(k.ps[:, 2, at:at + 2], lw[:, tile, hp * P:(hp + 1) * P], blkcol,
                                       start=True, stop=True)
                mm.then_inc(k.turn_joint.sem, 1)
                joint(pe, n, 10)
                for m, src in enumerate((at_, rt, bt, kt)):
                    for hp in range(2):
                        for tile in range(TILES):
                            at = (hp * TILES + tile) * P
                            mm = pe.transpose(k.ps[:, m, at:at + P], src[:, tile, hp * P:(hp + 1) * P], k.ident[:, :])
                mm.then_inc(k.turn_joint.sem, 1)
                joint(pe, n, PREP)

                for step in range(0, TILE_STEPS, 2):
                    for tile in range(TILES):
                        if step:
                            tile_turn(pe, n, tile, step)
                        pb = lambda i: k.ps[:, 4 * tile + i, :]
                        L, LT, QT = (lq[:, tile, :, w] for w in range(3))
                        MT, KT = (mq[:, tile, :, w] for w in range(2))
                        for o, (par, hp) in enumerate(ORDER):
                            j = 2 * hp + par
                            half = slice(par * 64, par * 64 + 64)
                            vj = b.v[:, tile, q * FS + j * HN:q * FS + (j + 1) * HN]
                            if step == 0:
                                for m, side in enumerate((btT, ktT)):
                                    mm = pe.matmul(pb(2 * m + par)[:, hp * 256:(hp + 1) * 256], side[half, hp, tile],
                                                   art[half, hp, tile].rearrange("p w n -> p (w n)"),
                                                   start=True, stop=True)
                            elif step == 2:
                                mm = pe.matmul(pb(par)[:, hp * P:(hp + 1) * P], art[half, hp, tile, 0],
                                               btT[half, hp, tile], start=True, stop=True)
                            elif step < TILE_STEPS - 6:
                                if step % 4 == 0:
                                    mm = pe.matmul(pb(2)[:, o * P:(o + 1) * P], LT[:, o], inv[:, tile, o, 0],
                                                   start=True, stop=True)
                                else:
                                    w = pb(o // 2)[:, (o % 2) * 256:(o % 2 + 1) * 256]
                                    pe.matmul(w[:, 0:P], inv[:, tile, o, 1], xb[:, tile, o], start=True, stop=True)
                                    mm = pe.matmul(w[:, P:2 * P], xb[:, tile, o], inv[:, tile, o, 1],
                                                   start=True, stop=True)
                            elif step == TILE_STEPS - 6:
                                mm = pe.matmul(pb(2)[:, o * HN:(o + 1) * HN], MT[:, o], vj, start=True, stop=True)
                            elif step == TILE_STEPS - 4:
                                aj = at_[:, tile, j * HN:(j + 1) * HN]
                                g = pb(0)[:, o * P:(o + 1) * P]
                                pe.matmul(g[:, 0:HN], inv[:, tile, o, 1], aj, start=True, stop=True)
                                pe.matmul(g[:, HN:P], inv[:, tile, o, 1], wv[:, tile, o], start=True, stop=True)
                                mm = pe.matmul(pb(1)[half, hp * P:(hp + 1) * P], aj,
                                               inv[:, tile, o, 1], start=True, stop=True)
                            else:
                                pe.matmul(pb(2)[half, hp * P:(hp + 1) * P], gu[:, tile, o, 0:HN], QT[:, o],
                                          start=True, stop=True)
                                pe.matmul(pb(3)[:, o * HN:(o + 1) * HN], QT[:, o], gu[:, tile, o, HN:P],
                                          start=True, stop=False)
                                mm = pe.matmul(pb(3)[:, o * HN:(o + 1) * HN], KT[:, o], vj, start=False, stop=True)
                        mm.then_inc(turn_tile[tile].sem, 1)

                at = PREP
                for tile in range(TILES):
                    tile_turn(pe, n, tile, TILE_STEPS)
                for i, ch in enumerate(range(chunks) if z == 0 else reversed(range(chunks))):
                    tile, rows_ = ch // 2, slice((ch % 2) * CH, (ch % 2 + 1) * CH)
                    if i:
                        joint(pe, n, at)
                        for o, (par, hp) in enumerate(ORDER):
                            half = slice(par * 64, par * 64 + 64)
                            mm = pe.matmul(k.ps[rows_, 4 + par, hp * HN:(hp + 1) * HN], ght[half, tile, 1, hp, rows_],
                                           st[half, hp], start=True, stop=True)
                            if i < chunks - 1:
                                mm = pe.matmul(k.ps[rows_, par, hp * HN:(hp + 1) * HN], ght[half, tile, 0, hp, rows_],
                                               st[half, hp], start=True, stop=True)
                        mm.then_inc(k.turn_joint.sem, 1)
                        at += 2
                    if i < chunks - 1:
                        joint(pe, n, at)
                        for o, (par, hp) in enumerate(ORDER):
                            j = 2 * hp + par
                            half = slice(par * 64, par * 64 + 64)
                            u = us[rows_, o] if i else gu[rows_, tile, o, HN:P]
                            out = k.ps[half, 6, hp * HN:(hp + 1) * HN]
                            pe.matmul(out, bh[rows_, tile, j * HN:(j + 1) * HN], u, start=True, stop=False)
                            mm = pe.matmul(out, kh[rows_, tile, j * HN:(j + 1) * HN],
                                           b.v[rows_, tile, q * FS + j * HN:q * FS + (j + 1) * HN],
                                           start=False, stop=True)
                        mm.then_inc(k.turn_joint.sem, 1)
                        at += 2
                assert at == FINISH
                joint(pe, n, FINISH)
                for tile in range(TILES):
                    mm = pe.matmul(k.ps[:, 7, tile * FS:(tile + 1) * FS], b.tg[:, z, tile * P:(tile + 1) * P],
                                   g2[:, z, fs], start=True, stop=True)
                mm.then_inc(k.turn_joint.sem, 1)

        @block.scalar
        def _(act):
            mark = k.act_chain.mark
            ps3 = lambda i: v3(k.ps[:, i, :], TILES, FS)

            def done():
                act.wait_ge(k.act_chain.sem, k.act_chain.n)
                joint_end(act)

            for n, (q, z) in enumerate(batches):
                if z == 0:
                    act.wait_ge(k.vec_done.sem, k.vec_done.at(q + 1))
                    act.activation(sm[:, 0:8], sm[:, 0:8], ACT.Sqrt).then_inc(k.act_done.sem, 1)
                joint(act, n, 3)
                mark(act.activation(lw, lw, ACT.Sigmoid))
                mark(act.activation(ar, ar, ACT.Sigmoid))
                done()
                joint(act, n, 6)
                mark(act.activation(cum, ps3(0), ACT.Copy))
                mark(act.activation(ein, ps3(0), ACT.Exp))
                mark(act.activation(eneg, ps3(0), ACT.Exp, scale=-1.0))
                mark(act.activation(pc, k.ps[:, 2, 0:8], ACT.Exp))
                done()
                joint(act, n, 8)
                mark(act.activation(ex, ex, ACT.Exp))
                mark(act.activation(eh, eh, ACT.Exp))
                done()
                joint(act, n, FINISH + 2)
                mark(act.activation(sm[:, 16:24], sm[:, 16:24], ACT.Sqrt))
                done()

        @block.vector
        def _(vec):
            link = lambda ins: k.vec_chain.link(vec, ins)
            mark = k.vec_chain.mark

            def settle():
                vec.wait_ge(k.vec_chain.sem, k.vec_chain.n)

            def done():
                settle()
                joint_end(vec)

            def bc_tiles(j, fs):
                return vecs[:, j:j + 1, fs].to_broadcast([P, TILES, FS])

            def per_head(ap):
                return ap.rearrange("p t (h n) -> p (t h) n", n=HN)

            def bc_head(cols):
                return cols.rearrange("p (h a) -> p h a", a=1).to_broadcast([P, 8, HN])

            ps3 = lambda i: v3(k.ps[:, i, :], TILES, FS)
            vec.wait_ge(k.small_landed.sem, k.small_landed.at(n_small))
            vec.wait_ge(k.pool_done.sem, k.pool_done.at(1))
            for n, (q, z) in enumerate(batches):
                fs = slice(q * FS, (q + 1) * FS)
                r_, k_, v_ = (t[:, :, fs] for t in (b.r, b.k, b.v))
                if z == 0:
                    link(vec.tensor_tensor(kk, k_, bc_tiles(4, fs), MUL))
                    link(vec.tensor_tensor(ex, kk, kk, MUL))
                    link(vec.tensor_reduce(sm[:, 0:8], per_head(ex), X, ADD))
                    vec.sem_inc(k.vec_done.sem, 1)
                    vec.wait_ge(k.act_done.sem, k.act_done.at(q + 1))
                    link(vec.tensor_scalar(sm[:, 0:8], sm[:, 0:8], 1e-12, None, MAX))
                    link(vec.reciprocal(sm[:, 0:8], sm[:, 0:8]))
                    link(vec.tensor_tensor(per_head(kk), per_head(kk), bc_head(sm[:, 0:8]), MUL))
                joint_end(vec)
                joint(vec, n, 2)
                mark(vec.tensor_tensor(lw, ps3(0), bc_tiles(2 * z, fs), ADD))
                mark(vec.tensor_tensor(ar, ps3(1), bc_tiles(2 * z + 1, fs), ADD))
                done()
                joint(vec, n, 4)
                mark(vec.tensor_scalar(lw, lw, -math.exp(-0.5), None, MUL))
                mark(vec.tensor_tensor(bd, kk, ar, MUL))
                link(vec.scalar_tensor_tensor(out=kd, in0=ar, scalar=-1.0, in1=bc_tiles(5, fs), op0=ADD, op1=MUL))
                link(vec.scalar_tensor_tensor(out=kd, in0=kd, scalar=1.0, in1=k_, op0=ADD, op1=MUL))
                link(vec.tensor_tensor(ex, r_, kd, MUL))
                link(vec.tensor_tensor(ex, ex, bc_tiles(6, fs), MUL))
                mark(vec.tensor_reduce(sm[:, 8:16], per_head(ex), X, ADD))
                done()
                joint(vec, n, 7)
                mark(vec.tensor_tensor(ex, cum, lw, SUB))
                mark(vec.tensor_tensor(eh, ps3(1), cum, SUB))
                done()
                joint(vec, n, 9)
                mark(vec.scalar_tensor_tensor(out=at_, in0=kk, scalar=-1.0, in1=ex, op0=MUL, op1=MUL))
                mark(vec.tensor_tensor(rt, r_, ein, MUL))
                mark(vec.tensor_tensor(bt, bd, eneg, MUL))
                mark(vec.tensor_tensor(kt, kd, eneg, MUL))
                mark(vec.tensor_tensor(bh, bd, eh, MUL))
                mark(vec.tensor_tensor(kh, kd, eh, MUL))
                done()
                joint(vec, n, 11)
                for m, dst in enumerate((art[:, :, :, 0], art[:, :, :, 1], btT, ktT)):
                    mark(vec.tensor_copy(dst, k.ps[:, m, :].rearrange("p (h t n) -> p h t n", h=2, t=TILES)))
                done()

                for step in range(1, TILE_STEPS, 2):
                    for tile in range(TILES):
                        tile_turn(vec, n, tile, step)
                        b0 = 4 * tile
                        inv_t = inv[:, tile].rearrange("p o w n -> p (o w n)")
                        if step == 1:
                            for m, dst in enumerate((lq[:, tile, :, 1:3], mq[:, tile])):
                                mark(vec.tensor_tensor(
                                    dst.rearrange("p o w n -> p o (w n)"), v3(bank(k, b0 + 2 * m, 2), 4, 2 * P),
                                    tri[:, z].rearrange("p w n -> p (w n)").rearrange("p (a m) -> p a m", a=1)
                                    .to_broadcast([P, 4, 2 * P]), MUL))
                            settle()
                        elif step == 3:
                            for par in range(2):
                                mark(vec.tensor_tensor(lq[:, tile, 2 * par:2 * par + 2, 0], v3(k.ps[:, b0 + par, 0:256], 2, P),
                                                       tri[:, 1 - z, 0:1].to_broadcast([P, 2, P]), MUL))
                            settle()
                            for w in range(2):
                                m = (z, 1 - z)[w]
                                mark(vec.tensor_tensor(inv[:, tile, :, w], lq[:, tile, :, w],
                                                       stage[:, m, 0:1].to_broadcast([P, 4, P]), MUL))
                            settle()
                            flat = inv[:, tile].rearrange("p o w n -> p (o w) n")
                            link(vec.tensor_tensor(flat, flat, v3(k.ident[:, :], 1, P).to_broadcast([P, 8, P]), ADD))
                        elif step < TILE_STEPS - 6:
                            if step % 4 == 1:
                                i = (step - 1) // 4
                                link(vec.tensor_tensor(xb[:, tile], v3(k.ps[:, b0 + 2, :], 4, P),
                                                       stage[:, z, i:i + 1].to_broadcast([P, 4, P]), MUL))
                            else:
                                link(vec.tensor_tensor(inv_t, inv_t, bank(k, b0, 2), ADD))
                        elif step == TILE_STEPS - 5:
                            link(vec.tensor_copy(wv[:, tile], v3(k.ps[:, b0 + 2, 0:4 * HN], 4, HN)))
                        elif step == TILE_STEPS - 3:
                            mark(vec.tensor_copy(gu[:, tile].rearrange("p o n -> p (o n)"), k.ps[:, b0, :]))
                            mark(vec.tensor_copy(ght[:, tile, 0].rearrange("p h n -> p (h n)"), k.ps[:, b0 + 1, 0:256]))
                            settle()
                        else:
                            mark(vec.tensor_tensor(ght[:, tile, 1], v3(k.ps[:, b0 + 2, 0:256], 2, P), art[:, :, tile, 1], ADD))
                            mark(vec.tensor_copy(by_parity(yb[:, tile]),
                                                 k.ps[:, b0 + 3, 0:256].rearrange("p (q h n) -> p q h n", q=2, h=2)))
                            settle()
                        tile_end(vec, tile)

                at = PREP
                for i, ch in enumerate(range(chunks) if z == 0 else reversed(range(chunks))):
                    tile, rows_ = ch // 2, slice((ch % 2) * CH, (ch % 2 + 1) * CH)
                    if i:
                        joint(vec, n, at + 1)
                        y_ = by_parity(yb[rows_, tile])
                        mark(vec.tensor_tensor(y_, k.ps[rows_, 4:6, 0:P].rearrange("p q (h n) -> p q h n", h=2), y_, ADD))
                        if i < chunks - 1:
                            mark(vec.tensor_tensor(us[rows_].rearrange("p (q h) n -> p q h n", q=2),
                                                   k.ps[rows_, 0:2, 0:P].rearrange("p q (h n) -> p q h n", h=2),
                                                   gu[rows_, tile, :, HN:P].rearrange("p (q h) n -> p q h n", q=2), ADD))
                        done()
                        at += 2
                    if i < chunks - 1:
                        joint(vec, n, at + 1)
                        for hp in range(2):
                            new = k.ps[:, 6, hp * HN:(hp + 1) * HN]
                            if i == 0:
                                mark(vec.tensor_copy(st[:, hp], new))
                            else:
                                col = hp * 4 + ch
                                mark(vec.scalar_tensor_tensor(out=st[:, hp], in0=st[:, hp], scalar=pc[:, col:col + 1],
                                                              in1=new, op0=MUL, op1=ADD))
                        done()
                        at += 2
                joint(vec, n, FINISH + 1)
                yh, eh_ = per_head(yb), per_head(ex)
                link(vec.tensor_reduce(sm[:, 24:32], yh, X, ADD))
                link(vec.tensor_scalar(sm[:, 24:32], sm[:, 24:32], 1.0 / HN, None, MUL))
                link(vec.tensor_tensor(yh, yh, bc_head(sm[:, 24:32]), SUB))
                link(vec.tensor_tensor(eh_, yh, yh, MUL))
                link(vec.tensor_reduce(sm[:, 16:24], eh_, X, ADD))
                link(vec.tensor_scalar(sm[:, 16:24], sm[:, 16:24], 1.0 / HN, GN_EPS, MUL, ADD))
                joint_end(vec)
                joint(vec, n, FINISH + 3)
                link(vec.reciprocal(sm[:, 16:24], sm[:, 16:24]))
                link(vec.tensor_tensor(yh, yh, bc_head(sm[:, 16:24]), MUL))
                link(vec.tensor_tensor(yb, yb, bc_tiles(7, fs), MUL))
                link(vec.tensor_tensor(yb, yb, bc_tiles(8, fs), ADD))
                link(vec.tensor_tensor(ex.rearrange("p t (h n) -> p t h n", n=HN),
                                       v_.rearrange("p t (h n) -> p t h n", n=HN),
                                       sm[:, 8:16].rearrange("p (t h a) -> p t h a", t=TILES, a=1)
                                       .to_broadcast([P, TILES, 4, HN]), MUL))
                link(vec.tensor_tensor(yb, yb, ex, ADD))
                if z == 0:
                    link(vec.tensor_tensor(og[:, :, fs], ps3(7), yb, MUL))
                else:
                    link(vec.tensor_tensor(yb, ps3(7), yb, MUL))
                    link(vec.tensor_tensor(og[:, :, fs], og[:, :, fs], yb, ADD))
                joint_end(vec)
    k.small_landed.close(n_small)
    k.pool_done.close(1)
    k.vec_done.close(HEADS // 4)
    k.act_done.close(HEADS // 4)
    k.turn_joint.close(len(batches) * JOINT)
    for sig in turn_tile:
        sig.close(len(batches) * TILE_STEPS)
    return og


def route_phase(k, i, end):
    a = k.a
    first = i < DEPTH
    NR = N_GROUPS + EXPERTS
    c = Carver(k.region, k.region_w)
    k.gates_bc = c.take(EXPERTS * T).rearrange("p (e t) -> p e t", e=EXPERTS)
    k.moe_end = c.at
    rw = v3(c.take(K8 * NR), K8, NR)
    rb = c.take(NR)
    lg = v3(c.take(TILES * NR), TILES, NR)
    gT = c.take(T)
    gates = c.take(TILES * EXPERTS).rearrange("p (t g e) -> p t g e", t=TILES, g=N_GROUPS)
    tmp4 = c.take(TILES * EXPERTS).rearrange("p (t g e) -> p t g e", t=TILES, g=N_GROUPS)
    ohg, eg, s4 = (v3(c.take(TILES * N_GROUPS), TILES, N_GROUPS) for _ in range(3))
    sel, oh1, oh2, s8, e2 = (v3(c.take(TILES * PER_GROUP), TILES, PER_GROUP) for _ in range(5))
    cols = v3(c.take(8 * TILES), 8, TILES)
    m0, mm, pg, m1, m2, ex, w1, w2 = (cols[:, j, :] for j in range(8))
    small = []
    if first:
        small.append((rw[:, :, 0:N_GROUPS], a["moe_router_g"][i].rearrange("(p k) g -> p k g", k=K8)))
        small.append((rb[:, 0:N_GROUPS], a["moe_router_g_b"][i].partition_broadcast(P)))
        for g in range(N_GROUPS):
            at = N_GROUPS + g * PER_GROUP
            small.append((rw[:, :, at:at + PER_GROUP], a["moe_router_e"][i, g].rearrange("(p k) e -> p k e", k=K8)))
            small.append((rb[:, at:at + PER_GROUP], a["moe_router_e_b"][i, g].partition_broadcast(P)))
    else:
        j = i - DEPTH
        small.append((rw[:, :, 0:N_GROUPS], a["w_route_group_2"][j].rearrange("(p k) g -> p k g", k=K8)))
        small.append((rb[:, 0:N_GROUPS], a["b_route_group_2"][j].partition_broadcast(P)))
        small.append((rw[:, :, N_GROUPS:NR], a["w_route_expert_2"][j].rearrange("(p k) e -> p k e", k=K8)))
        small.append((rb[:, N_GROUPS:NR], a["b_route_expert_2"][j].partition_broadcast(P)))
    n_small = 16 * len(small)

    def last(col, n):
        return col.rearrange("p (t a) -> p t a", a=1).to_broadcast([P, TILES, n])

    with k.nc.Block() as block:
        @block.sync
        def _(sp):
            for dst, src in small:
                sp.dma_start(dst, src).then_inc(k.small_landed.sem, 16)
            ahead(k, sp, end)

        @block.tensor
        def _(pe):
            pe.wait_ge(k.small_landed.sem, k.small_landed.at(n_small))
            for tile in range(TILES):
                for s in range(K8):
                    mm_ = pe.matmul(k.ps[:, tile, 0:NR], k.xT[:, s, tile * P:(tile + 1) * P], rw[:, s],
                                    start=(s == 0), stop=(s == K8 - 1))
            mm_.then_inc(k.pe_done.sem, 1)
            pe.wait_ge(k.vec_done.sem, k.vec_done.at(3))
            for tile in range(TILES):
                mm_ = pe.transpose(k.ps[0:EXPERTS, 2, tile * P:(tile + 1) * P],
                                   gates[:, tile].rearrange("p g e -> p (g e)"), k.ident[:, :])
            mm_.then_inc(k.pe_done.sem, 1)
            pe.wait_ge(k.vec_done.sem, k.vec_done.at(4))
            for r in range(EXPERTS // 8):
                if r >= 2:
                    pe.wait_ge(k.act_done.sem, k.act_done.at(1 + r))
                for e in range(8):
                    mm_ = pe.matmul(k.ps[:, 4 * (r % 2) + e // 2, (e % 2) * T:(e % 2 + 1) * T],
                                    k.ident[0:EXPERTS, r * 8 + e:r * 8 + e + 1].to_broadcast([EXPERTS, P]),
                                    gT[0:EXPERTS, :], start=True, stop=True)
                mm_.then_inc(k.pe_done.sem, 1)

        @block.scalar
        def _(act):
            act.wait_ge(k.vec_done.sem, k.vec_done.at(1))
            act.activation(eg, eg, ACT.Exp).then_inc(k.act_done.sem, 1)
            act.wait_ge(k.vec_done.sem, k.vec_done.at(2))
            act.activation(ex, ex, ACT.Exp).then_inc(k.act_done.sem, 1)
            for r in range(EXPERTS // 8):
                act.wait_ge(k.pe_done.sem, k.pe_done.at(3 + r))
                act.activation(k.gates_bc[:, r * 8:(r + 1) * 8, :], v3(bank(k, 4 * (r % 2), 4), 8, T),
                               ACT.Copy).then_inc(k.act_done.sem, 1)

        @block.vector
        def _(vec):
            link = lambda ins: k.vec_chain.link(vec, ins)

            def first_best(values, best, onehot, scratch, n):
                link(vec.tensor_reduce(best, values, X, MAX))
                link(vec.tensor_tensor(scratch, values, last(best, n), ALU.is_equal))
                link(vec.tensor_tensor(scratch, scratch, v3(k.desc[:, 0:n], 1, n).to_broadcast([P, TILES, n]), MUL))
                link(vec.tensor_reduce(mm, scratch, X, MAX))
                link(vec.tensor_tensor(onehot, scratch, last(mm, n), ALU.is_equal))

            vec.wait_ge(k.pe_done.sem, k.pe_done.at(1))
            vec.wait_ge(k.small_landed.sem, k.small_landed.at(n_small))
            link(vec.tensor_tensor(lg, k.ps[:, 0:TILES, 0:NR], v3(rb, 1, NR).to_broadcast([P, TILES, NR]), ADD))
            lgg = lg[:, :, 0:N_GROUPS]
            first_best(lgg, m0, ohg, s4, N_GROUPS)
            link(vec.tensor_tensor(eg, lgg, last(m0, N_GROUPS), SUB))
            vec.sem_inc(k.vec_done.sem, 1)
            link(vec.tensor_tensor(tmp4, lg[:, :, N_GROUPS:NR].rearrange("p t (g e) -> p t g e", g=N_GROUPS),
                                   ohg.rearrange("p t (g a) -> p t g a", a=1).to_broadcast([P, TILES, N_GROUPS, PER_GROUP]), MUL))
            link(vec.tensor_reduce(sel, tmp4.rearrange("p t g e -> p t e g"), X, ADD))
            first_best(sel, m1, oh1, s8, PER_GROUP)
            link(vec.scalar_tensor_tensor(out=e2, in0=oh1, scalar=-BIG, in1=sel, op0=MUL, op1=ADD))
            first_best(e2, m2, oh2, s8, PER_GROUP)
            link(vec.tensor_tensor(ex, m2, m1, SUB))
            vec.sem_inc(k.vec_done.sem, 1)
            vec.wait_ge(k.act_done.sem, k.act_done.at(1))
            link(vec.tensor_reduce(pg, eg, X, ADD))
            link(vec.reciprocal(pg, pg))
            vec.wait_ge(k.act_done.sem, k.act_done.at(2))
            link(vec.tensor_scalar(w1, ex, 1.0, None, ADD))
            link(vec.reciprocal(w1, w1))
            link(vec.tensor_tensor(w1, w1, pg, MUL))
            link(vec.tensor_tensor(w2, w1, ex, MUL))
            link(vec.tensor_tensor(oh1, oh1, last(w1, PER_GROUP), MUL))
            link(vec.tensor_tensor(oh2, oh2, last(w2, PER_GROUP), MUL))
            link(vec.tensor_tensor(oh1, oh1, oh2, ADD))
            for tile in range(TILES):
                link(vec.tensor_tensor(gates[:, tile], ohg[:, tile].rearrange("p (g a) -> p g a", a=1).to_broadcast([P, N_GROUPS, PER_GROUP]),
                                       oh1[:, tile:tile + 1].to_broadcast([P, N_GROUPS, PER_GROUP]), MUL))
            vec.sem_inc(k.vec_done.sem, 1)
            vec.wait_ge(k.pe_done.sem, k.pe_done.at(2))
            link(vec.tensor_copy(gT[0:EXPERTS, :], k.ps[0:EXPERTS, 2, 0:T]))
            vec.sem_inc(k.vec_done.sem, 1)
    k.small_landed.close(n_small)
    k.pe_done.close(2 + EXPERTS // 8)
    k.vec_done.close(4)
    k.act_done.close(2 + EXPERTS // 8)


def experts_phase(k, i):
    a = k.a
    j = i % DEPTH
    wg, wu, wd = ((a["moe_w_gate"], a["moe_w_up"], a["moe_w_down"]) if i < DEPTH else
                  (a["w_exp_gate_2"], a["w_exp_up_2"], a["w_exp_down_2"]))
    wg = wg[j].rearrange("g e (p k) f -> (g e) p (k f)", k=K8)
    wu = wu[j].rearrange("g e (p k) f -> (g e) p (k f)", k=K8)
    wd = wd[j].rearrange("g e (p r) n -> (g e) p (r n)", r=2)
    n0 = k.starts[f"moe{i}"]
    passes = (EXPERTS - UNROLL) // UNROLL
    c = Carver(k.region, k.region_w, k.moe_end)
    act_out = c.take(2 * 2 * T).rearrange("p (b r t) -> p b r t", b=2, r=2)
    hid = c.take(2 * 2 * T).rearrange("p (b r t) -> p b r t", b=2, r=2)
    zeros = c.take(HALF)
    up_at = lambda e: 3 * e - 1 if e else 0
    down_at = lambda e: min(3 * e + 4, 3 * EXPERTS - 1)
    assert k.issued >= n0 + SLOTS, "the first units are loaded ahead"

    def slot(n):
        at = ((n0 + n) % SLOTS) * SLOT
        return k.arena[:, at:at + SLOT]

    def wait_slot(eng, n, p):
        eng.wait_ge(k.landed[(n0 + n) % SLOTS], 16 * ((n0 + n) // SLOTS + 1) + 16 * p)

    with k.nc.Block() as block:
        @block.sync
        def _(sp):
            def load(n, p, src):
                sp.wait_ge(k.used, n0 + n + 1 - SLOTS + SLOTS * p)
                sp.dma_start(slot(n), src).then_inc(k.landed[(n0 + n) % SLOTS], 16)

            issue(k, sp, n0 + 2 + SLOTS)
            with sp.Fori(1, passes) as p:
                for s in range(UNROLL):
                    one = lambda w, e: w[bass.ds(p * UNROLL + e, 1)].rearrange("a p n -> p (a n)")
                    load(2 + 3 * s, p, one(wg, s + 1))
                    load(3 + 3 * s, p, one(wu, s + 1))
                    load(4 + 3 * s, p, one(wd, s))
            k.issued = n0 + 2 + SLOTS * passes
            ahead(k, sp, n0 + 3 * EXPERTS)

        @block.tensor
        def _(pe):
            def first_layer(s, p):
                for m in range(2):
                    n = up_at(s) + m
                    wait_slot(pe, n, p)
                    w = slot(n).rearrange("p (k f) -> p k f", k=K8)
                    for r in range(2):
                        for q in range(K8):
                            mm = pe.matmul(k.ps[:, 4 + 2 * (s % 2) + m, r * T:(r + 1) * T], w[:, q, r:F:2], k.xT[:, q, :],
                                           start=(q == 0), stop=(q == K8 - 1))
                    mm.then_inc(k.used, 1)

            def second_layer(s, p):
                n = down_at(s)
                wait_slot(pe, n, p)
                pe.wait_ge(k.vec_done.sem, k.vec_done.at(s + 1) + UNROLL * p)
                w = v3(slot(n), 2, D)
                for r in range(2):
                    for tile in range(TILES):
                        for h in range(2):
                            mm = pe.matmul(k.ps[:, 2 * tile + h, :], hid[:, s % 2, r, tile * P:(tile + 1) * P],
                                           w[:, r, h * HALF:(h + 1) * HALF], start=False, stop=True,
                                           skip_group_check=True)
                mm.then_inc(k.used, 1)

            pe.wait_ge(k.pool_done.sem, k.pool_done.at(1))
            for b in range(4):
                pe.matmul(k.ps[:, b, :], zeros[:, 0:P], zeros, start=True, stop=True)
            first_layer(0, 0)
            with pe.Fori(0, passes) as p:
                for s in range(UNROLL):
                    first_layer(s + 1, p)
                    second_layer(s, p)
            for e in range(EXPERTS - UNROLL, EXPERTS):
                if e + 1 < EXPERTS:
                    first_layer(e + 1, 0)
                second_layer(e, 0)

        @block.scalar
        def _(act):
            def silu(s, p):
                act.wait_ge(k.used, n0 + up_after(s) + SLOTS * p)
                act.activation(act_out[:, s % 2], v3(k.ps[:, 4 + 2 * (s % 2), :], 2, T),
                               ACT.Silu).then_inc(k.act_done.sem, 1)

            up_after = lambda s: up_at(s) + 2
            silu(0, 0)
            with act.Fori(0, passes) as p:
                for s in range(UNROLL):
                    silu(s + 1, p)
            for e in range(EXPERTS - UNROLL, EXPERTS - 1):
                silu(e + 1, 0)

        @block.vector
        def _(vec):
            def gated(s, p):
                vec.wait_ge(k.act_done.sem, k.act_done.at(s + 1) + UNROLL * p)
                vec.tensor_tensor(hid[:, s % 2], v3(k.ps[:, 5 + 2 * (s % 2), :], 2, T), act_out[:, s % 2],
                                  MUL).then_inc(k.pass_mid.sem, 1)
                vec.wait_ge(k.pass_mid.sem, k.pass_mid.at(s + 1) + UNROLL * p)
                gate = k.gates_bc[:, bass.ds(p * UNROLL + s, 1), :] if not isinstance(p, int) else k.gates_bc[:, s:s + 1, :]
                vec.tensor_tensor(hid[:, s % 2], hid[:, s % 2], gate.to_broadcast([P, 2, T]),
                                  MUL).then_inc(k.vec_done.sem, 1)

            with vec.Fori(0, passes) as p:
                for s in range(UNROLL):
                    gated(s, p)
            for e in range(EXPERTS - UNROLL, EXPERTS):
                gated(e, 0)

        @block.gpsimd
        def _(pool):
            k.pool_chain.link(pool, pool.memset(zeros, 0.0))
            pool.sem_inc(k.pool_done.sem, 1)
    k.act_done.close(EXPERTS)
    k.vec_done.close(EXPERTS)
    k.pass_mid.close(EXPERTS)
    k.pool_done.close(1)


def moe_residual_phase(k, i):
    with k.nc.Block() as block:
        @block.vector
        def _(vec):
            link = lambda ins: k.vec_chain.link(vec, ins)
            add_gated(k, vec, link, 1, k.region[:, 0:TILES * D])


def qkv_phase(k, b):
    n0 = k.starts["qkv"]
    c = Carver(k.region, k.region_w)
    b.q, b.k = (c.take(len(GROUPS) * AH * T).rearrange("p (g h t) -> p g h t", g=len(GROUPS), h=AH) for _ in range(2))
    b.v = c.take(len(GROUPS) * TILES * D).rearrange("p (g t d) -> p g t d", g=len(GROUPS), t=TILES)
    b.o = v3(c.take(TILES * D), TILES, D)
    jobs = [(g, j) for g in range(len(GROUPS)) for j in range(3)]
    with k.nc.Block() as block:
        @block.sync
        def _(sp):
            ahead(k, sp, n0 + 4 * len(jobs))

        @block.tensor
        def _(pe):
            for n, (g, j) in enumerate(jobs):
                if n >= 2:
                    pe.wait_ge(k.act_done.sem, k.act_done.at(n - 1))
                if j < 2:
                    project_features(k, pe, n0 + 4 * n, k.xT, K8, n % 2)
                else:
                    project_tokens(k, pe, n0 + 4 * n, k.xT, K8, D, n % 2)

        @block.scalar
        def _(act):
            for n, (g, j) in enumerate(jobs):
                used_up(k, act, n0 + 4 * (n + 1))
                src = bank(k, 4 * (n % 2), 4)
                dst = (b.q[:, g], b.k[:, g], b.v[:, g])[j]
                act.activation(dst, v3(src, dst.shape[1], dst.shape[2]), ACT.Copy,
                               scale=ADH ** -0.5 if j == 0 else 1.0).then_inc(k.act_done.sem, 1)
    k.act_done.close(len(jobs))


def dilated_phase(k, b):
    G = len(GROUPS)
    s = Carver(k.arena, SLOTS * SLOT)
    away = s.take(G * TILES * T).rearrange("p (g t n) -> p g t n", g=G, t=TILES)
    diff = v3(s.take(TILES * T), TILES, T).bitcast(I32)
    rem = v3(s.take(TILES * T), TILES, T).bitcast(I32)
    tmp = v3(s.take(TILES * T), TILES, T)
    sc = s.take(TILES * G * T).rearrange("p (t g n) -> p t g n", t=TILES, g=G)
    pT = s.take(TILES * G * T).rearrange("p (t g n) -> p t g n", t=TILES, g=G)
    neg_max, den = s.take(TILES), s.take(TILES)
    slopes = [2.0 ** (-8.0 * (j + 1) / (G * AH)) for j in range(G * AH)]
    STEPS = 7
    turn_tile = (k.turn_tile0, k.turn_tile1)

    def turn(eng, tile, h, done):
        if h * STEPS + done:
            eng.wait_ge(turn_tile[tile].sem, turn_tile[tile].at(h * STEPS + done))

    with k.nc.Block() as block:
        @block.gpsimd
        def _(pool):
            k.pool_chain.link(pool, pool.iota(diff, pattern=[[-P, TILES], [1, T]], base=0, channel_multiplier=-1))
            pool.sem_inc(k.pool_done.sem, 1)

        @block.tensor
        def _(pe):
            for h in range(AH):
                for tile in range(TILES):
                    turn(pe, tile, h, 0)
                    for g in range(G):
                        mm = pe.matmul(k.ps[:, 4 * tile + g // 2, (g % 2) * T:(g % 2 + 1) * T],
                                       b.q[:, g, h, tile * P:(tile + 1) * P], b.k[:, g, h], start=True, stop=True)
                    mm.then_inc(turn_tile[tile].sem, 1)
                for tile in range(TILES):
                    turn(pe, tile, h, 3)
                    for g in range(G):
                        for n in range(TILES):
                            at = (g % 2) * T + n * P
                            mm = pe.transpose(k.ps[:, 4 * tile + 2 + g // 2, at:at + P], sc[:, tile, g, n * P:(n + 1) * P],
                                              k.ident[:, :])
                    mm.then_inc(turn_tile[tile].sem, 1)
                for tile in range(TILES):
                    turn(pe, tile, h, 5)
                    for g in range(G):
                        for n in range(TILES):
                            mm = pe.matmul(k.ps[:, 4 * tile, 0:ADH], pT[:, tile, g, n * P:(n + 1) * P],
                                           b.v[:, g, n, h * ADH:(h + 1) * ADH], start=(g == 0 and n == 0),
                                           stop=(g == G - 1 and n == TILES - 1))
                    mm.then_inc(turn_tile[tile].sem, 1)

        @block.scalar
        def _(act):
            for h in range(AH):
                for tile in range(TILES):
                    turn(act, tile, h, 2)
                    act.activation(sc[:, tile], sc[:, tile], ACT.Exp, bias=neg_max[:, tile:tile + 1],
                                   accum_out=den[:, tile:tile + 1]).then_inc(turn_tile[tile].sem, 1)
                for tile in range(TILES):
                    turn(act, tile, h, 4)
                    act.activation(pT[:, tile].rearrange("p g n -> p (g n)"), bank(k, 4 * tile + 2, 2)[:, 0:G * T],
                                   ACT.Copy).then_inc(turn_tile[tile].sem, 1)

        @block.vector
        def _(vec):
            link = lambda ins: k.vec_chain.link(vec, ins)
            mark = k.vec_chain.mark
            vec.wait_ge(k.pool_done.sem, k.pool_done.at(1))
            link(vec.tensor_copy(tmp, diff))
            link(vec.scalar_tensor_tensor(out=tmp, in0=tmp, scalar=-1.0, in1=tmp, op0=MUL, op1=MAX))
            for g, (window, dil) in enumerate(GROUPS):
                link(vec.tensor_scalar(away[:, g], tmp, float(window // 2), BIG * 100, ALU.is_gt, MUL))
                if dil > 1:
                    link(vec.tensor_scalar(rem, diff, dil - 1, None, ALU.bitwise_and))
                    link(vec.tensor_copy(sc[:, :, 0], rem))
                    link(vec.tensor_scalar(sc[:, :, 0], sc[:, :, 0], 0.0, BIG * 100, ALU.is_gt, MUL))
                    link(vec.tensor_tensor(away[:, g], away[:, g], sc[:, :, 0], ADD))
                link(vec.tensor_tensor(away[:, g], away[:, g], tmp, ADD))
            for h in range(AH):
                for tile in range(TILES):
                    turn(vec, tile, h, 1)
                    for g in range(G):
                        mark(vec.scalar_tensor_tensor(out=sc[:, tile, g], in0=away[:, g, tile], scalar=-slopes[g * AH + h],
                                                      in1=k.ps[:, 4 * tile + g // 2, (g % 2) * T:(g % 2 + 1) * T],
                                                      op0=MUL, op1=ADD))
                    vec.wait_ge(k.vec_chain.sem, k.vec_chain.n)
                    vec.tensor_reduce(neg_max[:, tile:tile + 1], sc[:, tile].rearrange("p g n -> p (g n)"), X, MAX,
                                      negate=True).then_inc(turn_tile[tile].sem, 1)
                for tile in range(TILES):
                    turn(vec, tile, h, 6)
                    link(vec.reciprocal(den[:, tile:tile + 1], den[:, tile:tile + 1]))
                    vec.tensor_scalar(b.o[:, tile, h * ADH:(h + 1) * ADH], k.ps[:, 4 * tile, 0:ADH], den[:, tile:tile + 1],
                                      None, MUL).then_inc(turn_tile[tile].sem, 1)
            for tile in range(TILES):
                turn(vec, tile, AH, 0)
    k.pool_done.close(1)
    for sig in turn_tile:
        sig.close(AH * STEPS)


def rms_rows_phase(k, gain):
    c = Carver(k.region, k.region_w)
    row, sq = c.take(D), c.take(D)
    ss = k.stat[:, 0:TILES]
    with k.nc.Block() as block:
        @block.sync
        def _(sp):
            sp.dma_start(row, gain.partition_broadcast(P)).then_inc(k.small_landed.sem, 16)

        @block.scalar
        def _(act):
            act.wait_ge(k.vec_done.sem, k.vec_done.at(1))
            act.activation(ss, ss, ACT.Sqrt).then_inc(k.act_done.sem, 1)

        @block.vector
        def _(vec):
            link = lambda ins: k.vec_chain.link(vec, ins)
            for tile in range(TILES):
                link(vec.tensor_tensor_reduce(sq, k.x[:, tile], k.x[:, tile], 1.0, 0.0, MUL, ADD, ss[:, tile:tile + 1]))
            link(vec.tensor_scalar(ss, ss, 1.0 / D, RMS_EPS, MUL, ADD))
            vec.sem_inc(k.vec_done.sem, 1)
            vec.wait_ge(k.small_landed.sem, k.small_landed.at(16))
            vec.wait_ge(k.act_done.sem, k.act_done.at(1))
            link(vec.reciprocal(ss, ss))
            for tile in range(TILES):
                link(vec.scalar_tensor_tensor(out=k.x[:, tile], in0=k.x[:, tile], scalar=ss[:, tile:tile + 1], in1=row,
                                              op0=MUL, op1=MUL))
    k.small_landed.close(16)
    k.vec_done.close(1)
    k.act_done.close(1)


def layer_norm_phase(k, gain, bias, n_used, extra=None):
    c = Carver(k.region, k.region_w)
    row, off, sq = c.take(D), c.take(D), c.take(D)
    mean, var = k.stat[:, 0:TILES], k.stat[:, TILES:2 * TILES]
    with k.nc.Block() as block:
        @block.sync
        def _(sp):
            sp.dma_start(row, gain.partition_broadcast(P)).then_inc(k.small_landed.sem, 16)
            sp.dma_start(off, bias.partition_broadcast(P)).then_inc(k.small_landed.sem, 16)
            ahead(k, sp, n_used)

        @block.scalar
        def _(act):
            act.wait_ge(k.vec_done.sem, k.vec_done.at(1))
            act.activation(var, var, ACT.Sqrt).then_inc(k.act_done.sem, 1)

        @block.vector
        def _(vec):
            link = lambda ins: k.vec_chain.link(vec, ins)
            mark = k.vec_chain.mark
            used_up(k, vec, n_used)
            link(vec.scalar_tensor_tensor(out=k.x[:, :, :], in0=k.x[:, :, :], scalar=ALPHA,
                                          in1=v3(bank(k, 0, 4), TILES, D), op0=MUL, op1=ADD))
            if extra is not None:
                link(vec.tensor_tensor(k.x[:, :, :], k.x[:, :, :], extra, ADD))
            link(vec.tensor_reduce(mean, k.x[:, :, :], X, ADD))
            link(vec.tensor_scalar(mean, mean, 1.0 / D, None, MUL))
            for tile in range(TILES):
                link(vec.tensor_scalar(k.x[:, tile], k.x[:, tile], mean[:, tile:tile + 1], None, SUB))
                link(vec.tensor_tensor_reduce(sq, k.x[:, tile], k.x[:, tile], 1.0, 0.0, MUL, ADD, var[:, tile:tile + 1]))
            link(vec.tensor_scalar(var, var, 1.0 / D, LN_EPS, MUL, ADD))
            vec.sem_inc(k.vec_done.sem, 1)
            vec.wait_ge(k.small_landed.sem, k.small_landed.at(32))
            vec.wait_ge(k.act_done.sem, k.act_done.at(1))
            link(vec.reciprocal(var, var))
            for tile in range(TILES):
                link(vec.scalar_tensor_tensor(out=k.x[:, tile], in0=k.x[:, tile], scalar=var[:, tile:tile + 1], in1=row,
                                              op0=MUL, op1=MUL))
            link(vec.tensor_tensor(k.x[:, :, :], k.x[:, :, :], v3(off, 1, D).to_broadcast([P, TILES, D]), ADD))
    k.small_landed.close(32)
    k.vec_done.close(1)
    k.act_done.close(1)


SLICES = ("dq", "dk", "sq", "sk", "iq")
SLOT_OF = {name: 4 * j for j, name in enumerate(SLICES)}
IK_SLOT = 4 * len(SLICES)


def second_buffers(k):
    c = Carver(k.region, k.region_w)
    b = Core()
    b.h = v3(c.take(TILES * SEG["ga"]), TILES, SEG["ga"])
    b.sg = c.take(2 * TILES * D).rearrange("p (j t d) -> p j t d", j=2, t=TILES)
    b.f = v3(c.take((IK_SLOT + 1) * T), IK_SLOT + 1, T)
    b.ya, b.yb = (v3(c.take(TILES * 4 * P), TILES, 4 * P) for _ in range(2))
    b.ik2 = v3(c.take(TILES * P), TILES, P)
    b.lam = c.take(4)
    b.end = c.at
    return b


def w_in_phase(k, b, i):
    n0 = k.starts[f"win{i}"]
    spans = [(0, D), (D, D), (2 * D, D), (3 * D, SEG["ga"] - 3 * D), (SEG["ga"], D), (SEG["gb"], D)]
    with k.nc.Block() as block:
        @block.sync
        def _(sp):
            ahead(k, sp, n0 + 4 * len(spans))

        @block.tensor
        def _(pe):
            for n, (c0, width) in enumerate(spans):
                if n >= 2:
                    pe.wait_ge(k.act_done.sem, k.act_done.at(n - 1))
                project_tokens(k, pe, n0 + 4 * n, k.xT, K8, width, n % 2)

        @block.scalar
        def _(act):
            for n, (c0, width) in enumerate(spans):
                used_up(k, act, n0 + 4 * (n + 1))
                src = v3(bank(k, 4 * (n % 2), 4), TILES, D)[:, :, 0:width]
                if n < 4:
                    ins = act.activation(b.h[:, :, c0:c0 + width], src, ACT.Copy)
                else:
                    ins = act.activation(b.sg[:, n - 4], src, ACT.Sigmoid)
                ins.then_inc(k.act_done.sem, 1)
    k.act_done.close(len(spans))


def rotary_phase(k, b, i):
    R2 = ROT // 2
    s = Carver(k.arena, SLOTS * SLOT)
    t1, t2, t3, t4 = (s.take(TILES * 16 * R2).rearrange("p (t h r) -> p t h r", t=TILES, r=R2) for _ in range(4))
    lp = v3(s.take(4 * HN), 4, HN)
    lt = v3(s.take(2 * HN), 2, HN)
    lam_init = 0.8 - 0.6 * math.exp(-0.3 * i)
    groups = [[(seg, j) for seg in SLICES for j in range(4)][g:g + 2] for g in range(0, IK_SLOT, 2)] + [[("ik", 0)]]
    with k.nc.Block() as block:
        @block.sync
        def _(sp):
            sp.dma_start(lp.rearrange("p j n -> p (j n)"),
                         k.a["diff_lambda_2"][i].rearrange("j n -> (j n)").partition_broadcast(P)).then_inc(k.small_landed.sem, 16)

        @block.vector
        def _(vec):
            link = lambda ins: k.vec_chain.link(vec, ins)
            mark = k.vec_chain.mark
            for c0, heads in ((SEG["dq"], 16), (SEG["sq"], 16), (SEG["iq"], 9)):
                v = b.h[:, :, c0:c0 + heads * HN].rearrange("p t (h n) -> p t h n", n=HN)
                x1, x2 = v[:, :, :, 0:R2], v[:, :, :, R2:ROT]
                cos, sin = (tab[:, :, :].rearrange("p t (a r) -> p t a r", a=1).to_broadcast([P, TILES, heads, R2])
                            for tab in (k.cos, k.sin))
                a1, a2, a3, a4 = (t[:, :, 0:heads] for t in (t1, t2, t3, t4))
                mark(vec.tensor_tensor(a1, x1, cos, MUL))
                mark(vec.tensor_tensor(a2, x2, sin, MUL))
                mark(vec.tensor_tensor(a3, x2, cos, MUL))
                link(vec.tensor_tensor(a4, x1, sin, MUL))
                mark(vec.tensor_tensor(x1, a1, a2, SUB))
                link(vec.tensor_tensor(x2, a3, a4, ADD))
            for r in range(2):
                mark(vec.tensor_copy(b.ik2[:, :, r * HN:(r + 1) * HN], b.h[:, :, SEG["ik"]:SEG["ik"] + HN]))
            vec.wait_ge(k.vec_chain.sem, k.vec_chain.n)
            vec.sem_inc(k.vec_done.sem, 1)
            vec.wait_ge(k.small_landed.sem, k.small_landed.at(16))
            l4 = lp.rearrange("p (a b) n -> p a b n", b=2)
            link(vec.tensor_tensor(lt, l4[:, :, 0], l4[:, :, 1], MUL))
            link(vec.tensor_reduce(b.lam[:, 0:2], lt, X, ADD))
            vec.sem_inc(k.vec_done.sem, 1)
            vec.wait_ge(k.act_done.sem, k.act_done.at(1))
            link(vec.tensor_tensor(b.lam[:, 2:3], b.lam[:, 1:2], b.lam[:, 0:1], SUB))
            link(vec.tensor_scalar(b.lam[:, 2:3], b.lam[:, 2:3], -lam_init, None, ADD))

        @block.tensor
        def _(pe):
            pe.wait_ge(k.vec_done.sem, k.vec_done.at(1))
            for g, members in enumerate(groups):
                if g >= 8:
                    pe.wait_ge(k.act_done.sem, k.act_done.at(1 + g - 7))
                for m, (seg, j) in enumerate(members):
                    for tile in range(TILES):
                        src = b.ik2[:, tile] if seg == "ik" else b.h[:, tile, SEG[seg] + j * P:SEG[seg] + (j + 1) * P]
                        at = m * T + tile * P
                        mm = pe.transpose(k.ps[:, g % 8, at:at + P], src, k.ident[:, :])
                mm.then_inc(k.pe_done.sem, 1)

        @block.scalar
        def _(act):
            act.wait_ge(k.vec_done.sem, k.vec_done.at(2))
            act.activation(b.lam[:, 0:2], b.lam[:, 0:2], ACT.Exp).then_inc(k.act_done.sem, 1)
            for g, members in enumerate(groups):
                act.wait_ge(k.pe_done.sem, k.pe_done.at(g + 1))
                n = len(members)
                act.activation(b.f[:, 2 * g:2 * g + n], v3(k.ps[:, g % 8, 0:n * T], n, T), ACT.Copy).then_inc(k.act_done.sem, 1)
    k.small_landed.close(16)
    k.vec_done.close(2)
    k.pe_done.close(len(groups))
    k.act_done.close(1 + len(groups))


def pair_attention_phase(k, b, i):
    s = Carver(k.arena, SLOTS * SLOT)
    causal = v3(s.take(TILES * T), TILES, T)
    mask = v3(s.take(TILES * T), TILES, T)
    work, best = v3(s.take(TILES * T), TILES, T), v3(s.take(TILES * 8), TILES, 8)
    relu = s.take(TILES * 8 * T).rearrange("p (t h n) -> p t h n", t=TILES, h=8)
    iw = v3(s.take(TILES * SH), TILES, SH)
    sc = s.take(TILES * 2 * T).rearrange("p (t w n) -> p t w n", t=TILES, w=2)
    pT = s.take(TILES * 2 * T).rearrange("p (t w n) -> p t w n", t=TILES, w=2)
    neg_max, den = v3(s.take(TILES * 2), TILES, 2), v3(s.take(TILES * 2), TILES, 2)
    scale = HN ** -0.5
    IDX, STEPS = 3, 8
    turn_tile = (k.turn_tile0, k.turn_tile1)

    def turn(eng, tile, unit_, done):
        n = IDX + unit_ * STEPS + done
        eng.wait_ge(turn_tile[tile].sem, turn_tile[tile].at(n))

    def end(ins, tile):
        ins.then_inc(turn_tile[tile].sem, 1)

    def keys(tile):
        return (tile + 1) * P

    with k.nc.Block() as block:
        @block.gpsimd
        def _(pool):
            k.pool_chain.link(pool, pool.memset(causal, 0.0))
            for tile in range(TILES):
                k.pool_chain.link(pool, pool.affine_select(out=causal[:, tile], in_=causal[:, tile], pattern=[[-1, T]],
                                                           compare_op=ALU.is_ge, fill=-BIG, base=tile * P,
                                                           channel_multiplier=1))
            pool.sem_inc(k.pool_done.sem, 1)

        @block.tensor
        def _(pe):
            for tile in range(TILES):
                for hd in range(SH):
                    par, pair = hd % 2, hd // 2
                    half = slice(par * HN, (par + 1) * HN)
                    mm = pe.matmul(k.ps[:, 4 * tile + 2 * par + pair // 2, (pair % 2) * T:(pair % 2) * T + keys(tile)],
                                   b.f[half, SLOT_OF["iq"] + pair, tile * P:(tile + 1) * P], b.f[half, IK_SLOT, 0:keys(tile)],
                                   start=True, stop=True)
                end(mm, tile)
            for u in range(DH + SH // 2):
                qs, ks = (SLOT_OF["dq"] + u, SLOT_OF["dk"] + u) if u < DH else (SLOT_OF["sq"] + u - DH, SLOT_OF["sk"] + u - DH)
                for tile in range(TILES):
                    turn(pe, tile, u, 0)
                    for w in range(2):
                        half = slice(w * HN, (w + 1) * HN)
                        mm = pe.matmul(k.ps[:, 4 * tile + w, 0:keys(tile)], b.f[half, qs, tile * P:(tile + 1) * P],
                                       b.f[half, ks, 0:keys(tile)], start=True, stop=True)
                    end(mm, tile)
                for tile in range(TILES):
                    turn(pe, tile, u, 4)
                    for w in range(1 if u < DH else 2):
                        for n in range(tile + 1):
                            at = w * T + n * P
                            mm = pe.transpose(k.ps[:, 4 * tile + 2, at:at + P], sc[:, tile, w, n * P:(n + 1) * P], k.ident[:, :])
                    end(mm, tile)
                for tile in range(TILES):
                    turn(pe, tile, u, 6)
                    for w in range(1 if u < DH else 2):
                        width = P if u < DH else HN
                        c0 = SEG["dv"] + u * P if u < DH else SEG["sv"] + ((u - DH) * 2 + w) * HN
                        for n in range(tile + 1):
                            mm = pe.matmul(k.ps[:, 4 * tile + 3, w * HN:w * HN + width], pT[:, tile, w, n * P:(n + 1) * P],
                                           b.h[:, n, c0:c0 + width], start=(n == 0), stop=(n == tile))
                    end(mm, tile)

        @block.scalar
        def _(act):
            for tile in range(TILES):
                act.wait_ge(turn_tile[tile].sem, turn_tile[tile].at(1))
                end(act.activation(relu[:, tile, :, 0:keys(tile)], v3(bank(k, 4 * tile, 4), 8, T)[:, :, 0:keys(tile)],
                                   ACT.Relu, scale=scale), tile)
            for u in range(DH + SH // 2):
                for tile in range(TILES):
                    turn(act, tile, u, 2)
                    for w in range(2):
                        k.act_chain.mark(act.activation(sc[:, tile, w, 0:keys(tile)], sc[:, tile, w, 0:keys(tile)], ACT.Exp,
                                                        bias=neg_max[:, tile, w:w + 1], accum_out=den[:, tile, w:w + 1]))
                    act.wait_ge(k.act_chain.sem, k.act_chain.n)
                    act.sem_inc(turn_tile[tile].sem, 1)
                for tile in range(TILES):
                    turn(act, tile, u, 5)
                    n = 1 if u < DH else 2
                    end(act.activation(pT[:, tile, 0:n, 0:keys(tile)], v3(k.ps[:, 4 * tile + 2, 0:n * T], n, T)[:, :, 0:keys(tile)],
                                       ACT.Copy), tile)

        @block.vector
        def _(vec):
            link = lambda ins: k.vec_chain.link(vec, ins)
            mark = k.vec_chain.mark
            link(vec.tensor_scalar(iw, b.h[:, :, SEG["iw"]:SEG["iw"] + SH], SH ** -0.5, None, MUL))
            vec.wait_ge(k.pool_done.sem, k.pool_done.at(1))
            for tile in range(TILES):
                vec.wait_ge(turn_tile[tile].sem, turn_tile[tile].at(2))
                n = keys(tile)
                wk = work[:, tile, 0:n]
                for hd in range(SH):
                    r = relu[:, tile, (hd % 2) * 4 + hd // 2, 0:n]
                    if hd == 0:
                        link(vec.tensor_scalar(wk, r, iw[:, tile, 0:1], None, MUL))
                    else:
                        link(vec.scalar_tensor_tensor(out=wk, in0=r, scalar=iw[:, tile, hd:hd + 1], in1=wk, op0=MUL, op1=ADD))
                link(vec.tensor_tensor(wk, wk, causal[:, tile, 0:n], ADD))
                for _ in range(TOPK // 8):
                    link(vec.max(best[:, tile], wk))
                    link(vec.match_replace(wk, best[:, tile], wk, -3e38))
                link(vec.tensor_scalar(mask[:, tile, 0:n], wk, -2e38, -BIG, ALU.is_gt, MUL))
                link(vec.tensor_tensor(mask[:, tile, 0:n], mask[:, tile, 0:n], causal[:, tile, 0:n], ADD))
                vec.sem_inc(turn_tile[tile].sem, 1)
            for u in range(DH + SH // 2):
                hide = causal if u < DH else mask
                for tile in range(TILES):
                    turn(vec, tile, u, 1)
                    n = keys(tile)
                    link(vec.scalar_tensor_tensor(out=sc[:, tile, :, 0:n], in0=k.ps[:, 4 * tile:4 * tile + 2, 0:n], scalar=scale,
                                                  in1=hide[:, tile:tile + 1, 0:n].to_broadcast([P, 2, n]), op0=MUL, op1=ADD))
                    end(vec.tensor_reduce(neg_max[:, tile], sc[:, tile, :, 0:n], X, MAX, negate=True), tile)
                for tile in range(TILES):
                    turn(vec, tile, u, 3)
                    n = keys(tile)
                    link(vec.reciprocal(den[:, tile], den[:, tile]))
                    if u < DH:
                        link(vec.tensor_tensor(den[:, tile, 1:2], den[:, tile, 1:2], b.lam[:, 2:3], MUL))
                        link(vec.tensor_scalar(sc[:, tile, 0, 0:n], sc[:, tile, 0, 0:n], den[:, tile, 0:1], None, MUL))
                        end(vec.scalar_tensor_tensor(out=sc[:, tile, 0, 0:n], in0=sc[:, tile, 1, 0:n], scalar=den[:, tile, 1:2],
                                                     in1=sc[:, tile, 0, 0:n], op0=MUL, op1=ADD), tile)
                    else:
                        vec.sem_inc(turn_tile[tile].sem, 1)
                for tile in range(TILES):
                    turn(vec, tile, u, 7)
                    src = k.ps[:, 4 * tile + 3, 0:P]
                    if u < DH:
                        end(vec.tensor_copy(b.ya[:, tile, u * P:(u + 1) * P], src), tile)
                    else:
                        end(vec.tensor_tensor(v3(b.yb[:, tile, (u - DH) * P:(u - DH + 1) * P], 2, HN), v3(src, 2, HN),
                                              den[:, tile].rearrange("p (w a) -> p w a", a=1).to_broadcast([P, 2, HN]), MUL), tile)
    k.pool_done.close(1)
    for sig in turn_tile:
        sig.close(IDX + (DH + SH // 2) * STEPS)


def subnorm_phase(k, b, i, end):
    lam_init = 0.8 - 0.6 * math.exp(-0.3 * i)
    c = Carver(k.region, k.region_w, b.end)
    gain = c.take(P)
    rms = c.take(TILES * DH)
    sq = v3(b.f[:, 0:4].rearrange("p s t -> p (s t)"), TILES * DH, P)
    y = b.ya.rearrange("p t (h n) -> p (t h) n", n=P)
    with k.nc.Block() as block:
        @block.sync
        def _(sp):
            sp.dma_start(gain, k.a["diff_subln_g_2"][i].partition_broadcast(P)).then_inc(k.small_landed.sem, 16)
            ahead(k, sp, end)

        @block.scalar
        def _(act):
            act.wait_ge(k.vec_done.sem, k.vec_done.at(1))
            act.activation(rms, rms, ACT.Sqrt).then_inc(k.act_done.sem, 1)

        @block.vector
        def _(vec):
            link = lambda ins: k.vec_chain.link(vec, ins)
            link(vec.tensor_tensor(sq, y, y, MUL))
            link(vec.tensor_reduce(rms, sq, X, ADD))
            link(vec.tensor_scalar(rms, rms, 1.0 / P, LN_EPS, MUL, ADD))
            vec.sem_inc(k.vec_done.sem, 1)
            vec.wait_ge(k.act_done.sem, k.act_done.at(1))
            link(vec.reciprocal(rms, rms))
            link(vec.tensor_scalar(rms, rms, 1.0 - lam_init, None, MUL))
            link(vec.tensor_tensor(y, y, rms.rearrange("p (h a) -> p h a", a=1).to_broadcast([P, TILES * DH, P]), MUL))
            vec.wait_ge(k.small_landed.sem, k.small_landed.at(16))
            link(vec.tensor_tensor(y, y, v3(gain, 1, P).to_broadcast([P, TILES * DH, P]), MUL))
    k.small_landed.close(16)
    k.vec_done.close(1)
    k.act_done.close(1)


def two_products_phase(k, names, lhs, rows, finish):
    n0, n1 = (k.starts[n] for n in names)
    end = n1 + rows[1] // 2
    with k.nc.Block() as block:
        @block.sync
        def _(sp):
            ahead(k, sp, end)

        @block.tensor
        def _(pe):
            project_tokens(k, pe, n0, lhs[0], rows[0], D, 0)
            project_tokens(k, pe, n1, lhs[1], rows[1], D, 1)

        finish(block, n1, end)


def second_layer_phases(k, i):
    a = k.a
    b = second_buffers(k)
    w_in_phase(k, b, i)
    rotary_phase(k, b, i)
    pair_attention_phase(k, b, i)
    subnorm_phase(k, b, i, k.starts[f"wbd{i}"])
    yaT, ybT = b.f[:, 0:4], b.f[:, 4:8]
    to_features_phase(k, b.ya, yaT, 4, k.starts[f"wbd{i}"])
    to_features_phase(k, b.yb, ybT, 4, k.starts[f"wbd{i}"])
    merged = v3(k.region[:, 0:TILES * D], TILES, D)
    mergedT = v3(k.region[:, TILES * D:2 * TILES * D], K8, T)

    def merge(block, first, end):
        @block.vector
        def _(vec):
            link = lambda ins: k.vec_chain.link(vec, ins)
            used_up(k, vec, first)
            link(vec.tensor_tensor(merged, v3(bank(k, 0, 4), TILES, D), b.sg[:, 0], MUL))
            used_up(k, vec, end)
            link(vec.tensor_tensor(b.sg[:, 1], v3(bank(k, 4, 4), TILES, D), b.sg[:, 1], MUL))
            link(vec.tensor_tensor(merged, merged, b.sg[:, 1], ADD))

    two_products_phase(k, (f"wbd{i}", f"wbs{i}"), (yaT, ybT), (4, 4), merge)
    to_features_phase(k, merged, mergedT, K8, k.starts[f"wout{i}"])
    n0 = k.starts[f"wout{i}"]
    with k.nc.Block() as block:
        @block.sync
        def _(sp):
            ahead(k, sp, n0 + 4)

        @block.tensor
        def _(pe):
            project_tokens(k, pe, n0, mergedT, K8, D, 0)
    layer_norm_phase(k, a["ln1_g_2"][i], a["ln1_b_2"][i], n0 + 4)
    to_features_phase(k, k.x, k.xT, K8, k.starts[f"pleg{i}"])

    c = Carver(k.region, k.region_w, k.region_w - 2 * TILES * D)
    ple = v3(c.take(TILES * D), TILES, D)
    p_tok, pT = v3(c.take(TILES * T), TILES, T), v3(c.take(2 * T), 2, T)
    with k.nc.Block() as block:
        @block.sync
        def _(sp):
            sp.dma_start(p_tok, a["p_2"][i, 0].rearrange("(t p) d -> p t d", p=P)).then_inc(k.small_landed.sem, 16)

        @block.vector
        def _(vec):
            vec.wait_ge(k.small_landed.sem, k.small_landed.at(16))
    k.small_landed.close(16)
    to_features_phase(k, p_tok, pT, 2, k.starts[f"pleg{i}"])

    def embed(block, first, end):
        @block.scalar
        def _(act):
            used_up(k, act, first)
            act.activation(ple, v3(bank(k, 0, 4), TILES, D), ACT.Sigmoid).then_inc(k.act_done.sem, 1)

        @block.vector
        def _(vec):
            vec.wait_ge(k.act_done.sem, k.act_done.at(1))
            used_up(k, vec, end)
            k.vec_chain.link(vec, vec.tensor_tensor(ple, ple, v3(bank(k, 4, 4), TILES, D), MUL))

    two_products_phase(k, (f"pleg{i}", f"ple{i}"), (k.xT, pT), (K8, 2), embed)
    k.act_done.close(1)
    route_phase(k, DEPTH + i, k.starts[f"moe{DEPTH + i}"])
    experts_phase(k, DEPTH + i)
    layer_norm_phase(k, a["ln2_g_2"][i], a["ln2_b_2"][i], k.starts[f"moe{DEPTH + i}"] + 3 * EXPERTS, extra=ple)


def build(nc, a, out, upto=None):
    with ExitStack() as ctx:
        k = make_core(nc, ctx, a)
        phases = []

        def phase(name, f):
            phases.append((name, f))

        for i in range(DEPTH):
            phase(f"ada{i}", lambda i=i: ada_phase(k, i))
            first = "rkv0" if i == 0 else "qkv"
            phase(f"norm_tm{i}", lambda i=i, f=first: to_features_phase(k, k.x, k.xT, K8, k.starts[f], norm=0))
            if i == 0:
                def mix():
                    b = rwkv_buffers(k)
                    rwkv_project_phase(k, b)
                    og = rwkv_mix_phase(k, b)
                    k.mixT = v3(k.region[:, b.end:b.end + T * K8], K8, T)
                    to_features_phase(k, og, k.mixT, K8, k.starts["rwo"])
                    residual_phase(k, "rwo", k.mixT, 0)
                phase("rwkv", mix)

            else:
                def mix():
                    b = Core()
                    qkv_phase(k, b)
                    dilated_phase(k, b)
                    mixT = v3(k.region[:, 0:T * K8], K8, T)
                    to_features_phase(k, b.o, mixT, K8, k.starts["awo"])
                    residual_phase(k, "awo", mixT, 0)
                phase("dilated", mix)

            def moe(i=i):
                to_features_phase(k, k.x, k.xT, K8, k.starts[f"moe{i}"], norm=1)
                route_phase(k, i, k.starts[f"moe{i}"])
                experts_phase(k, i)
                moe_residual_phase(k, i)
            phase(f"moe{i}", moe)
        phase("final", lambda: rms_rows_phase(k, a["final_g"]))
        for i in range(DEPTH):
            phase(f"second_x{i}", lambda i=i: to_features_phase(k, k.x, k.xT, K8, k.starts[f"win{i}"]))
            phase(f"second{i}", lambda i=i: second_layer_phases(k, i))
        setup_phase(k)
        for name, f in phases:
            f()
            if name == upto:
                break
        src = k.x
        with nc.Block() as block:
            @block.sync
            def _(sp):
                sp.dma_start(out.rearrange("b (t p) d -> p (b t) d", p=P), src[:, :, :]).then_inc(k.stored.sem, 16)
                sp.wait_ge(k.stored.sem, k.stored.at(16))


def kernel(**inputs):
    import numpy as _np
    import concourse.bacc as _bacc
    from concourse import mybir as _mybir
    from concourse.bass_utils import run_bass_kernel_spmd as _run

    nc = _bacc.Bacc("TRN2", target_bir_lowering=False, num_devices=1)
    arrays, args = {}, {}
    for name, value in inputs.items():
        v = _np.ascontiguousarray(value)
        arrays[f"in_{name}"] = v
        args[name] = nc.dram_tensor(f"in_{name}", v.shape, _mybir.dt.from_np(v.dtype), kind="ExternalInput").ap()
    out = nc.dram_tensor("out", (1, T, D), F32, kind="ExternalOutput").ap()
    build(nc, args, out)
    r = _run(nc, [arrays], core_ids=[0])
    return r.results[0]["out"]
```

```python
import math
from contextlib import ExitStack

import numpy as np
import concourse.bass as bass
from concourse import mybir

F32 = mybir.dt.float32
I32 = mybir.dt.int32
ALU = mybir.AluOpType
ACT = mybir.ActivationFunctionType
X = mybir.AxisListType.X
MUL, ADD, SUB, MAX = ALU.mult, ALU.add, ALU.subtract, ALU.max

P = 128
T, D = 256, 1024
TILES = T // P
K8 = D // P
DEPTH = 2
SLOTS, SLOT = 12, 2048
HALF = 512

HEADS, HN = 16, 64
CH = 64
RMS_EPS, GN_EPS, LN_EPS = 1e-6, 64e-5, 1e-5

GROUPS = ((128, 1), (512, 4), (2048, 16))
AH, ADH = 8, 128

N_GROUPS, PER_GROUP = 4, 8
EXPERTS = N_GROUPS * PER_GROUP
F = 256
PAIRS = EXPERTS // 2
CAP = P // 2
UNROLL = 2
FAR = 1e4

SEG = dict(dq=0, dk=512, dv=1024, sq=1536, sk=2048, sv=2560, iq=3072, ik=3584, iw=3648, ga=3656, gb=4680)
W_IN = 5704
DH, SH = 4, 8
TOPK = min(256, T // 4)
ROT = 16
THETA = 500000.0
ALPHA = (2 * DEPTH) ** 0.25
BIG = 1e30


class Signal:

    def __init__(self, sem):
        self.sem, self.base = sem, 0

    def at(self, n):
        return self.base + n

    def close(self, n):
        self.base += n


class Chain:

    def __init__(self, sem):
        self.sem, self.n = sem, 0

    def mark(self, ins):
        self.n += 1
        ins.then_inc(self.sem, 1)

    def link(self, eng, ins):
        self.mark(ins)
        eng.wait_ge(self.sem, self.n)


class Carver:

    def __init__(self, buf, width, start=0):
        self.buf, self.width, self.at = buf, width, start

    def take(self, n):
        assert self.at + n <= self.width, (self.at + n, self.width)
        v = self.buf[:, self.at:self.at + n]
        self.at += n
        return v


class Core:
    pass


def plan_streams(a):

    def jobs(w, spans, per=2):
        rows = w.shape[0] // P
        v = w.rearrange("(p k) n -> p k n", k=rows)
        return [v[:, per * u:per * (u + 1), c0:c0 + n] for c0, n in spans for u in range(rows // per)]

    def wide(n):
        return [(c, min(D, n - c)) for c in range(0, n, D)]

    def moe(i, gate, up, down):
        g = gate[i].rearrange("g e (p k) f -> (g e) p (k f)", k=K8)
        u = up[i].rearrange("g e (p k) f -> (g e) p (k f)", k=K8)
        d = down[i].rearrange("g e (p j) n -> (g e) p (j n)", j=2)
        order = [g[0], u[0], g[1], u[1]]
        for e in range(0, EXPERTS - 2, 2):
            order += [g[e + 2], u[e + 2], g[e + 3], u[e + 3], d[e], d[e + 1]]
        return order + [d[EXPERTS - 2], d[EXPERTS - 1]]

    plan = []
    for i in range(DEPTH):
        plan.append((f"ada{i}", jobs(a["ada_w"][i], wide(6 * D))))
        if i == 0:
            for j in range(3):
                plan.append((f"rkv{j}", jobs(a["rw_w_rkv"][0, j], wide(D))))
            plan.append(("scratch", []))
            plan.append(("rwo", jobs(a["rw_w_o"][0], wide(D))))
        else:
            plan.append(("qkv", jobs(a["at_w_qkv"][0], wide(9 * D))))
            plan.append(("scratch", []))
            plan.append(("awo", jobs(a["at_w_o"][0], wide(D))))
        plan.append((f"moe{i}", moe(i, a["moe_w_gate"], a["moe_w_up"], a["moe_w_down"])))
    for i in range(DEPTH):
        spans = [(0, D), (D, D), (2 * D, D), (3 * D, SEG["ga"] - 3 * D), (SEG["ga"], D), (SEG["gb"], D)]
        plan.append((f"win{i}", jobs(a["w_in_2"][i], spans)))
        plan.append(("scratch", []))
        plan.append((f"wbd{i}", jobs(a["w_branch_diff_2"][i], wide(D))))
        plan.append((f"wbs{i}", jobs(a["w_branch_dsa_2"][i], wide(D))))
        plan.append((f"wout{i}", jobs(a["w_out_2"][i], wide(D))))
        plan.append((f"pleg{i}", jobs(a["w_ple_gate_2"][i], wide(D))))
        plan.append((f"ple{i}", jobs(a["w_ple_2"][i], wide(D), per=1)))
        plan.append((f"moe{DEPTH + i}", moe(i, a["w_exp_gate_2"], a["w_exp_up_2"], a["w_exp_down_2"])))
    return plan


def make_core(nc, ctx, a):
    k = Core()
    k.nc, k.a = nc, a

    def sb(name, shape, dt=F32):
        return ctx.enter_context(nc.sbuf_tensor(name, shape, dt))

    k.arena = sb("arena", [P, SLOTS * SLOT])
    k.region_w = 21248
    k.region = sb("region", [P, k.region_w])
    k.x = sb("x_tokens", [P, TILES, D])
    k.xT = sb("x_features", [P, K8, T])
    k.gate_row = sb("gate_rows", [P, 2, D])
    k.mod = sb("mod_columns", [P, 6, K8])
    k.scale_col = sb("scale_columns", [P, 2, K8])
    k.ident = sb("identity", [P, P])
    k.desc = sb("descending", [P, PER_GROUP])
    k.stat = sb("statistics", [P, 64])
    k.cos = sb("cos", [P, TILES, ROT // 2])
    k.sin = sb("sin", [P, TILES, ROT // 2])
    k.ps = ctx.enter_context(nc.psum_tensor("ps", [P, 8, HALF], F32))

    def sem(name):
        return ctx.enter_context(nc.semaphore(name))

    k.landed = [sem(f"slot_landed{s}") for s in range(SLOTS)]
    k.used = sem("units_used")
    k.vec_chain = Chain(sem("vector_chain"))
    k.act_chain = Chain(sem("scalar_chain"))
    k.pool_chain = Chain(sem("gpsimd_chain"))
    k.small_landed, k.stored = Signal(sem("small_landed")), Signal(sem("stored"))
    k.pe_done, k.vec_done = Signal(sem("pe_done")), Signal(sem("vec_done"))
    k.act_done, k.pool_done = Signal(sem("act_done")), Signal(sem("pool_done"))
    (k.slots_built, k.gated_built, k.gathered, k.tokens_half0, k.tokens_half1, k.turned, k.hidden_moved,
     k.gated_moved, k.silu_ready, k.hidden_ready, k.out_half, k.out_moved0, k.out_moved1) = (
        Signal(sem(name)) for name in (
            "slots_built", "gated_built", "gathered", "tokens_half0", "tokens_half1", "turned", "hidden_moved",
            "gated_moved", "silu_ready", "hidden_ready", "out_half", "out_moved0", "out_moved1"))
    k.over_landed = [sem(f"overflow_landed{i}") for i in range(2 * DEPTH)]
    k.over_turn = [sem(f"overflow_turn{i}") for i in range(2 * DEPTH)]
    k.turn_joint, k.turn_tile0, k.turn_tile1 = (Signal(sem(f"turn_{n}")) for n in ("joint", "tile0", "tile1"))
    k.plan, k.starts, k.stops, n = [], {}, [], 0
    for name, units in plan_streams(a):
        if name == "scratch":
            k.stops.append(n)
            continue
        k.starts[name] = n
        k.plan += units
        n += len(units)
        assert n % 2 == 0, "gate and up projections take neighbouring slots"
    k.issued = 0
    return k


def issue(k, sp, upto):
    for n in range(k.issued, min(upto, len(k.plan))):
        src = k.plan[n]
        size = int(np.prod(src.shape[1:]))
        at = (n % SLOTS) * SLOT
        dst = k.arena[:, at:at + size]
        if len(src.shape) == 3:
            dst = dst.rearrange("p (k n) -> p k n", k=src.shape[1])
        if n >= SLOTS:
            sp.wait_ge(k.used, n - SLOTS + 1)
        sp.dma_start(dst, src).then_inc(k.landed[n % SLOTS], 16)
    k.issued = max(k.issued, min(upto, len(k.plan)))


def ahead(k, sp, end):
    stop = min([s for s in k.stops if s >= end], default=len(k.plan))
    issue(k, sp, end)
    issue(k, sp, min(end + SLOTS, stop))


def landed(k, pe, n):
    pe.wait_ge(k.landed[n % SLOTS], 16 * (n // SLOTS + 1))


def used_up(k, eng, n):
    eng.wait_ge(k.used, n)


def unit(k, n, width, per=2):
    at = (n % SLOTS) * SLOT
    return k.arena[:, at:at + per * width].rearrange("p (k n) -> p k n", k=per)


def bank(k, b, n=1):
    return k.ps[:, b:b + n, :].rearrange("p b n -> p (b n)")


def project_tokens(k, pe, n0, xT, rows, width, set_, per=2):
    halves = [(0, min(HALF, width))] + ([(HALF, width - HALF)] if width > HALF else [])
    for u in range(rows // per):
        landed(k, pe, n0 + u)
        w = unit(k, n0 + u, width, per)
        for kk in range(per):
            s = per * u + kk
            for tile in range(TILES):
                for h, (c0, n) in enumerate(halves):
                    mm = pe.matmul(k.ps[:, set_ * 4 + tile * 2 + h, 0:n], xT[:, s, tile * P:(tile + 1) * P],
                                   w[:, kk, c0:c0 + n], start=(s == 0), stop=(s == rows - 1))
        mm.then_inc(k.used, 1)


def project_features(k, pe, n0, xT, rows, set_):
    for u in range(rows // 2):
        landed(k, pe, n0 + u)
        w = unit(k, n0 + u, D)
        for kk in range(2):
            s = 2 * u + kk
            for m in range(K8):
                mm = pe.matmul(k.ps[:, set_ * 4 + m // 2, (m % 2) * T:(m % 2 + 1) * T],
                               w[:, kk, m * P:(m + 1) * P], xT[:, s, :],
                               start=(s == 0 and m % 2 == 0), stop=(s == rows - 1), skip_group_check=True)
        mm.then_inc(k.used, 1)


def setup_phase(k):
    a = k.a
    c = Carver(k.region, k.region_w)
    pos = c.take(TILES).bitcast(I32)
    posf = c.take(TILES)
    freq = c.take(ROT // 2)
    ang, turns, red = (c.take(TILES * ROT // 2).rearrange("p (t r) -> p t r", t=TILES) for _ in range(3))
    inv = (np.float32(1.0) / np.float32(THETA) ** (np.arange(0, ROT, 2, dtype=np.float32) / np.float32(ROT)))
    two_pi = 2 * math.pi
    hi = float(np.float32(6.28125))
    mid = float(np.float32(np.round((two_pi - hi) * 2 ** 18) / 2 ** 18))
    lo = float(np.float32(two_pi - hi - mid))
    ROUND = float(np.float32(1.5 * 2 ** 23))

    with k.nc.Block() as block:
        @block.sync
        def _(sp):
            sp.dma_start(k.x[:, :, :], a["x"].rearrange("b (t p) d -> p (b t) d", p=P)).then_inc(k.small_landed.sem, 16)
            sp.dma_start(pos, a["positions_2"].rearrange("b (t p) -> p (b t)", p=P),
                         allow_slow_non_contiguous=True).then_inc(k.small_landed.sem, 16)
            ahead(k, sp, 0)

        @block.gpsimd
        def _(pool):
            link = lambda ins: k.pool_chain.link(pool, ins)
            link(pool.memset(k.ident[:, :], 0.0))
            link(pool.affine_select(out=k.ident[:, :], in_=k.ident[:, :], pattern=[[-1, P]], compare_op=ALU.not_equal,
                                    fill=1.0, base=0, channel_multiplier=1))

        @block.vector
        def _(vec):
            link = lambda ins: k.vec_chain.link(vec, ins)
            for j in range(PER_GROUP):
                k.vec_chain.mark(vec.memset(k.desc[:, j:j + 1], float(PER_GROUP - j)))
            for j in range(ROT // 2):
                k.vec_chain.mark(vec.memset(freq[:, j:j + 1], float(inv[j])))
            vec.wait_ge(k.small_landed.sem, k.small_landed.at(32))
            link(vec.tensor_copy(posf, pos))
            f3 = freq.rearrange("p (a r) -> p a r", a=1).to_broadcast([P, TILES, ROT // 2])
            p3 = posf.rearrange("p (t a) -> p t a", a=1).to_broadcast([P, TILES, ROT // 2])
            link(vec.tensor_tensor(ang, p3, f3, MUL))
            link(vec.tensor_scalar(turns, ang, 1.0 / two_pi, None, MUL))
            link(vec.tensor_scalar(turns, turns, ROUND, -ROUND, ADD, ADD))
            link(vec.scalar_tensor_tensor(out=red, in0=turns, scalar=-hi, in1=ang, op0=MUL, op1=ADD))
            link(vec.scalar_tensor_tensor(out=red, in0=turns, scalar=-mid, in1=red, op0=MUL, op1=ADD))
            link(vec.scalar_tensor_tensor(out=red, in0=turns, scalar=-lo, in1=red, op0=MUL, op1=ADD))
            vec.sem_inc(k.vec_done.sem, 1)
            vec.wait_ge(k.act_done.sem, k.act_done.at(1))
            link(vec.tensor_tensor(k.cos[:, :, :], ang, ang, MUL))
            link(vec.tensor_scalar(k.cos[:, :, :], k.cos[:, :, :], -2.0, 1.0, MUL, ADD))

        @block.scalar
        def _(act):
            link = lambda ins: k.act_chain.link(act, ins)
            act.wait_ge(k.vec_done.sem, k.vec_done.at(1))
            link(act.activation(k.sin[:, :, :], red, ACT.Sin))
            link(act.activation(ang, red, ACT.Sin, scale=0.5))
            act.sem_inc(k.act_done.sem, 1)
    k.small_landed.close(32)
    k.vec_done.close(1)
    k.act_done.close(1)


def ada_phase(k, i):
    a = k.a
    n0 = k.starts[f"ada{i}"]
    c = Carver(k.region, k.region_w)
    ccol, silu = c.take(K8), c.take(K8)
    bias = c.take(6 * K8).rearrange("p (j k) -> p j k", j=6)
    gain = c.take(2 * K8).rearrange("p (j k) -> p j k", j=2)
    diag = c.take(2 * D).rearrange("p (g k m) -> p g k m", g=2, k=K8)
    ones = c.take(P)
    small = (
        (ccol, a["c"].rearrange("b (p k) -> p (b k)", k=K8)),
        (bias, a["ada_b"][i].rearrange("(j p k) -> p j k", p=P, k=K8)),
        (gain[:, 0, :], a["norm_tm_g"][i].rearrange("(p k) -> p k", k=K8)),
        (gain[:, 1, :], a["norm_cm_g"][i].rearrange("(p k) -> p k", k=K8)),
    )
    with k.nc.Block() as block:
        @block.sync
        def _(sp):
            ahead(k, sp, n0 + 24)

        @block.scalar
        def _(act):
            for dst, src in small:
                act.dma_start(dst, src).then_inc(k.small_landed.sem, 16)
            act.wait_ge(k.small_landed.sem, k.small_landed.at(64))
            act.activation(silu, ccol, ACT.Silu).then_inc(k.act_done.sem, 1)
            act.wait_ge(k.pe_done.sem, k.pe_done.at(1))
            act.activation(k.gate_row[:, :, :], k.ps[:, 1:5, :].rearrange("p (g h) n -> p g (h n)", g=2),
                           ACT.Copy).then_inc(k.act_done.sem, 1)

        @block.tensor
        def _(pe):
            pe.wait_ge(k.act_done.sem, k.act_done.at(1))
            for j in range(6):
                for u in range(4):
                    landed(k, pe, n0 + 4 * j + u)
                    w = unit(k, n0 + 4 * j + u, D)
                    for kk in range(2):
                        s = 2 * u + kk
                        for f in range(K8):
                            mm = pe.matmul(k.ps[:, 0, j * K8 + f:j * K8 + f + 1], w[:, kk, f:D:K8], silu[:, s:s + 1],
                                           start=(j == 0 and s == 0 and f == 0), stop=(s == K8 - 1),
                                           skip_group_check=True)
                    mm.then_inc(k.used, 1)
            pe.wait_ge(k.vec_done.sem, k.vec_done.at(1))
            for g in range(2):
                for h in range(2):
                    mm = pe.matmul(k.ps[:, 1 + 2 * g + h, :], ones,
                                   diag[:, g, :, h * 64:(h + 1) * 64].rearrange("p k m -> p m k"),
                                   start=True, stop=True)
            mm.then_inc(k.pe_done.sem, 1)

        @block.vector
        def _(vec):
            link = lambda ins: k.vec_chain.link(vec, ins)
            k.vec_chain.mark(vec.memset(ones, 1.0))
            vec.wait_ge(k.small_landed.sem, k.small_landed.at(64))
            used_up(k, vec, n0 + 24)
            link(vec.tensor_tensor(k.mod[:, :, :], k.ps[:, 0, 0:6 * K8].rearrange("p (j k) -> p j k", j=6), bias, ADD))
            for g in range(2):
                k.vec_chain.mark(vec.tensor_tensor(
                    diag[:, g], k.ident[:, :].rearrange("p (a m) -> p a m", a=1).to_broadcast([P, K8, P]),
                    k.mod[:, 3 * g + 2, :].rearrange("p (k a) -> p k a", a=1).to_broadcast([P, K8, P]), MUL))
                link(vec.scalar_tensor_tensor(out=k.scale_col[:, g, :], in0=k.mod[:, 3 * g + 1, :], scalar=1.0,
                                              in1=gain[:, g, :], op0=ADD, op1=MUL))
            vec.sem_inc(k.vec_done.sem, 1)
    k.small_landed.close(64)
    k.act_done.close(2)
    k.pe_done.close(1)
    k.vec_done.close(1)


def transposes(k, pe, src, rows, bank0, cols=None):
    for s in range(rows):
        for tile in range(TILES):
            mm = pe.transpose(k.ps[:, bank0 + s // 2, (s % 2) * T + tile * P:(s % 2) * T + (tile + 1) * P],
                              src[:, tile, s:rows * P:rows], k.ident[:, :])
    return mm


def to_features_phase(k, src, dst, rows, end, norm=None, copy_out=None):
    c = Carver(k.region, k.region_w, k.region_w - TILES * D)
    xn = c.take(TILES * D).rearrange("p (t d) -> p t d", t=TILES)
    ss = k.stat[:, 0:TILES]
    rms = k.stat[:, TILES:2 * TILES]
    with k.nc.Block() as block:
        @block.sync
        def _(sp):
            ahead(k, sp, end)

        if norm is not None:
            @block.scalar
            def _(act):
                act.wait_ge(k.vec_done.sem, k.vec_done.at(1))
                act.activation(rms, rms, ACT.Sqrt).then_inc(k.act_done.sem, 1)

        @block.tensor
        def _(pe):
            if norm is not None:
                pe.wait_ge(k.vec_done.sem, k.vec_done.at(2))
            transposes(k, pe, src if norm is None else xn, rows, 0).then_inc(k.pe_done.sem, 1)

        @block.vector
        def _(vec):
            link = lambda ins: k.vec_chain.link(vec, ins)
            if norm is not None:
                for tile in range(TILES):
                    k.vec_chain.mark(vec.tensor_tensor_reduce(xn[:, tile], src[:, tile], src[:, tile], 1.0, 0.0, MUL,
                                                              ADD, ss[:, tile:tile + 1]))
                vec.wait_ge(k.vec_chain.sem, k.vec_chain.n)
                link(vec.tensor_scalar(rms, ss, 1.0 / D, RMS_EPS, MUL, ADD))
                vec.sem_inc(k.vec_done.sem, 1)
                vec.wait_ge(k.act_done.sem, k.act_done.at(1))
                link(vec.reciprocal(rms, rms))
                for tile in range(TILES):
                    link(vec.tensor_scalar(xn[:, tile], src[:, tile], rms[:, tile:tile + 1], None, MUL))
                vec.sem_inc(k.vec_done.sem, 1)
            vec.wait_ge(k.pe_done.sem, k.pe_done.at(1))
            for s in range(rows):
                t = k.ps[:, s // 2, (s % 2) * T:(s % 2 + 1) * T]
                if norm is None:
                    k.vec_chain.mark(vec.tensor_copy(dst[:, s, :], t))
                else:
                    k.vec_chain.mark(vec.tensor_scalar(dst[:, s, :], t, k.scale_col[:, norm, s:s + 1],
                                                       k.mod[:, 3 * norm, s:s + 1], MUL, ADD))
            vec.wait_ge(k.vec_chain.sem, k.vec_chain.n)
    k.pe_done.close(1)
    if norm is not None:
        k.vec_done.close(2)
        k.act_done.close(1)


def residual_phase(k, name, xT, which):
    n0 = k.starts[name]
    with k.nc.Block() as block:
        @block.sync
        def _(sp):
            ahead(k, sp, n0 + 4)

        @block.tensor
        def _(pe):
            project_tokens(k, pe, n0, xT, K8, D, 0)

        @block.vector
        def _(vec):
            link = lambda ins: k.vec_chain.link(vec, ins)
            used_up(k, vec, n0 + 4)
            add_gated(k, vec, link, which, k.region[:, 0:TILES * D])


def add_gated(k, vec, link, which, scratch):
    tmp = scratch.rearrange("p (t d) -> p t d", t=TILES)
    link(vec.tensor_tensor(tmp, bank(k, 0, 4).rearrange("p (t d) -> p t d", t=TILES),
                           k.gate_row[:, which:which + 1, :].to_broadcast([P, TILES, D]), MUL))
    link(vec.tensor_tensor(k.x[:, :, :], k.x[:, :, :], tmp, ADD))


def v3(ap, a, n):
    return ap.rearrange("p (a n) -> p a n", a=a)


def rwkv_buffers(k):
    c = Carver(k.region, k.region_w)
    b = Core()
    b.r, b.k, b.v = (v3(c.take(TILES * D), TILES, D) for _ in range(3))
    b.tw, b.ta = c.take(T), c.take(T)
    b.tg = v3(c.take(2 * T), 2, T)
    b.end = c.at
    return b


def rwkv_project_phase(k, b):
    a = k.a
    n0 = k.starts["rkv0"]
    c = Carver(k.region, k.region_w, b.end)
    xx = v3(c.take(K8 * T), K8, T)
    xs = c.take(2 * K8 * T).rearrange("p (b k t) -> p b k t", b=2, k=K8)
    mu = v3(c.take(6 * K8), 6, K8)
    w1 = c.take(K8 * P).rearrange("p (k z r) -> p k z r", k=K8, z=2)
    a1 = c.take(K8 * P).rearrange("p (k z r) -> p k z r", k=K8, z=2)
    g1 = c.take(K8 * 2 * P).rearrange("p (k z r) -> p k z r", k=K8, z=2)
    small = [(mu, a["rw_mu"][0].rearrange("j (p k) -> p j k", k=K8))]
    for z in range(2):
        small += [(w1[:, :, z, :], a["rw_w1"][0, z].rearrange("(p k) r -> p k r", k=K8)),
                  (a1[:, :, z, :], a["rw_a1"][0, z].rearrange("(p k) r -> p k r", k=K8)),
                  (g1[:, :, z, :], a["rw_g1"][0, z].rearrange("(p k) r -> p k r", k=K8))]
    n_small = 16 * len(small)
    with k.nc.Block() as block:
        @block.sync
        def _(sp):
            ahead(k, sp, n0 + 12)

        @block.scalar
        def _(act):
            for dst, src in small:
                act.dma_start(dst, src).then_inc(k.small_landed.sem, 16)
            for j, dst in enumerate((b.r, b.k, b.v)):
                used_up(k, act, n0 + 4 * (j + 1))
                act.activation(dst, bank(k, 4 * (j % 2), 4).rearrange("p (t d) -> p t d", t=TILES),
                               ACT.Copy).then_inc(k.act_done.sem, 1)
            act.wait_ge(k.pe_done.sem, k.pe_done.at(1))
            act.activation(b.tw, k.ps[:, 4, 0:T], ACT.Tanh).then_inc(k.act_done.sem, 1)
            act.wait_ge(k.pe_done.sem, k.pe_done.at(2))
            act.activation(b.ta, k.ps[:, 5, 0:T], ACT.Copy).then_inc(k.act_done.sem, 1)
            act.wait_ge(k.pe_done.sem, k.pe_done.at(3))
            act.activation(b.tg, v3(k.ps[:, 6, :], 2, T), ACT.Sigmoid).then_inc(k.act_done.sem, 1)

        @block.vector
        def _(vec):
            link = lambda ins: k.vec_chain.link(vec, ins)
            mark = k.vec_chain.mark
            h = k.xT
            mark(vec.tensor_copy(xx[:, :, 0:1], h[:, :, 1:2]))
            mark(vec.tensor_copy(xx[:, :, T - 1:T], h[:, :, T - 2:T - 1]))
            link(vec.tensor_tensor(xx[:, :, 1:T - 1], h[:, :, 0:T - 2], h[:, :, 2:T], ADD))
            link(vec.scalar_tensor_tensor(out=xx, in0=xx, scalar=0.5, in1=h[:, :, :], op0=MUL, op1=SUB))
            vec.wait_ge(k.small_landed.sem, k.small_landed.at(n_small))
            for j in range(6):
                if 2 <= j < 5:
                    used_up(k, vec, n0 + 4 * (j - 1))
                elif j == 5:
                    vec.wait_ge(k.pe_done.sem, k.pe_done.at(1))
                for s in range(K8):
                    mark(vec.scalar_tensor_tensor(out=xs[:, j % 2, s], in0=xx[:, s], scalar=mu[:, j, s:s + 1],
                                                  in1=h[:, s], op0=MUL, op1=ADD))
                vec.wait_ge(k.vec_chain.sem, k.vec_chain.n)
                vec.sem_inc(k.vec_done.sem, 1)

        @block.tensor
        def _(pe):
            for j in range(3):
                pe.wait_ge(k.vec_done.sem, k.vec_done.at(j + 1))
                if j == 2:
                    pe.wait_ge(k.act_done.sem, k.act_done.at(1))
                project_tokens(k, pe, n0 + 4 * j, xs[:, j % 2], K8, D, j % 2)
            pe.wait_ge(k.act_done.sem, k.act_done.at(2))
            pe.wait_ge(k.small_landed.sem, k.small_landed.at(n_small))
            for j, w in ((3, w1), (4, a1)):
                pe.wait_ge(k.vec_done.sem, k.vec_done.at(j + 1))
                for s in range(K8):
                    mm = pe.matmul(k.ps[:, 1 + j, 0:T], w[:, s].rearrange("p z r -> p (z r)"), xs[:, j % 2, s],
                                   start=(s == 0), stop=(s == K8 - 1))
                mm.then_inc(k.pe_done.sem, 1)
            pe.wait_ge(k.vec_done.sem, k.vec_done.at(6))
            for z in range(2):
                for s in range(K8):
                    mm = pe.matmul(k.ps[:, 6, z * T:(z + 1) * T], g1[:, s, z], xs[:, 1, s],
                                   start=(s == 0), stop=(s == K8 - 1))
            mm.then_inc(k.pe_done.sem, 1)
    k.small_landed.close(n_small)
    k.act_done.close(6)
    k.vec_done.close(6)
    k.pe_done.close(3)


STAGES = tuple(2 ** s for s in range(1, int(math.log2(CH)) + 1))
FS = 256
ORDER = [(par, hp) for par in range(2) for hp in range(2)]


def rwkv_mix_phase(k, b):
    a = k.a
    c = Carver(k.region, k.region_w, b.end)
    vecs = c.take(9 * D).rearrange("p (j d) -> p j d", j=9)
    w2, a2 = c.take(D), c.take(D)
    g2 = v3(c.take(2 * D), 2, D)
    s = Carver(k.arena, SLOTS * SLOT)
    full = lambda: v3(s.take(TILES * FS), TILES, FS)
    cum, ein, eneg, ex, eh, lw, ar, kd, bd, kk, rt, bt, kt, bh, kh = (full() for _ in range(15))
    at_ = full()
    wv = s.take(TILES * 4 * HN).rearrange("p (t o n) -> p t o n", t=TILES, o=4)
    art = s.take(8 * P).rearrange("p (h t w n) -> p h t w n", h=2, t=TILES, w=2)
    btT = s.take(4 * P).rearrange("p (h t n) -> p h t n", h=2, t=TILES)
    ktT = s.take(4 * P).rearrange("p (h t n) -> p h t n", h=2, t=TILES)
    lq = s.take(TILES * 12 * P).rearrange("p (t o w n) -> p t o w n", t=TILES, o=4, w=3)
    mq = s.take(TILES * 8 * P).rearrange("p (t o w n) -> p t o w n", t=TILES, o=4, w=2)
    inv = s.take(TILES * 8 * P).rearrange("p (t o w n) -> p t o w n", t=TILES, o=4, w=2)
    xb = s.take(TILES * 4 * P).rearrange("p (t o n) -> p t o n", t=TILES, o=4)
    gu = s.take(TILES * 4 * P).rearrange("p (t o n) -> p t o n", t=TILES, o=4)
    ght = s.take(TILES * 4 * P).rearrange("p (t w h n) -> p t w h n", t=TILES, w=2, h=2)
    us = v3(s.take(4 * HN), 4, HN)
    st = v3(s.take(2 * HN), 2, HN)
    yb = full()
    pc = s.take(8)
    sm = s.take(4 * 8)
    stage = s.take(2 * len(STAGES) * P).rearrange("p (z s n) -> p z s n", z=2, s=len(STAGES))
    tri = s.take(2 * 2 * P).rearrange("p (z w n) -> p z w n", z=2, w=2)
    blk = s.take(P)
    blkcol = s.take(2)
    og = v3(k.xT[:, :, :].rearrange("p k t -> p (k t)"), TILES, D)
    rows = [a["rw_w0"][0, 0], a["rw_a0"][0, 0], a["rw_w0"][0, 1], a["rw_a0"][0, 1], a["rw_k_k"][0], a["rw_k_a"][0],
            a["rw_r_k"][0].rearrange("h n -> (h n)"), a["rw_ln_w"][0], a["rw_ln_b"][0]]
    small = [(vecs[:, j, :], r.partition_broadcast(P)) for j, r in enumerate(rows)]
    small += [(w2, a["rw_w2"][0].rearrange("z r d -> (z r) d")), (a2, a["rw_a2"][0].rearrange("z r d -> (z r) d")),
              (g2, a["rw_g2"][0].rearrange("z r d -> r z d"))]
    n_small = 16 * len(small)

    batches = [(q, z) for q in range(HEADS // 4) for z in range(2)]
    chunks = T // CH
    PREP, TILE_STEPS = 12, 4 + 4 * (len(STAGES) - 1) + 6
    FINISH = PREP + 2 + 4 * (chunks - 2) + 2
    JOINT = FINISH + 4
    turn_tile = (k.turn_tile0, k.turn_tile1)

    def joint(eng, n, done):
        eng.wait_ge(k.turn_joint.sem, k.turn_joint.at(n * JOINT + done))

    def joint_end(eng):
        eng.sem_inc(k.turn_joint.sem, 1)

    def tile_turn(eng, n, tile, done):
        eng.wait_ge(turn_tile[tile].sem, turn_tile[tile].at(n * TILE_STEPS + done))

    def tile_end(eng, tile):
        eng.sem_inc(turn_tile[tile].sem, 1)

    def by_parity(ap):
        return ap.rearrange("p (h q n) -> p q h n", h=2, q=2)

    with k.nc.Block() as block:
        @block.sync
        def _(sp):
            for dst, src in small:
                sp.dma_start(dst, src).then_inc(k.small_landed.sem, 16)

        @block.gpsimd
        def _(pool):
            link = lambda ins: k.pool_chain.link(pool, ins)

            def keep(v, pattern, base, mult):
                link(pool.affine_select(out=v, in_=v, pattern=pattern, compare_op=ALU.is_ge, fill=0.0, base=base,
                                        channel_multiplier=mult))

            link(pool.memset(blk, 1.0))
            v = blk.rearrange("p (b m) -> p b m", m=CH)
            keep(v, [[-CH, P // CH], [0, CH]], 0, 1)
            keep(v, [[CH, P // CH], [0, CH]], CH - 1, -1)
            link(pool.tensor_copy(blkcol, v[:, :, 0]))
            link(pool.memset(stage, 1.0))
            for z in range(2):
                for w in range(2):
                    link(pool.tensor_copy(tri[:, z, w], blk))
                    keep(tri[:, z, w], [[1 - 2 * z, P]], w - 1, 2 * z - 1)
                for i, m in enumerate(STAGES):
                    v = stage[:, z, i].rearrange("p (b q m) -> p b q m", q=2, m=m // 2)
                    if z == 0:
                        keep(v, [[-m, P // m], [-1000, 2], [0, m // 2]], -(m // 2), 1)
                        keep(v, [[m, P // m], [0, 2], [0, m // 2]], m - 1, -1)
                    else:
                        keep(v, [[-m, P // m], [1000, 2], [0, m // 2]], -1000, 1)
                        keep(v, [[m, P // m], [0, 2], [0, m // 2]], m // 2 - 1, -1)
            pool.sem_inc(k.pool_done.sem, 1)

        @block.tensor
        def _(pe):
            pe.wait_ge(k.small_landed.sem, k.small_landed.at(n_small))
            pe.wait_ge(k.pool_done.sem, k.pool_done.at(1))
            for n, (q, z) in enumerate(batches):
                fs = slice(q * FS, (q + 1) * FS)
                joint(pe, n, 1)
                for m, (t1, t2) in enumerate(((b.tw, w2), (b.ta, a2))):
                    for tile in range(TILES):
                        mm = pe.matmul(k.ps[:, m, tile * FS:(tile + 1) * FS],
                                       t1[z * 64:(z + 1) * 64, tile * P:(tile + 1) * P],
                                       t2[z * 64:(z + 1) * 64, fs], start=True, stop=True)
                mm.then_inc(k.turn_joint.sem, 1)
                joint(pe, n, 5)
                for tile in range(TILES):
                    pe.matmul(k.ps[:, 0, tile * FS:(tile + 1) * FS], tri[:, z, 1], lw[:, tile], start=True, stop=True)
                    pe.matmul(k.ps[:, 1, tile * FS:(tile + 1) * FS], blk, lw[:, tile], start=True, stop=True)
                    for hp in range(2):
                        at = hp * 4 + tile * 2
                        mm = pe.matmul(k.ps[:, 2, at:at + 2], lw[:, tile, hp * P:(hp + 1) * P], blkcol,
                                       start=True, stop=True)
                mm.then_inc(k.turn_joint.sem, 1)
                joint(pe, n, 10)
                for m, src in enumerate((at_, rt, bt, kt)):
                    for hp in range(2):
                        for tile in range(TILES):
                            at = (hp * TILES + tile) * P
                            mm = pe.transpose(k.ps[:, m, at:at + P], src[:, tile, hp * P:(hp + 1) * P], k.ident[:, :])
                mm.then_inc(k.turn_joint.sem, 1)
                joint(pe, n, PREP)

                for step in range(0, TILE_STEPS, 2):
                    for tile in range(TILES):
                        if step:
                            tile_turn(pe, n, tile, step)
                        pb = lambda i: k.ps[:, 4 * tile + i, :]
                        L, LT, QT = (lq[:, tile, :, w] for w in range(3))
                        MT, KT = (mq[:, tile, :, w] for w in range(2))
                        for o, (par, hp) in enumerate(ORDER):
                            j = 2 * hp + par
                            half = slice(par * 64, par * 64 + 64)
                            vj = b.v[:, tile, q * FS + j * HN:q * FS + (j + 1) * HN]
                            if step == 0:
                                for m, side in enumerate((btT, ktT)):
                                    mm = pe.matmul(pb(2 * m + par)[:, hp * 256:(hp + 1) * 256], side[half, hp, tile],
                                                   art[half, hp, tile].rearrange("p w n -> p (w n)"),
                                                   start=True, stop=True)
                            elif step == 2:
                                mm = pe.matmul(pb(par)[:, hp * P:(hp + 1) * P], art[half, hp, tile, 0],
                                               btT[half, hp, tile], start=True, stop=True)
                            elif step < TILE_STEPS - 6:
                                if step % 4 == 0:
                                    mm = pe.matmul(pb(2)[:, o * P:(o + 1) * P], LT[:, o], inv[:, tile, o, 0],
                                                   start=True, stop=True)
                                else:
                                    w = pb(o // 2)[:, (o % 2) * 256:(o % 2 + 1) * 256]
                                    pe.matmul(w[:, 0:P], inv[:, tile, o, 1], xb[:, tile, o], start=True, stop=True)
                                    mm = pe.matmul(w[:, P:2 * P], xb[:, tile, o], inv[:, tile, o, 1],
                                                   start=True, stop=True)
                            elif step == TILE_STEPS - 6:
                                mm = pe.matmul(pb(2)[:, o * HN:(o + 1) * HN], MT[:, o], vj, start=True, stop=True)
                            elif step == TILE_STEPS - 4:
                                aj = at_[:, tile, j * HN:(j + 1) * HN]
                                g = pb(0)[:, o * P:(o + 1) * P]
                                pe.matmul(g[:, 0:HN], inv[:, tile, o, 1], aj, start=True, stop=True)
                                pe.matmul(g[:, HN:P], inv[:, tile, o, 1], wv[:, tile, o], start=True, stop=True)
                                mm = pe.matmul(pb(1)[half, hp * P:(hp + 1) * P], aj,
                                               inv[:, tile, o, 1], start=True, stop=True)
                            else:
                                pe.matmul(pb(2)[half, hp * P:(hp + 1) * P], gu[:, tile, o, 0:HN], QT[:, o],
                                          start=True, stop=True)
                                pe.matmul(pb(3)[:, o * HN:(o + 1) * HN], QT[:, o], gu[:, tile, o, HN:P],
                                          start=True, stop=False)
                                mm = pe.matmul(pb(3)[:, o * HN:(o + 1) * HN], KT[:, o], vj, start=False, stop=True)
                        mm.then_inc(turn_tile[tile].sem, 1)

                at = PREP
                for tile in range(TILES):
                    tile_turn(pe, n, tile, TILE_STEPS)
                for i, ch in enumerate(range(chunks) if z == 0 else reversed(range(chunks))):
                    tile, rows_ = ch // 2, slice((ch % 2) * CH, (ch % 2 + 1) * CH)
                    if i:
                        joint(pe, n, at)
                        for o, (par, hp) in enumerate(ORDER):
                            half = slice(par * 64, par * 64 + 64)
                            mm = pe.matmul(k.ps[rows_, 4 + par, hp * HN:(hp + 1) * HN], ght[half, tile, 1, hp, rows_],
                                           st[half, hp], start=True, stop=True)
                            if i < chunks - 1:
                                mm = pe.matmul(k.ps[rows_, par, hp * HN:(hp + 1) * HN], ght[half, tile, 0, hp, rows_],
                                               st[half, hp], start=True, stop=True)
                        mm.then_inc(k.turn_joint.sem, 1)
                        at += 2
                    if i < chunks - 1:
                        joint(pe, n, at)
                        for o, (par, hp) in enumerate(ORDER):
                            j = 2 * hp + par
                            half = slice(par * 64, par * 64 + 64)
                            u = us[rows_, o] if i else gu[rows_, tile, o, HN:P]
                            out = k.ps[half, 6, hp * HN:(hp + 1) * HN]
                            pe.matmul(out, bh[rows_, tile, j * HN:(j + 1) * HN], u, start=True, stop=False)
                            mm = pe.matmul(out, kh[rows_, tile, j * HN:(j + 1) * HN],
                                           b.v[rows_, tile, q * FS + j * HN:q * FS + (j + 1) * HN],
                                           start=False, stop=True)
                        mm.then_inc(k.turn_joint.sem, 1)
                        at += 2
                assert at == FINISH
                joint(pe, n, FINISH)
                for tile in range(TILES):
                    mm = pe.matmul(k.ps[:, 7, tile * FS:(tile + 1) * FS], b.tg[:, z, tile * P:(tile + 1) * P],
                                   g2[:, z, fs], start=True, stop=True)
                mm.then_inc(k.turn_joint.sem, 1)

        @block.scalar
        def _(act):
            mark = k.act_chain.mark
            ps3 = lambda i: v3(k.ps[:, i, :], TILES, FS)

            def done():
                act.wait_ge(k.act_chain.sem, k.act_chain.n)
                joint_end(act)

            for n, (q, z) in enumerate(batches):
                if z == 0:
                    act.wait_ge(k.vec_done.sem, k.vec_done.at(q + 1))
                    act.activation(sm[:, 0:8], sm[:, 0:8], ACT.Sqrt).then_inc(k.act_done.sem, 1)
                joint(act, n, 3)
                mark(act.activation(lw, lw, ACT.Sigmoid))
                mark(act.activation(ar, ar, ACT.Sigmoid))
                done()
                joint(act, n, 6)
                mark(act.activation(cum, ps3(0), ACT.Copy))
                mark(act.activation(ein, ps3(0), ACT.Exp))
                mark(act.activation(eneg, ps3(0), ACT.Exp, scale=-1.0))
                mark(act.activation(pc, k.ps[:, 2, 0:8], ACT.Exp))
                done()
                joint(act, n, 8)
                mark(act.activation(ex, ex, ACT.Exp))
                mark(act.activation(eh, eh, ACT.Exp))
                done()
                joint(act, n, FINISH + 2)
                mark(act.activation(sm[:, 16:24], sm[:, 16:24], ACT.Sqrt))
                done()

        @block.vector
        def _(vec):
            link = lambda ins: k.vec_chain.link(vec, ins)
            mark = k.vec_chain.mark

            def settle():
                vec.wait_ge(k.vec_chain.sem, k.vec_chain.n)

            def done():
                settle()
                joint_end(vec)

            def bc_tiles(j, fs):
                return vecs[:, j:j + 1, fs].to_broadcast([P, TILES, FS])

            def per_head(ap):
                return ap.rearrange("p t (h n) -> p (t h) n", n=HN)

            def bc_head(cols):
                return cols.rearrange("p (h a) -> p h a", a=1).to_broadcast([P, 8, HN])

            ps3 = lambda i: v3(k.ps[:, i, :], TILES, FS)
            vec.wait_ge(k.small_landed.sem, k.small_landed.at(n_small))
            vec.wait_ge(k.pool_done.sem, k.pool_done.at(1))
            for n, (q, z) in enumerate(batches):
                fs = slice(q * FS, (q + 1) * FS)
                r_, k_, v_ = (t[:, :, fs] for t in (b.r, b.k, b.v))
                if z == 0:
                    link(vec.tensor_tensor(kk, k_, bc_tiles(4, fs), MUL))
                    link(vec.tensor_tensor(ex, kk, kk, MUL))
                    link(vec.tensor_reduce(sm[:, 0:8], per_head(ex), X, ADD))
                    vec.sem_inc(k.vec_done.sem, 1)
                    vec.wait_ge(k.act_done.sem, k.act_done.at(q + 1))
                    link(vec.tensor_scalar(sm[:, 0:8], sm[:, 0:8], 1e-12, None, MAX))
                    link(vec.reciprocal(sm[:, 0:8], sm[:, 0:8]))
                    link(vec.tensor_tensor(per_head(kk), per_head(kk), bc_head(sm[:, 0:8]), MUL))
                joint_end(vec)
                joint(vec, n, 2)
                mark(vec.tensor_tensor(lw, ps3(0), bc_tiles(2 * z, fs), ADD))
                mark(vec.tensor_tensor(ar, ps3(1), bc_tiles(2 * z + 1, fs), ADD))
                done()
                joint(vec, n, 4)
                mark(vec.tensor_scalar(lw, lw, -math.exp(-0.5), None, MUL))
                mark(vec.tensor_tensor(bd, kk, ar, MUL))
                link(vec.scalar_tensor_tensor(out=kd, in0=ar, scalar=-1.0, in1=bc_tiles(5, fs), op0=ADD, op1=MUL))
                link(vec.scalar_tensor_tensor(out=kd, in0=kd, scalar=1.0, in1=k_, op0=ADD, op1=MUL))
                link(vec.tensor_tensor(ex, r_, kd, MUL))
                link(vec.tensor_tensor(ex, ex, bc_tiles(6, fs), MUL))
                mark(vec.tensor_reduce(sm[:, 8:16], per_head(ex), X, ADD))
                done()
                joint(vec, n, 7)
                mark(vec.tensor_tensor(ex, cum, lw, SUB))
                mark(vec.tensor_tensor(eh, ps3(1), cum, SUB))
                done()
                joint(vec, n, 9)
                mark(vec.scalar_tensor_tensor(out=at_, in0=kk, scalar=-1.0, in1=ex, op0=MUL, op1=MUL))
                mark(vec.tensor_tensor(rt, r_, ein, MUL))
                mark(vec.tensor_tensor(bt, bd, eneg, MUL))
                mark(vec.tensor_tensor(kt, kd, eneg, MUL))
                mark(vec.tensor_tensor(bh, bd, eh, MUL))
                mark(vec.tensor_tensor(kh, kd, eh, MUL))
                done()
                joint(vec, n, 11)
                for m, dst in enumerate((art[:, :, :, 0], art[:, :, :, 1], btT, ktT)):
                    mark(vec.tensor_copy(dst, k.ps[:, m, :].rearrange("p (h t n) -> p h t n", h=2, t=TILES)))
                done()

                for step in range(1, TILE_STEPS, 2):
                    for tile in range(TILES):
                        tile_turn(vec, n, tile, step)
                        b0 = 4 * tile
                        inv_t = inv[:, tile].rearrange("p o w n -> p (o w n)")
                        if step == 1:
                            for m, dst in enumerate((lq[:, tile, :, 1:3], mq[:, tile])):
                                mark(vec.tensor_tensor(
                                    dst.rearrange("p o w n -> p o (w n)"), v3(bank(k, b0 + 2 * m, 2), 4, 2 * P),
                                    tri[:, z].rearrange("p w n -> p (w n)").rearrange("p (a m) -> p a m", a=1)
                                    .to_broadcast([P, 4, 2 * P]), MUL))
                            settle()
                        elif step == 3:
                            for par in range(2):
                                mark(vec.tensor_tensor(lq[:, tile, 2 * par:2 * par + 2, 0], v3(k.ps[:, b0 + par, 0:256], 2, P),
                                                       tri[:, 1 - z, 0:1].to_broadcast([P, 2, P]), MUL))
                            settle()
                            for w in range(2):
                                m = (z, 1 - z)[w]
                                mark(vec.tensor_tensor(inv[:, tile, :, w], lq[:, tile, :, w],
                                                       stage[:, m, 0:1].to_broadcast([P, 4, P]), MUL))
                            settle()
                            flat = inv[:, tile].rearrange("p o w n -> p (o w) n")
                            link(vec.tensor_tensor(flat, flat, v3(k.ident[:, :], 1, P).to_broadcast([P, 8, P]), ADD))
                        elif step < TILE_STEPS - 6:
                            if step % 4 == 1:
                                i = (step - 1) // 4
                                link(vec.tensor_tensor(xb[:, tile], v3(k.ps[:, b0 + 2, :], 4, P),
                                                       stage[:, z, i:i + 1].to_broadcast([P, 4, P]), MUL))
                            else:
                                link(vec.tensor_tensor(inv_t, inv_t, bank(k, b0, 2), ADD))
                        elif step == TILE_STEPS - 5:
                            link(vec.tensor_copy(wv[:, tile], v3(k.ps[:, b0 + 2, 0:4 * HN], 4, HN)))
                        elif step == TILE_STEPS - 3:
                            mark(vec.tensor_copy(gu[:, tile].rearrange("p o n -> p (o n)"), k.ps[:, b0, :]))
                            mark(vec.tensor_copy(ght[:, tile, 0].rearrange("p h n -> p (h n)"), k.ps[:, b0 + 1, 0:256]))
                            settle()
                        else:
                            mark(vec.tensor_tensor(ght[:, tile, 1], v3(k.ps[:, b0 + 2, 0:256], 2, P), art[:, :, tile, 1], ADD))
                            mark(vec.tensor_copy(by_parity(yb[:, tile]),
                                                 k.ps[:, b0 + 3, 0:256].rearrange("p (q h n) -> p q h n", q=2, h=2)))
                            settle()
                        tile_end(vec, tile)

                at = PREP
                for i, ch in enumerate(range(chunks) if z == 0 else reversed(range(chunks))):
                    tile, rows_ = ch // 2, slice((ch % 2) * CH, (ch % 2 + 1) * CH)
                    if i:
                        joint(vec, n, at + 1)
                        y_ = by_parity(yb[rows_, tile])
                        mark(vec.tensor_tensor(y_, k.ps[rows_, 4:6, 0:P].rearrange("p q (h n) -> p q h n", h=2), y_, ADD))
                        if i < chunks - 1:
                            mark(vec.tensor_tensor(us[rows_].rearrange("p (q h) n -> p q h n", q=2),
                                                   k.ps[rows_, 0:2, 0:P].rearrange("p q (h n) -> p q h n", h=2),
                                                   gu[rows_, tile, :, HN:P].rearrange("p (q h) n -> p q h n", q=2), ADD))
                        done()
                        at += 2
                    if i < chunks - 1:
                        joint(vec, n, at + 1)
                        for hp in range(2):
                            new = k.ps[:, 6, hp * HN:(hp + 1) * HN]
                            if i == 0:
                                mark(vec.tensor_copy(st[:, hp], new))
                            else:
                                col = hp * 4 + ch
                                mark(vec.scalar_tensor_tensor(out=st[:, hp], in0=st[:, hp], scalar=pc[:, col:col + 1],
                                                              in1=new, op0=MUL, op1=ADD))
                        done()
                        at += 2
                joint(vec, n, FINISH + 1)
                yh, eh_ = per_head(yb), per_head(ex)
                link(vec.tensor_reduce(sm[:, 24:32], yh, X, ADD))
                link(vec.tensor_scalar(sm[:, 24:32], sm[:, 24:32], 1.0 / HN, None, MUL))
                link(vec.tensor_tensor(yh, yh, bc_head(sm[:, 24:32]), SUB))
                link(vec.tensor_tensor(eh_, yh, yh, MUL))
                link(vec.tensor_reduce(sm[:, 16:24], eh_, X, ADD))
                link(vec.tensor_scalar(sm[:, 16:24], sm[:, 16:24], 1.0 / HN, GN_EPS, MUL, ADD))
                joint_end(vec)
                joint(vec, n, FINISH + 3)
                link(vec.reciprocal(sm[:, 16:24], sm[:, 16:24]))
                link(vec.tensor_tensor(yh, yh, bc_head(sm[:, 16:24]), MUL))
                link(vec.tensor_tensor(yb, yb, bc_tiles(7, fs), MUL))
                link(vec.tensor_tensor(yb, yb, bc_tiles(8, fs), ADD))
                link(vec.tensor_tensor(ex.rearrange("p t (h n) -> p t h n", n=HN),
                                       v_.rearrange("p t (h n) -> p t h n", n=HN),
                                       sm[:, 8:16].rearrange("p (t h a) -> p t h a", t=TILES, a=1)
                                       .to_broadcast([P, TILES, 4, HN]), MUL))
                link(vec.tensor_tensor(yb, yb, ex, ADD))
                if z == 0:
                    link(vec.tensor_tensor(og[:, :, fs], ps3(7), yb, MUL))
                else:
                    link(vec.tensor_tensor(yb, ps3(7), yb, MUL))
                    link(vec.tensor_tensor(og[:, :, fs], og[:, :, fs], yb, ADD))
                joint_end(vec)
    k.small_landed.close(n_small)
    k.pool_done.close(1)
    k.vec_done.close(HEADS // 4)
    k.act_done.close(HEADS // 4)
    k.turn_joint.close(len(batches) * JOINT)
    for sig in turn_tile:
        sig.close(len(batches) * TILE_STEPS)
    return og


def route_phase(k, i, end):
    a = k.a
    first = i < DEPTH
    NR = N_GROUPS + EXPERTS
    c = Carver(k.region, k.region_w)
    k.key, k.gate = (c.take(TILES * EXPERTS).rearrange("p (q t w) -> p q t w", q=PAIRS, t=TILES) for _ in range(2))
    k.over = v3(c.take(TILES * EXPERTS), EXPERTS, TILES)
    k.count = c.take(1).bitcast(I32)
    k.slot_ids = c.take(CAP)
    k.xm = c.take(TILES * D).rearrange("p (t s m) -> p t s m", t=TILES, s=K8)
    k.moe_end = c.at
    before, ones = c.take(P), c.take(P)
    chosen, rank = (v3(c.take(TILES * EXPERTS), TILES, EXPERTS) for _ in range(2))
    peak = c.take(1)
    ids = c.take(CAP).bitcast(I32)
    rw = v3(c.take(K8 * NR), K8, NR)
    rb = c.take(NR)
    lg = v3(c.take(TILES * NR), TILES, NR)
    gates = c.take(TILES * EXPERTS).rearrange("p (t g e) -> p t g e", t=TILES, g=N_GROUPS)
    tmp4 = c.take(TILES * EXPERTS).rearrange("p (t g e) -> p t g e", t=TILES, g=N_GROUPS)
    ohg, eg, s4 = (v3(c.take(TILES * N_GROUPS), TILES, N_GROUPS) for _ in range(3))
    sel, oh1, oh2, s8, e2 = (v3(c.take(TILES * PER_GROUP), TILES, PER_GROUP) for _ in range(5))
    cols = v3(c.take(8 * TILES), 8, TILES)
    m0, mm, pg, m1, m2, ex, w1, w2 = (cols[:, j, :] for j in range(8))
    small = []
    if first:
        small.append((rw[:, :, 0:N_GROUPS], a["moe_router_g"][i].rearrange("(p k) g -> p k g", k=K8)))
        small.append((rb[:, 0:N_GROUPS], a["moe_router_g_b"][i].partition_broadcast(P)))
        for g in range(N_GROUPS):
            at = N_GROUPS + g * PER_GROUP
            small.append((rw[:, :, at:at + PER_GROUP], a["moe_router_e"][i, g].rearrange("(p k) e -> p k e", k=K8)))
            small.append((rb[:, at:at + PER_GROUP], a["moe_router_e_b"][i, g].partition_broadcast(P)))
    else:
        j = i - DEPTH
        small.append((rw[:, :, 0:N_GROUPS], a["w_route_group_2"][j].rearrange("(p k) g -> p k g", k=K8)))
        small.append((rb[:, 0:N_GROUPS], a["b_route_group_2"][j].partition_broadcast(P)))
        small.append((rw[:, :, N_GROUPS:NR], a["w_route_expert_2"][j].rearrange("(p k) e -> p k e", k=K8)))
        small.append((rb[:, N_GROUPS:NR], a["b_route_expert_2"][j].partition_broadcast(P)))
    n_small = 16 * len(small)

    def last(col, n):
        return col.rearrange("p (t a) -> p t a", a=1).to_broadcast([P, TILES, n])

    with k.nc.Block() as block:
        @block.sync
        def _(sp):
            for dst, src in small:
                sp.dma_start(dst, src).then_inc(k.small_landed.sem, 16)
            ahead(k, sp, end)

        @block.tensor
        def _(pe):
            pe.wait_ge(k.small_landed.sem, k.small_landed.at(n_small))
            for tile in range(TILES):
                for s in range(K8):
                    mm_ = pe.matmul(k.ps[:, tile, 0:NR], k.xT[:, s, tile * P:(tile + 1) * P], rw[:, s],
                                    start=(s == 0), stop=(s == K8 - 1))
            mm_.then_inc(k.pe_done.sem, 1)
            if first:
                for tile in range(TILES):
                    for s in range(K8):
                        mm_ = pe.transpose(k.ps[:, 4 + 2 * tile + s // 4, (s % 4) * P:(s % 4 + 1) * P],
                                           k.xT[:, s, tile * P:(tile + 1) * P], k.ident[:, :])
                mm_.then_inc(k.pe_done.sem, 1)
            pe.wait_ge(k.vec_done.sem, k.vec_done.at(3))
            pe.wait_ge(k.pool_done.sem, k.pool_done.at(1))
            for n, terms in enumerate((((before, 0),), ((ones, 0), (before, 1)), ((ones, 0), (ones, 1)))):
                for m, (w, tile) in enumerate(terms):
                    mm_ = pe.matmul(k.ps[:, 3, n * EXPERTS:(n + 1) * EXPERTS], w, chosen[:, tile], start=(m == 0),
                                    stop=(m == len(terms) - 1))
            mm_.then_inc(k.pe_done.sem, 1)

        @block.scalar
        def _(act):
            act.wait_ge(k.vec_done.sem, k.vec_done.at(1))
            act.activation(eg, eg, ACT.Exp).then_inc(k.act_done.sem, 1)
            act.wait_ge(k.vec_done.sem, k.vec_done.at(2))
            act.activation(ex, ex, ACT.Exp).then_inc(k.act_done.sem, 1)
            if first:
                act.wait_ge(k.pe_done.sem, k.pe_done.at(2))
                act.activation(k.xm.rearrange("p t s m -> p (t s m)"), bank(k, 4, 4), ACT.Copy).then_inc(k.act_done.sem, 1)

        @block.gpsimd
        def _(pool):
            link = lambda ins: k.pool_chain.link(pool, ins)
            link(pool.memset(ones, 1.0))
            link(pool.memset(before, 1.0))
            link(pool.affine_select(out=before, in_=before, pattern=[[1, P]], compare_op=ALU.is_ge, fill=0.0, base=-1,
                                    channel_multiplier=-1))
            link(pool.iota(ids, pattern=[[1, CAP]], base=0, channel_multiplier=0))
            pool.sem_inc(k.pool_done.sem, 1)

        @block.vector
        def _(vec):
            link = lambda ins: k.vec_chain.link(vec, ins)

            def first_best(values, best, onehot, scratch, n):
                link(vec.tensor_reduce(best, values, X, MAX))
                link(vec.tensor_tensor(scratch, values, last(best, n), ALU.is_equal))
                link(vec.tensor_tensor(scratch, scratch, v3(k.desc[:, 0:n], 1, n).to_broadcast([P, TILES, n]), MUL))
                link(vec.tensor_reduce(mm, scratch, X, MAX))
                link(vec.tensor_tensor(onehot, scratch, last(mm, n), ALU.is_equal))

            vec.wait_ge(k.pe_done.sem, k.pe_done.at(1))
            vec.wait_ge(k.small_landed.sem, k.small_landed.at(n_small))
            link(vec.tensor_tensor(lg, k.ps[:, 0:TILES, 0:NR], v3(rb, 1, NR).to_broadcast([P, TILES, NR]), ADD))
            lgg = lg[:, :, 0:N_GROUPS]
            first_best(lgg, m0, ohg, s4, N_GROUPS)
            link(vec.tensor_tensor(eg, lgg, last(m0, N_GROUPS), SUB))
            vec.sem_inc(k.vec_done.sem, 1)
            link(vec.tensor_tensor(tmp4, lg[:, :, N_GROUPS:NR].rearrange("p t (g e) -> p t g e", g=N_GROUPS),
                                   ohg.rearrange("p t (g a) -> p t g a", a=1).to_broadcast([P, TILES, N_GROUPS, PER_GROUP]), MUL))
            link(vec.tensor_reduce(sel, tmp4.rearrange("p t g e -> p t e g"), X, ADD))
            first_best(sel, m1, oh1, s8, PER_GROUP)
            link(vec.scalar_tensor_tensor(out=e2, in0=oh1, scalar=-BIG, in1=sel, op0=MUL, op1=ADD))
            first_best(e2, m2, oh2, s8, PER_GROUP)
            link(vec.tensor_tensor(ex, m2, m1, SUB))
            vec.sem_inc(k.vec_done.sem, 1)
            vec.wait_ge(k.act_done.sem, k.act_done.at(1))
            link(vec.tensor_reduce(pg, eg, X, ADD))
            link(vec.reciprocal(pg, pg))
            vec.wait_ge(k.act_done.sem, k.act_done.at(2))
            link(vec.tensor_scalar(w1, ex, 1.0, None, ADD))
            link(vec.reciprocal(w1, w1))
            link(vec.tensor_tensor(w1, w1, pg, MUL))
            link(vec.tensor_tensor(w2, w1, ex, MUL))
            group = ohg.rearrange("p t (g a) -> p t g a", a=1)
            link(vec.tensor_tensor(s8, oh1, oh2, ADD))
            for tile in range(TILES):
                link(vec.tensor_tensor(v3(chosen[:, tile], N_GROUPS, PER_GROUP), group[:, tile].to_broadcast([P, N_GROUPS, PER_GROUP]),
                                       s8[:, tile:tile + 1].to_broadcast([P, N_GROUPS, PER_GROUP]), MUL))
            vec.sem_inc(k.vec_done.sem, 1)
            link(vec.tensor_tensor(oh1, oh1, last(w1, PER_GROUP), MUL))
            link(vec.tensor_tensor(oh2, oh2, last(w2, PER_GROUP), MUL))
            link(vec.tensor_tensor(oh1, oh1, oh2, ADD))
            for tile in range(TILES):
                link(vec.tensor_tensor(gates[:, tile], group[:, tile].to_broadcast([P, N_GROUPS, PER_GROUP]),
                                       oh1[:, tile:tile + 1].to_broadcast([P, N_GROUPS, PER_GROUP]), MUL))
            flat = gates.rearrange("p t g e -> p t (g e)")
            paired = lambda ap: ap.rearrange("p t (q w) -> p q t w", w=2)
            link(vec.tensor_copy(k.gate, paired(flat)))
            vec.wait_ge(k.pool_done.sem, k.pool_done.at(1))
            link(vec.tensor_copy(k.slot_ids, ids))
            n = 3 if first else 2
            vec.wait_ge(k.pe_done.sem, k.pe_done.at(n))
            link(vec.tensor_copy(rank, v3(k.ps[:, 3, 0:TILES * EXPERTS], TILES, EXPERTS)))
            link(vec.tensor_reduce(peak, k.ps[:, 3, TILES * EXPERTS:(TILES + 1) * EXPERTS], X, MAX))
            link(vec.tensor_copy(k.count, peak))
            link(vec.scalar_tensor_tensor(out=k.over.rearrange("p e t -> p t e"), in0=rank, scalar=float(CAP), in1=flat,
                                          op0=ALU.is_ge, op1=MUL))
            link(vec.tensor_scalar(chosen, chosen, -FAR, FAR, MUL, ADD))
            link(vec.tensor_tensor(k.key, paired(rank), paired(chosen), ADD))
    k.small_landed.close(n_small)
    k.pe_done.close(3 if first else 2)
    k.vec_done.close(3)
    k.act_done.close(3 if first else 2)
    k.pool_done.close(1)


def experts_phase(k, i):
    a = k.a
    j = i % DEPTH
    wg, wu, wd = ((a["moe_w_gate"], a["moe_w_up"], a["moe_w_down"]) if i < DEPTH else
                  (a["w_exp_gate_2"], a["w_exp_up_2"], a["w_exp_down_2"]))
    wg = wg[j].rearrange("g e (p k) f -> (g e) p (k f)", k=K8)
    wu = wu[j].rearrange("g e (p k) f -> (g e) p (k f)", k=K8)
    wd = wd[j].rearrange("g e (p r) n -> (g e) p (r n)", r=2)
    n0 = k.starts[f"moe{i}"]
    passes = (PAIRS - UNROLL) // UNROLL
    c = Carver(k.region, k.region_w, k.moe_end)
    zeros = c.take(HALF)
    slots, gated = (c.take(TILES * P).rearrange("p (t w n) -> p t w n", t=TILES, w=2) for _ in range(2))
    gatedT = v3(c.take(2 * T), 2, T)
    xe = v3(c.take(K8 * P), K8, P)
    silu_out, hid = c.take(F), c.take(F)
    hidT = v3(c.take(2 * P), 2, P)
    out = c.take(D)
    over_w = v3(c.take(3 * SLOT), 3, SLOT)
    over_silu, over_hid, over_hidT = (v3(c.take(TILES * F), TILES, F) for _ in range(3))
    landed_, turn_ = k.over_landed[i], k.over_turn[i]
    OVER_STEPS = 7
    gate_at = lambda q: 6 * q - 2 if q else 0
    down_at = lambda q: min(6 * q + 8, 3 * EXPERTS - 2)
    assert k.issued >= n0 + SLOTS, "the first units are loaded ahead"

    def slot(n, width=1):
        at = ((n0 + n) % SLOTS) * SLOT
        return k.arena[:, at:at + width * SLOT]

    def wait_slot(eng, n, p):
        eng.wait_ge(k.landed[(n0 + n) % SLOTS], 16 * ((n0 + n) // SLOTS + 1) + 16 * p)

    def wait_pair(eng, sig, q, p):
        eng.wait_ge(sig.sem, sig.at(q + 1) + UNROLL * p)

    def column(v, q, p):
        one = v[:, q] if isinstance(p, int) else v[:, bass.ds(p * UNROLL + q, 1)].rearrange("p a t w -> p (a t) w")
        return one.rearrange("p t (w n) -> p t w n", n=1).to_broadcast([P, TILES, 2, CAP])

    def overflow(eng, body):
        count = eng.value_load(k.count[0:1, 0:1], min_val=0, max_val=T)
        with eng.If(count > CAP):
            with eng.Fori(0, EXPERTS) as e:
                body(e)

    with k.nc.Block() as block:
        @block.sync
        def _(sp):
            def general(e):
                sp.wait_ge(turn_, OVER_STEPS * e + 1)
                for m, w in enumerate((wg, wu, wd)):
                    sp.dma_start(over_w[:, m], w[bass.ds(e, 1)].rearrange("a p n -> p (a n)")).then_inc(landed_, 16)

            def load(n, p, src):
                sp.wait_ge(k.used, n0 + n + 1 - SLOTS + SLOTS * p)
                sp.dma_start(slot(n), src).then_inc(k.landed[(n0 + n) % SLOTS], 16)

            overflow(sp, general)
            issue(k, sp, n0 + 4 + SLOTS)
            with sp.Fori(1, passes) as p:
                for s in range(UNROLL):
                    one = lambda w, e: w[bass.ds(p * 2 * UNROLL + e, 1)].rearrange("a p n -> p (a n)")
                    for e in range(2):
                        load(gate_at(s + 1) + 2 * e, p, one(wg, 2 * s + 2 + e))
                        load(gate_at(s + 1) + 2 * e + 1, p, one(wu, 2 * s + 2 + e))
                    for e in range(2):
                        load(down_at(s) + e, p, one(wd, 2 * s + e))
            k.issued = n0 + 4 + SLOTS * passes
            ahead(k, sp, n0 + 3 * EXPERTS)

        @block.tensor
        def _(pe):
            def general(e):
                pe.wait_ge(landed_, 48 * e + 48)
                pe.wait_ge(turn_, OVER_STEPS * e + 1)
                for m in range(2):
                    w = v3(over_w[:, m], K8, F)
                    for tile in range(TILES):
                        for s in range(K8):
                            mm = pe.matmul(k.ps[:, 4 + m, tile * F:(tile + 1) * F], k.xT[:, s, tile * P:(tile + 1) * P],
                                           w[:, s], start=(s == 0), stop=(s == K8 - 1))
                mm.then_inc(turn_, 1)
                pe.wait_ge(turn_, OVER_STEPS * e + 5)
                for tile in range(TILES):
                    for r in range(2):
                        mm = pe.transpose(k.ps[:, 6, r * T + tile * P:r * T + (tile + 1) * P], over_hid[:, tile, r:F:2],
                                          k.ident[:, :])
                mm.then_inc(turn_, 1)
                pe.wait_ge(turn_, OVER_STEPS * e + 7)
                w = v3(over_w[:, 2], 2, D)
                for r in range(2):
                    for tile in range(TILES):
                        for h in range(2):
                            mm = pe.matmul(k.ps[:, 2 * tile + h, :], over_hidT[:, r, tile * P:(tile + 1) * P],
                                           w[:, r, h * HALF:(h + 1) * HALF], start=False, stop=True, skip_group_check=True)
                mm.then_inc(turn_, 1)

            def gather(q, p):
                wait_pair(pe, k.slots_built, q, p)
                for s in range(K8):
                    for tile in range(TILES):
                        tokens = k.xm[:, tile, s] if i < DEPTH else k.x[:, tile, s:D:K8]
                        mm = pe.matmul(k.ps[:, 4 + s // 4, (s % 4) * P:(s % 4 + 1) * P], tokens,
                                       slots[:, tile].rearrange("p w n -> p (w n)"), start=(tile == 0), stop=(tile == 1))
                mm.then_inc(k.gathered.sem, 1)

            def turn(q, p, hidden, slots_):
                if hidden:
                    wait_pair(pe, k.hidden_ready, q, p)
                    for r in range(2):
                        mm = pe.transpose(k.ps[:, 7, r * P:(r + 1) * P], hid[:, r:F:2], k.ident[:, :])
                if slots_:
                    wait_pair(pe, k.gated_built, q + 1, p)
                    if q >= 0:
                        wait_pair(pe, k.gated_moved, q, p)
                    for tile in range(TILES):
                        mm = pe.transpose(k.ps[:, 7, T + tile * P:T + (tile + 1) * P],
                                          gated[:, tile].rearrange("p w n -> p (w n)"), k.ident[:, :])
                mm.then_inc(k.turned.sem, 1)

            def first_layer(q, p):
                wait_pair(pe, k.tokens_half0, q, p)
                wait_pair(pe, k.tokens_half1, q, p)
                for m in range(4):
                    wait_slot(pe, gate_at(q) + m, p)
                for s in range(K8):
                    for e in range(2):
                        w = v3(slot(gate_at(q) + 2 * e, 2), 2, SLOT)[:, :, s * F:(s + 1) * F]
                        mm = pe.matmul(v3(k.ps[e * CAP:(e + 1) * CAP, 6, :], 2, F), xe[:, s, e * CAP:(e + 1) * CAP], w,
                                       start=(s == 0), stop=(s == K8 - 1), skip_group_check=True)
                        if s == K8 - 1:
                            mm.then_inc(k.used, 2)

            def second_layer(q, p):
                wait_pair(pe, k.hidden_moved, q, p)
                for m in range(2):
                    wait_slot(pe, down_at(q) + m, p)
                for h in range(2):
                    for r in range(2):
                        for e in range(2):
                            w = v3(slot(down_at(q) + e), 2, D)
                            mm = pe.matmul(k.ps[e * CAP:(e + 1) * CAP, 4 + h, :], hidT[:, r, e * CAP:(e + 1) * CAP],
                                           w[:, r, h * HALF:(h + 1) * HALF], start=(r == 0), stop=(r == 1),
                                           skip_group_check=True)
                            if h and r:
                                mm.then_inc(k.used, 1)
                    if h == 0:
                        mm.then_inc(k.out_half.sem, 1)

            def scatter(q, p):
                for h, moved in enumerate((k.out_moved0, k.out_moved1)):
                    wait_pair(pe, moved, q, p)
                    for tile in range(TILES):
                        pe.matmul(k.ps[:, 2 * tile + h, :], gatedT[:, q % 2, tile * P:(tile + 1) * P],
                                  out[:, h * HALF:(h + 1) * HALF], start=False, stop=True, skip_group_check=True)

            pe.wait_ge(k.pool_done.sem, k.pool_done.at(1))
            for b in range(4):
                pe.matmul(k.ps[:, b, :], zeros[:, 0:P], zeros, start=True, stop=True)
            overflow(pe, general)
            gather(0, 0)
            turn(-1, 0, False, True)
            first_layer(0, 0)

            def pair(q, p, more):
                if more:
                    gather(q + 1, p)
                turn(q, p, True, more)
                if more:
                    first_layer(q + 1, p)
                second_layer(q, p)
                scatter(q, p)

            with pe.Fori(0, passes) as p:
                for s in range(UNROLL):
                    pair(s, p, True)
            for q in range(PAIRS - UNROLL, PAIRS):
                pair(q, 0, q + 1 < PAIRS)
            pe.transpose(k.ps[:, 7, 0:P], k.ident[:, :], k.ident[:, :]).then_inc(k.pe_done.sem, 1)

        @block.scalar
        def _(act):
            def general(e):
                act.wait_ge(turn_, OVER_STEPS * e + 2)
                act.activation(over_silu, v3(k.ps[:, 4, :], TILES, F), ACT.Silu).then_inc(turn_, 1)

            def move_tokens(q, p):
                wait_pair(act, k.gathered, q, p)
                act.activation(xe[:, 0:4].rearrange("p s n -> p (s n)"), k.ps[:, 4, :], ACT.Copy).then_inc(k.tokens_half0.sem, 1)

            def pair(q, p, more):
                act.wait_ge(k.used, n0 + gate_at(q) + 4 + SLOTS * p)
                act.activation(silu_out, k.ps[:, 6, 0:F], ACT.Silu).then_inc(k.silu_ready.sem, 1)
                if more:
                    move_tokens(q + 1, p)
                wait_pair(act, k.out_half, q, p)
                act.activation(out[:, 0:HALF], k.ps[:, 4, :], ACT.Copy).then_inc(k.out_moved0.sem, 1)

            overflow(act, general)
            move_tokens(0, 0)
            with act.Fori(0, passes) as p:
                for s in range(UNROLL):
                    pair(s, p, True)
            for q in range(PAIRS - UNROLL, PAIRS):
                pair(q, 0, q + 1 < PAIRS)

        @block.vector
        def _(vec):
            def general(e):
                vec.wait_ge(turn_, OVER_STEPS * e + 3)
                vec.tensor_tensor(over_hid, v3(k.ps[:, 5, :], TILES, F), over_silu, MUL).then_inc(turn_, 1)
                vec.wait_ge(turn_, OVER_STEPS * e + 4)
                gate = k.over[:, bass.ds(e, 1)].rearrange("p a (t n) -> p (a t) n", n=1)
                vec.tensor_tensor(over_hid, over_hid, gate.to_broadcast([P, TILES, F]), MUL).then_inc(turn_, 1)
                vec.wait_ge(turn_, OVER_STEPS * e + 6)
                vec.tensor_copy(over_hidT, v3(k.ps[:, 6, :], 2, T)).then_inc(turn_, 1)

            def build(q, p):
                ids = k.slot_ids.rearrange("p (a b n) -> p a b n", a=1, b=1).to_broadcast([P, TILES, 2, CAP])
                vec.tensor_tensor(slots, ids, column(k.key, q, p), ALU.is_equal).then_inc(k.slots_built.sem, 1)
                wait_pair(vec, k.slots_built, q, p)
                vec.tensor_tensor(gated, slots, column(k.gate, q, p), MUL).then_inc(k.gated_built.sem, 1)

            def move_tokens(q, p):
                wait_pair(vec, k.gathered, q, p)
                vec.tensor_copy(xe[:, 4:8].rearrange("p s n -> p (s n)"), k.ps[:, 5, :]).then_inc(k.tokens_half1.sem, 1)

            def move_gated(q, p):
                wait_pair(vec, k.turned, q, p)
                vec.tensor_copy(gatedT[:, q % 2], k.ps[:, 7, T:2 * T]).then_inc(k.gated_moved.sem, 1)

            def pair(q, p, left):
                wait_pair(vec, k.silu_ready, q, p)
                vec.tensor_tensor(hid, k.ps[:, 6, F:2 * F], silu_out, MUL).then_inc(k.hidden_ready.sem, 1)
                if left > 1:
                    move_tokens(q + 1, p)
                wait_pair(vec, k.turned, q + 1, p)
                vec.tensor_copy(hidT.rearrange("p r n -> p (r n)"), k.ps[:, 7, 0:T]).then_inc(k.hidden_moved.sem, 1)
                if left > 1:
                    move_gated(q + 1, p)
                if left > 2:
                    build(q + 2, p)
                vec.wait_ge(k.used, n0 + down_at(q) + 2 + SLOTS * p)
                vec.tensor_copy(out[:, HALF:D], k.ps[:, 5, :]).then_inc(k.out_moved1.sem, 1)

            vec.sem_inc(turn_, 1)
            overflow(vec, general)
            build(0, 0)
            move_tokens(0, 0)
            move_gated(0, 0)
            build(1, 0)
            with vec.Fori(0, passes) as p:
                for s in range(UNROLL):
                    pair(s, p, 3)
            for q in range(PAIRS - UNROLL, PAIRS):
                pair(q, 0, PAIRS - q)
            vec.wait_ge(k.pe_done.sem, k.pe_done.at(1))

        @block.gpsimd
        def _(pool):
            k.pool_chain.link(pool, pool.memset(zeros, 0.0))
            pool.sem_inc(k.pool_done.sem, 1)
    for sig in (k.slots_built, k.gated_built, k.gathered, k.tokens_half0, k.tokens_half1, k.hidden_moved, k.gated_moved,
                k.silu_ready, k.hidden_ready, k.out_half, k.out_moved0, k.out_moved1):
        sig.close(PAIRS)
    k.turned.close(PAIRS + 1)
    k.pe_done.close(1)
    k.pool_done.close(1)


def moe_residual_phase(k, i):
    with k.nc.Block() as block:
        @block.vector
        def _(vec):
            link = lambda ins: k.vec_chain.link(vec, ins)
            add_gated(k, vec, link, 1, k.region[:, 0:TILES * D])


def qkv_phase(k, b):
    n0 = k.starts["qkv"]
    c = Carver(k.region, k.region_w)
    b.q, b.k = (c.take(len(GROUPS) * AH * T).rearrange("p (g h t) -> p g h t", g=len(GROUPS), h=AH) for _ in range(2))
    b.v = c.take(len(GROUPS) * TILES * D).rearrange("p (g t d) -> p g t d", g=len(GROUPS), t=TILES)
    b.o = v3(c.take(TILES * D), TILES, D)
    jobs = [(g, j) for g in range(len(GROUPS)) for j in range(3)]
    with k.nc.Block() as block:
        @block.sync
        def _(sp):
            ahead(k, sp, n0 + 4 * len(jobs))

        @block.tensor
        def _(pe):
            for n, (g, j) in enumerate(jobs):
                if n >= 2:
                    pe.wait_ge(k.act_done.sem, k.act_done.at(n - 1))
                if j < 2:
                    project_features(k, pe, n0 + 4 * n, k.xT, K8, n % 2)
                else:
                    project_tokens(k, pe, n0 + 4 * n, k.xT, K8, D, n % 2)

        @block.scalar
        def _(act):
            for n, (g, j) in enumerate(jobs):
                used_up(k, act, n0 + 4 * (n + 1))
                src = bank(k, 4 * (n % 2), 4)
                dst = (b.q[:, g], b.k[:, g], b.v[:, g])[j]
                act.activation(dst, v3(src, dst.shape[1], dst.shape[2]), ACT.Copy,
                               scale=ADH ** -0.5 if j == 0 else 1.0).then_inc(k.act_done.sem, 1)
    k.act_done.close(len(jobs))


def dilated_phase(k, b):
    G = len(GROUPS)
    s = Carver(k.arena, SLOTS * SLOT)
    away = s.take(G * TILES * T).rearrange("p (g t n) -> p g t n", g=G, t=TILES)
    diff = v3(s.take(TILES * T), TILES, T).bitcast(I32)
    rem = v3(s.take(TILES * T), TILES, T).bitcast(I32)
    tmp = v3(s.take(TILES * T), TILES, T)
    sc = s.take(TILES * G * T).rearrange("p (t g n) -> p t g n", t=TILES, g=G)
    pT = s.take(TILES * G * T).rearrange("p (t g n) -> p t g n", t=TILES, g=G)
    neg_max, den = s.take(TILES), s.take(TILES)
    slopes = [2.0 ** (-8.0 * (j + 1) / (G * AH)) for j in range(G * AH)]
    STEPS = 7
    turn_tile = (k.turn_tile0, k.turn_tile1)

    def turn(eng, tile, h, done):
        if h * STEPS + done:
            eng.wait_ge(turn_tile[tile].sem, turn_tile[tile].at(h * STEPS + done))

    with k.nc.Block() as block:
        @block.gpsimd
        def _(pool):
            k.pool_chain.link(pool, pool.iota(diff, pattern=[[-P, TILES], [1, T]], base=0, channel_multiplier=-1))
            pool.sem_inc(k.pool_done.sem, 1)

        @block.tensor
        def _(pe):
            for h in range(AH):
                for tile in range(TILES):
                    turn(pe, tile, h, 0)
                    for g in range(G):
                        mm = pe.matmul(k.ps[:, 4 * tile + g // 2, (g % 2) * T:(g % 2 + 1) * T],
                                       b.q[:, g, h, tile * P:(tile + 1) * P], b.k[:, g, h], start=True, stop=True)
                    mm.then_inc(turn_tile[tile].sem, 1)
                for tile in range(TILES):
                    turn(pe, tile, h, 3)
                    for g in range(G):
                        for n in range(TILES):
                            at = (g % 2) * T + n * P
                            mm = pe.transpose(k.ps[:, 4 * tile + 2 + g // 2, at:at + P], sc[:, tile, g, n * P:(n + 1) * P],
                                              k.ident[:, :])
                    mm.then_inc(turn_tile[tile].sem, 1)
                for tile in range(TILES):
                    turn(pe, tile, h, 5)
                    for g in range(G):
                        for n in range(TILES):
                            mm = pe.matmul(k.ps[:, 4 * tile, 0:ADH], pT[:, tile, g, n * P:(n + 1) * P],
                                           b.v[:, g, n, h * ADH:(h + 1) * ADH], start=(g == 0 and n == 0),
                                           stop=(g == G - 1 and n == TILES - 1))
                    mm.then_inc(turn_tile[tile].sem, 1)

        @block.scalar
        def _(act):
            for h in range(AH):
                for tile in range(TILES):
                    turn(act, tile, h, 2)
                    act.activation(sc[:, tile], sc[:, tile], ACT.Exp, bias=neg_max[:, tile:tile + 1],
                                   accum_out=den[:, tile:tile + 1]).then_inc(turn_tile[tile].sem, 1)
                for tile in range(TILES):
                    turn(act, tile, h, 4)
                    act.activation(pT[:, tile].rearrange("p g n -> p (g n)"), bank(k, 4 * tile + 2, 2)[:, 0:G * T],
                                   ACT.Copy).then_inc(turn_tile[tile].sem, 1)

        @block.vector
        def _(vec):
            link = lambda ins: k.vec_chain.link(vec, ins)
            mark = k.vec_chain.mark
            vec.wait_ge(k.pool_done.sem, k.pool_done.at(1))
            link(vec.tensor_copy(tmp, diff))
            link(vec.scalar_tensor_tensor(out=tmp, in0=tmp, scalar=-1.0, in1=tmp, op0=MUL, op1=MAX))
            for g, (window, dil) in enumerate(GROUPS):
                link(vec.tensor_scalar(away[:, g], tmp, float(window // 2), BIG * 100, ALU.is_gt, MUL))
                if dil > 1:
                    link(vec.tensor_scalar(rem, diff, dil - 1, None, ALU.bitwise_and))
                    link(vec.tensor_copy(sc[:, :, 0], rem))
                    link(vec.tensor_scalar(sc[:, :, 0], sc[:, :, 0], 0.0, BIG * 100, ALU.is_gt, MUL))
                    link(vec.tensor_tensor(away[:, g], away[:, g], sc[:, :, 0], ADD))
                link(vec.tensor_tensor(away[:, g], away[:, g], tmp, ADD))
            for h in range(AH):
                for tile in range(TILES):
                    turn(vec, tile, h, 1)
                    for g in range(G):
                        mark(vec.scalar_tensor_tensor(out=sc[:, tile, g], in0=away[:, g, tile], scalar=-slopes[g * AH + h],
                                                      in1=k.ps[:, 4 * tile + g // 2, (g % 2) * T:(g % 2 + 1) * T],
                                                      op0=MUL, op1=ADD))
                    vec.wait_ge(k.vec_chain.sem, k.vec_chain.n)
                    vec.tensor_reduce(neg_max[:, tile:tile + 1], sc[:, tile].rearrange("p g n -> p (g n)"), X, MAX,
                                      negate=True).then_inc(turn_tile[tile].sem, 1)
                for tile in range(TILES):
                    turn(vec, tile, h, 6)
                    link(vec.reciprocal(den[:, tile:tile + 1], den[:, tile:tile + 1]))
                    vec.tensor_scalar(b.o[:, tile, h * ADH:(h + 1) * ADH], k.ps[:, 4 * tile, 0:ADH], den[:, tile:tile + 1],
                                      None, MUL).then_inc(turn_tile[tile].sem, 1)
            for tile in range(TILES):
                turn(vec, tile, AH, 0)
    k.pool_done.close(1)
    for sig in turn_tile:
        sig.close(AH * STEPS)


def rms_rows_phase(k, gain):
    c = Carver(k.region, k.region_w)
    row, sq = c.take(D), c.take(D)
    ss = k.stat[:, 0:TILES]
    with k.nc.Block() as block:
        @block.sync
        def _(sp):
            sp.dma_start(row, gain.partition_broadcast(P)).then_inc(k.small_landed.sem, 16)

        @block.scalar
        def _(act):
            act.wait_ge(k.vec_done.sem, k.vec_done.at(1))
            act.activation(ss, ss, ACT.Sqrt).then_inc(k.act_done.sem, 1)

        @block.vector
        def _(vec):
            link = lambda ins: k.vec_chain.link(vec, ins)
            for tile in range(TILES):
                link(vec.tensor_tensor_reduce(sq, k.x[:, tile], k.x[:, tile], 1.0, 0.0, MUL, ADD, ss[:, tile:tile + 1]))
            link(vec.tensor_scalar(ss, ss, 1.0 / D, RMS_EPS, MUL, ADD))
            vec.sem_inc(k.vec_done.sem, 1)
            vec.wait_ge(k.small_landed.sem, k.small_landed.at(16))
            vec.wait_ge(k.act_done.sem, k.act_done.at(1))
            link(vec.reciprocal(ss, ss))
            for tile in range(TILES):
                link(vec.scalar_tensor_tensor(out=k.x[:, tile], in0=k.x[:, tile], scalar=ss[:, tile:tile + 1], in1=row,
                                              op0=MUL, op1=MUL))
    k.small_landed.close(16)
    k.vec_done.close(1)
    k.act_done.close(1)


def layer_norm_phase(k, gain, bias, n_used, extra=None):
    c = Carver(k.region, k.region_w)
    row, off, sq = c.take(D), c.take(D), c.take(D)
    mean, var = k.stat[:, 0:TILES], k.stat[:, TILES:2 * TILES]
    with k.nc.Block() as block:
        @block.sync
        def _(sp):
            sp.dma_start(row, gain.partition_broadcast(P)).then_inc(k.small_landed.sem, 16)
            sp.dma_start(off, bias.partition_broadcast(P)).then_inc(k.small_landed.sem, 16)
            ahead(k, sp, n_used)

        @block.scalar
        def _(act):
            act.wait_ge(k.vec_done.sem, k.vec_done.at(1))
            act.activation(var, var, ACT.Sqrt).then_inc(k.act_done.sem, 1)

        @block.vector
        def _(vec):
            link = lambda ins: k.vec_chain.link(vec, ins)
            mark = k.vec_chain.mark
            used_up(k, vec, n_used)
            link(vec.scalar_tensor_tensor(out=k.x[:, :, :], in0=k.x[:, :, :], scalar=ALPHA,
                                          in1=v3(bank(k, 0, 4), TILES, D), op0=MUL, op1=ADD))
            if extra is not None:
                link(vec.tensor_tensor(k.x[:, :, :], k.x[:, :, :], extra, ADD))
            link(vec.tensor_reduce(mean, k.x[:, :, :], X, ADD))
            link(vec.tensor_scalar(mean, mean, 1.0 / D, None, MUL))
            for tile in range(TILES):
                link(vec.tensor_scalar(k.x[:, tile], k.x[:, tile], mean[:, tile:tile + 1], None, SUB))
                link(vec.tensor_tensor_reduce(sq, k.x[:, tile], k.x[:, tile], 1.0, 0.0, MUL, ADD, var[:, tile:tile + 1]))
            link(vec.tensor_scalar(var, var, 1.0 / D, LN_EPS, MUL, ADD))
            vec.sem_inc(k.vec_done.sem, 1)
            vec.wait_ge(k.small_landed.sem, k.small_landed.at(32))
            vec.wait_ge(k.act_done.sem, k.act_done.at(1))
            link(vec.reciprocal(var, var))
            for tile in range(TILES):
                link(vec.scalar_tensor_tensor(out=k.x[:, tile], in0=k.x[:, tile], scalar=var[:, tile:tile + 1], in1=row,
                                              op0=MUL, op1=MUL))
            link(vec.tensor_tensor(k.x[:, :, :], k.x[:, :, :], v3(off, 1, D).to_broadcast([P, TILES, D]), ADD))
    k.small_landed.close(32)
    k.vec_done.close(1)
    k.act_done.close(1)


SLICES = ("dq", "dk", "sq", "sk", "iq")
SLOT_OF = {name: 4 * j for j, name in enumerate(SLICES)}
IK_SLOT = 4 * len(SLICES)


def second_buffers(k):
    c = Carver(k.region, k.region_w)
    b = Core()
    b.h = v3(c.take(TILES * SEG["ga"]), TILES, SEG["ga"])
    b.sg = c.take(2 * TILES * D).rearrange("p (j t d) -> p j t d", j=2, t=TILES)
    b.f = v3(c.take((IK_SLOT + 1) * T), IK_SLOT + 1, T)
    b.ya, b.yb = (v3(c.take(TILES * 4 * P), TILES, 4 * P) for _ in range(2))
    b.ik2 = v3(c.take(TILES * P), TILES, P)
    b.lam = c.take(4)
    b.end = c.at
    return b


def w_in_phase(k, b, i):
    n0 = k.starts[f"win{i}"]
    spans = [(0, D), (D, D), (2 * D, D), (3 * D, SEG["ga"] - 3 * D), (SEG["ga"], D), (SEG["gb"], D)]
    with k.nc.Block() as block:
        @block.sync
        def _(sp):
            ahead(k, sp, n0 + 4 * len(spans))

        @block.tensor
        def _(pe):
            for n, (c0, width) in enumerate(spans):
                if n >= 2:
                    pe.wait_ge(k.act_done.sem, k.act_done.at(n - 1))
                project_tokens(k, pe, n0 + 4 * n, k.xT, K8, width, n % 2)

        @block.scalar
        def _(act):
            for n, (c0, width) in enumerate(spans):
                used_up(k, act, n0 + 4 * (n + 1))
                src = v3(bank(k, 4 * (n % 2), 4), TILES, D)[:, :, 0:width]
                if n < 4:
                    ins = act.activation(b.h[:, :, c0:c0 + width], src, ACT.Copy)
                else:
                    ins = act.activation(b.sg[:, n - 4], src, ACT.Sigmoid)
                ins.then_inc(k.act_done.sem, 1)
    k.act_done.close(len(spans))


def rotary_phase(k, b, i):
    R2 = ROT // 2
    s = Carver(k.arena, SLOTS * SLOT)
    t1, t2, t3, t4 = (s.take(TILES * 16 * R2).rearrange("p (t h r) -> p t h r", t=TILES, r=R2) for _ in range(4))
    lp = v3(s.take(4 * HN), 4, HN)
    lt = v3(s.take(2 * HN), 2, HN)
    lam_init = 0.8 - 0.6 * math.exp(-0.3 * i)
    groups = [[(seg, j) for seg in SLICES for j in range(4)][g:g + 2] for g in range(0, IK_SLOT, 2)] + [[("ik", 0)]]
    with k.nc.Block() as block:
        @block.sync
        def _(sp):
            sp.dma_start(lp.rearrange("p j n -> p (j n)"),
                         k.a["diff_lambda_2"][i].rearrange("j n -> (j n)").partition_broadcast(P)).then_inc(k.small_landed.sem, 16)

        @block.vector
        def _(vec):
            link = lambda ins: k.vec_chain.link(vec, ins)
            mark = k.vec_chain.mark
            for c0, heads in ((SEG["dq"], 16), (SEG["sq"], 16), (SEG["iq"], 9)):
                v = b.h[:, :, c0:c0 + heads * HN].rearrange("p t (h n) -> p t h n", n=HN)
                x1, x2 = v[:, :, :, 0:R2], v[:, :, :, R2:ROT]
                cos, sin = (tab[:, :, :].rearrange("p t (a r) -> p t a r", a=1).to_broadcast([P, TILES, heads, R2])
                            for tab in (k.cos, k.sin))
                a1, a2, a3, a4 = (t[:, :, 0:heads] for t in (t1, t2, t3, t4))
                mark(vec.tensor_tensor(a1, x1, cos, MUL))
                mark(vec.tensor_tensor(a2, x2, sin, MUL))
                mark(vec.tensor_tensor(a3, x2, cos, MUL))
                link(vec.tensor_tensor(a4, x1, sin, MUL))
                mark(vec.tensor_tensor(x1, a1, a2, SUB))
                link(vec.tensor_tensor(x2, a3, a4, ADD))
            for r in range(2):
                mark(vec.tensor_copy(b.ik2[:, :, r * HN:(r + 1) * HN], b.h[:, :, SEG["ik"]:SEG["ik"] + HN]))
            vec.wait_ge(k.vec_chain.sem, k.vec_chain.n)
            vec.sem_inc(k.vec_done.sem, 1)
            vec.wait_ge(k.small_landed.sem, k.small_landed.at(16))
            l4 = lp.rearrange("p (a b) n -> p a b n", b=2)
            link(vec.tensor_tensor(lt, l4[:, :, 0], l4[:, :, 1], MUL))
            link(vec.tensor_reduce(b.lam[:, 0:2], lt, X, ADD))
            vec.sem_inc(k.vec_done.sem, 1)
            vec.wait_ge(k.act_done.sem, k.act_done.at(1))
            link(vec.tensor_tensor(b.lam[:, 2:3], b.lam[:, 1:2], b.lam[:, 0:1], SUB))
            link(vec.tensor_scalar(b.lam[:, 2:3], b.lam[:, 2:3], -lam_init, None, ADD))

        @block.tensor
        def _(pe):
            pe.wait_ge(k.vec_done.sem, k.vec_done.at(1))
            for g, members in enumerate(groups):
                if g >= 8:
                    pe.wait_ge(k.act_done.sem, k.act_done.at(1 + g - 7))
                for m, (seg, j) in enumerate(members):
                    for tile in range(TILES):
                        src = b.ik2[:, tile] if seg == "ik" else b.h[:, tile, SEG[seg] + j * P:SEG[seg] + (j + 1) * P]
                        at = m * T + tile * P
                        mm = pe.transpose(k.ps[:, g % 8, at:at + P], src, k.ident[:, :])
                mm.then_inc(k.pe_done.sem, 1)

        @block.scalar
        def _(act):
            act.wait_ge(k.vec_done.sem, k.vec_done.at(2))
            act.activation(b.lam[:, 0:2], b.lam[:, 0:2], ACT.Exp).then_inc(k.act_done.sem, 1)
            for g, members in enumerate(groups):
                act.wait_ge(k.pe_done.sem, k.pe_done.at(g + 1))
                n = len(members)
                act.activation(b.f[:, 2 * g:2 * g + n], v3(k.ps[:, g % 8, 0:n * T], n, T), ACT.Copy).then_inc(k.act_done.sem, 1)
    k.small_landed.close(16)
    k.vec_done.close(2)
    k.pe_done.close(len(groups))
    k.act_done.close(1 + len(groups))


def pair_attention_phase(k, b, i):
    s = Carver(k.arena, SLOTS * SLOT)
    causal = v3(s.take(TILES * T), TILES, T)
    mask = v3(s.take(TILES * T), TILES, T)
    work, best = v3(s.take(TILES * T), TILES, T), v3(s.take(TILES * 8), TILES, 8)
    relu = s.take(TILES * 8 * T).rearrange("p (t h n) -> p t h n", t=TILES, h=8)
    iw = v3(s.take(TILES * SH), TILES, SH)
    sc = s.take(TILES * 2 * T).rearrange("p (t w n) -> p t w n", t=TILES, w=2)
    pT = s.take(TILES * 2 * T).rearrange("p (t w n) -> p t w n", t=TILES, w=2)
    neg_max, den = v3(s.take(TILES * 2), TILES, 2), v3(s.take(TILES * 2), TILES, 2)
    scale = HN ** -0.5
    IDX, STEPS = 3, 8
    turn_tile = (k.turn_tile0, k.turn_tile1)

    def turn(eng, tile, unit_, done):
        n = IDX + unit_ * STEPS + done
        eng.wait_ge(turn_tile[tile].sem, turn_tile[tile].at(n))

    def end(ins, tile):
        ins.then_inc(turn_tile[tile].sem, 1)

    def keys(tile):
        return (tile + 1) * P

    with k.nc.Block() as block:
        @block.gpsimd
        def _(pool):
            k.pool_chain.link(pool, pool.memset(causal, 0.0))
            for tile in range(TILES):
                k.pool_chain.link(pool, pool.affine_select(out=causal[:, tile], in_=causal[:, tile], pattern=[[-1, T]],
                                                           compare_op=ALU.is_ge, fill=-BIG, base=tile * P,
                                                           channel_multiplier=1))
            pool.sem_inc(k.pool_done.sem, 1)

        @block.tensor
        def _(pe):
            for tile in range(TILES):
                for hd in range(SH):
                    par, pair = hd % 2, hd // 2
                    half = slice(par * HN, (par + 1) * HN)
                    mm = pe.matmul(k.ps[:, 4 * tile + 2 * par + pair // 2, (pair % 2) * T:(pair % 2) * T + keys(tile)],
                                   b.f[half, SLOT_OF["iq"] + pair, tile * P:(tile + 1) * P], b.f[half, IK_SLOT, 0:keys(tile)],
                                   start=True, stop=True)
                end(mm, tile)
            for u in range(DH + SH // 2):
                qs, ks = (SLOT_OF["dq"] + u, SLOT_OF["dk"] + u) if u < DH else (SLOT_OF["sq"] + u - DH, SLOT_OF["sk"] + u - DH)
                for tile in range(TILES):
                    turn(pe, tile, u, 0)
                    for w in range(2):
                        half = slice(w * HN, (w + 1) * HN)
                        mm = pe.matmul(k.ps[:, 4 * tile + w, 0:keys(tile)], b.f[half, qs, tile * P:(tile + 1) * P],
                                       b.f[half, ks, 0:keys(tile)], start=True, stop=True)
                    end(mm, tile)
                for tile in range(TILES):
                    turn(pe, tile, u, 4)
                    for w in range(1 if u < DH else 2):
                        for n in range(tile + 1):
                            at = w * T + n * P
                            mm = pe.transpose(k.ps[:, 4 * tile + 2, at:at + P], sc[:, tile, w, n * P:(n + 1) * P], k.ident[:, :])
                    end(mm, tile)
                for tile in range(TILES):
                    turn(pe, tile, u, 6)
                    for w in range(1 if u < DH else 2):
                        width = P if u < DH else HN
                        c0 = SEG["dv"] + u * P if u < DH else SEG["sv"] + ((u - DH) * 2 + w) * HN
                        for n in range(tile + 1):
                            mm = pe.matmul(k.ps[:, 4 * tile + 3, w * HN:w * HN + width], pT[:, tile, w, n * P:(n + 1) * P],
                                           b.h[:, n, c0:c0 + width], start=(n == 0), stop=(n == tile))
                    end(mm, tile)

        @block.scalar
        def _(act):
            for tile in range(TILES):
                act.wait_ge(turn_tile[tile].sem, turn_tile[tile].at(1))
                end(act.activation(relu[:, tile, :, 0:keys(tile)], v3(bank(k, 4 * tile, 4), 8, T)[:, :, 0:keys(tile)],
                                   ACT.Relu, scale=scale), tile)
            for u in range(DH + SH // 2):
                for tile in range(TILES):
                    turn(act, tile, u, 2)
                    for w in range(2):
                        k.act_chain.mark(act.activation(sc[:, tile, w, 0:keys(tile)], sc[:, tile, w, 0:keys(tile)], ACT.Exp,
                                                        bias=neg_max[:, tile, w:w + 1], accum_out=den[:, tile, w:w + 1]))
                    act.wait_ge(k.act_chain.sem, k.act_chain.n)
                    act.sem_inc(turn_tile[tile].sem, 1)
                for tile in range(TILES):
                    turn(act, tile, u, 5)
                    n = 1 if u < DH else 2
                    end(act.activation(pT[:, tile, 0:n, 0:keys(tile)], v3(k.ps[:, 4 * tile + 2, 0:n * T], n, T)[:, :, 0:keys(tile)],
                                       ACT.Copy), tile)

        @block.vector
        def _(vec):
            link = lambda ins: k.vec_chain.link(vec, ins)
            mark = k.vec_chain.mark
            link(vec.tensor_scalar(iw, b.h[:, :, SEG["iw"]:SEG["iw"] + SH], SH ** -0.5, None, MUL))
            vec.wait_ge(k.pool_done.sem, k.pool_done.at(1))
            for tile in range(TILES):
                vec.wait_ge(turn_tile[tile].sem, turn_tile[tile].at(2))
                n = keys(tile)
                wk = work[:, tile, 0:n]
                for hd in range(SH):
                    r = relu[:, tile, (hd % 2) * 4 + hd // 2, 0:n]
                    if hd == 0:
                        link(vec.tensor_scalar(wk, r, iw[:, tile, 0:1], None, MUL))
                    else:
                        link(vec.scalar_tensor_tensor(out=wk, in0=r, scalar=iw[:, tile, hd:hd + 1], in1=wk, op0=MUL, op1=ADD))
                link(vec.tensor_tensor(wk, wk, causal[:, tile, 0:n], ADD))
                for _ in range(TOPK // 8):
                    link(vec.max(best[:, tile], wk))
                    link(vec.match_replace(wk, best[:, tile], wk, -3e38))
                link(vec.tensor_scalar(mask[:, tile, 0:n], wk, -2e38, -BIG, ALU.is_gt, MUL))
                link(vec.tensor_tensor(mask[:, tile, 0:n], mask[:, tile, 0:n], causal[:, tile, 0:n], ADD))
                vec.sem_inc(turn_tile[tile].sem, 1)
            for u in range(DH + SH // 2):
                hide = causal if u < DH else mask
                for tile in range(TILES):
                    turn(vec, tile, u, 1)
                    n = keys(tile)
                    link(vec.scalar_tensor_tensor(out=sc[:, tile, :, 0:n], in0=k.ps[:, 4 * tile:4 * tile + 2, 0:n], scalar=scale,
                                                  in1=hide[:, tile:tile + 1, 0:n].to_broadcast([P, 2, n]), op0=MUL, op1=ADD))
                    end(vec.tensor_reduce(neg_max[:, tile], sc[:, tile, :, 0:n], X, MAX, negate=True), tile)
                for tile in range(TILES):
                    turn(vec, tile, u, 3)
                    n = keys(tile)
                    link(vec.reciprocal(den[:, tile], den[:, tile]))
                    if u < DH:
                        link(vec.tensor_tensor(den[:, tile, 1:2], den[:, tile, 1:2], b.lam[:, 2:3], MUL))
                        link(vec.tensor_scalar(sc[:, tile, 0, 0:n], sc[:, tile, 0, 0:n], den[:, tile, 0:1], None, MUL))
                        end(vec.scalar_tensor_tensor(out=sc[:, tile, 0, 0:n], in0=sc[:, tile, 1, 0:n], scalar=den[:, tile, 1:2],
                                                     in1=sc[:, tile, 0, 0:n], op0=MUL, op1=ADD), tile)
                    else:
                        vec.sem_inc(turn_tile[tile].sem, 1)
                for tile in range(TILES):
                    turn(vec, tile, u, 7)
                    src = k.ps[:, 4 * tile + 3, 0:P]
                    if u < DH:
                        end(vec.tensor_copy(b.ya[:, tile, u * P:(u + 1) * P], src), tile)
                    else:
                        end(vec.tensor_tensor(v3(b.yb[:, tile, (u - DH) * P:(u - DH + 1) * P], 2, HN), v3(src, 2, HN),
                                              den[:, tile].rearrange("p (w a) -> p w a", a=1).to_broadcast([P, 2, HN]), MUL), tile)
    k.pool_done.close(1)
    for sig in turn_tile:
        sig.close(IDX + (DH + SH // 2) * STEPS)


def subnorm_phase(k, b, i, end):
    lam_init = 0.8 - 0.6 * math.exp(-0.3 * i)
    c = Carver(k.region, k.region_w, b.end)
    gain = c.take(P)
    rms = c.take(TILES * DH)
    sq = v3(b.f[:, 0:4].rearrange("p s t -> p (s t)"), TILES * DH, P)
    y = b.ya.rearrange("p t (h n) -> p (t h) n", n=P)
    with k.nc.Block() as block:
        @block.sync
        def _(sp):
            sp.dma_start(gain, k.a["diff_subln_g_2"][i].partition_broadcast(P)).then_inc(k.small_landed.sem, 16)
            ahead(k, sp, end)

        @block.scalar
        def _(act):
            act.wait_ge(k.vec_done.sem, k.vec_done.at(1))
            act.activation(rms, rms, ACT.Sqrt).then_inc(k.act_done.sem, 1)

        @block.vector
        def _(vec):
            link = lambda ins: k.vec_chain.link(vec, ins)
            link(vec.tensor_tensor(sq, y, y, MUL))
            link(vec.tensor_reduce(rms, sq, X, ADD))
            link(vec.tensor_scalar(rms, rms, 1.0 / P, LN_EPS, MUL, ADD))
            vec.sem_inc(k.vec_done.sem, 1)
            vec.wait_ge(k.act_done.sem, k.act_done.at(1))
            link(vec.reciprocal(rms, rms))
            link(vec.tensor_scalar(rms, rms, 1.0 - lam_init, None, MUL))
            link(vec.tensor_tensor(y, y, rms.rearrange("p (h a) -> p h a", a=1).to_broadcast([P, TILES * DH, P]), MUL))
            vec.wait_ge(k.small_landed.sem, k.small_landed.at(16))
            link(vec.tensor_tensor(y, y, v3(gain, 1, P).to_broadcast([P, TILES * DH, P]), MUL))
    k.small_landed.close(16)
    k.vec_done.close(1)
    k.act_done.close(1)


def two_products_phase(k, names, lhs, rows, finish):
    n0, n1 = (k.starts[n] for n in names)
    per = min(2, rows[1] // 2)
    end = n1 + rows[1] // per
    with k.nc.Block() as block:
        @block.sync
        def _(sp):
            ahead(k, sp, end)

        @block.tensor
        def _(pe):
            project_tokens(k, pe, n0, lhs[0], rows[0], D, 0)
            project_tokens(k, pe, n1, lhs[1], rows[1], D, 1, per)

        finish(block, n1, end)


def second_layer_phases(k, i):
    a = k.a
    b = second_buffers(k)
    w_in_phase(k, b, i)
    rotary_phase(k, b, i)
    pair_attention_phase(k, b, i)
    subnorm_phase(k, b, i, k.starts[f"wbd{i}"])
    yaT, ybT = b.f[:, 0:4], b.f[:, 4:8]
    to_features_phase(k, b.ya, yaT, 4, k.starts[f"wbd{i}"])
    to_features_phase(k, b.yb, ybT, 4, k.starts[f"wbd{i}"])
    merged = v3(k.region[:, 0:TILES * D], TILES, D)
    mergedT = v3(k.region[:, TILES * D:2 * TILES * D], K8, T)

    def merge(block, first, end):
        @block.vector
        def _(vec):
            link = lambda ins: k.vec_chain.link(vec, ins)
            used_up(k, vec, first)
            link(vec.tensor_tensor(merged, v3(bank(k, 0, 4), TILES, D), b.sg[:, 0], MUL))
            used_up(k, vec, end)
            link(vec.tensor_tensor(b.sg[:, 1], v3(bank(k, 4, 4), TILES, D), b.sg[:, 1], MUL))
            link(vec.tensor_tensor(merged, merged, b.sg[:, 1], ADD))

    two_products_phase(k, (f"wbd{i}", f"wbs{i}"), (yaT, ybT), (4, 4), merge)
    to_features_phase(k, merged, mergedT, K8, k.starts[f"wout{i}"])
    n0 = k.starts[f"wout{i}"]
    with k.nc.Block() as block:
        @block.sync
        def _(sp):
            ahead(k, sp, n0 + 4)

        @block.tensor
        def _(pe):
            project_tokens(k, pe, n0, mergedT, K8, D, 0)
    layer_norm_phase(k, a["ln1_g_2"][i], a["ln1_b_2"][i], n0 + 4)
    to_features_phase(k, k.x, k.xT, K8, k.starts[f"pleg{i}"])

    c = Carver(k.region, k.region_w, k.region_w - 2 * TILES * D)
    ple = v3(c.take(TILES * D), TILES, D)
    p_tok, pT = v3(c.take(TILES * T), TILES, T), v3(c.take(2 * T), 2, T)
    with k.nc.Block() as block:
        @block.sync
        def _(sp):
            sp.dma_start(p_tok, a["p_2"][i, 0].rearrange("(t p) d -> p t d", p=P)).then_inc(k.small_landed.sem, 16)

        @block.vector
        def _(vec):
            vec.wait_ge(k.small_landed.sem, k.small_landed.at(16))
    k.small_landed.close(16)
    to_features_phase(k, p_tok, pT, 2, k.starts[f"pleg{i}"])

    def embed(block, first, end):
        @block.scalar
        def _(act):
            used_up(k, act, first)
            act.activation(ple, v3(bank(k, 0, 4), TILES, D), ACT.Sigmoid).then_inc(k.act_done.sem, 1)

        @block.vector
        def _(vec):
            vec.wait_ge(k.act_done.sem, k.act_done.at(1))
            used_up(k, vec, end)
            k.vec_chain.link(vec, vec.tensor_tensor(ple, ple, v3(bank(k, 4, 4), TILES, D), MUL))

    two_products_phase(k, (f"pleg{i}", f"ple{i}"), (k.xT, pT), (K8, 2), embed)
    k.act_done.close(1)
    route_phase(k, DEPTH + i, k.starts[f"moe{DEPTH + i}"])
    experts_phase(k, DEPTH + i)
    layer_norm_phase(k, a["ln2_g_2"][i], a["ln2_b_2"][i], k.starts[f"moe{DEPTH + i}"] + 3 * EXPERTS, extra=ple)


def build(nc, a, out, upto=None):
    with ExitStack() as ctx:
        k = make_core(nc, ctx, a)
        phases = []

        def phase(name, f):
            phases.append((name, f))

        for i in range(DEPTH):
            phase(f"ada{i}", lambda i=i: ada_phase(k, i))
            first = "rkv0" if i == 0 else "qkv"
            phase(f"norm_tm{i}", lambda i=i, f=first: to_features_phase(k, k.x, k.xT, K8, k.starts[f], norm=0))
            if i == 0:
                def mix():
                    b = rwkv_buffers(k)
                    rwkv_project_phase(k, b)
                    og = rwkv_mix_phase(k, b)
                    k.mixT = v3(k.region[:, b.end:b.end + T * K8], K8, T)
                    to_features_phase(k, og, k.mixT, K8, k.starts["rwo"])
                    residual_phase(k, "rwo", k.mixT, 0)
                phase("rwkv", mix)

            else:
                def mix():
                    b = Core()
                    qkv_phase(k, b)
                    dilated_phase(k, b)
                    mixT = v3(k.region[:, 0:T * K8], K8, T)
                    to_features_phase(k, b.o, mixT, K8, k.starts["awo"])
                    residual_phase(k, "awo", mixT, 0)
                phase("dilated", mix)

            def moe(i=i):
                to_features_phase(k, k.x, k.xT, K8, k.starts[f"moe{i}"], norm=1)
                route_phase(k, i, k.starts[f"moe{i}"])
                experts_phase(k, i)
                moe_residual_phase(k, i)
            phase(f"moe{i}", moe)
        phase("final", lambda: rms_rows_phase(k, a["final_g"]))
        for i in range(DEPTH):
            phase(f"second_x{i}", lambda i=i: to_features_phase(k, k.x, k.xT, K8, k.starts[f"win{i}"]))
            phase(f"second{i}", lambda i=i: second_layer_phases(k, i))
        setup_phase(k)
        for name, f in phases:
            f()
            if name == upto:
                break
        src = k.x
        with nc.Block() as block:
            @block.sync
            def _(sp):
                sp.dma_start(out.rearrange("b (t p) d -> p (b t) d", p=P), src[:, :, :]).then_inc(k.stored.sem, 16)
                sp.wait_ge(k.stored.sem, k.stored.at(16))


def kernel(**inputs):
    import numpy as _np
    import concourse.bacc as _bacc
    from concourse import mybir as _mybir
    from concourse.bass_utils import run_bass_kernel_spmd as _run

    nc = _bacc.Bacc("TRN2", target_bir_lowering=False, num_devices=1)
    arrays, args = {}, {}
    for name, value in inputs.items():
        v = _np.ascontiguousarray(value)
        arrays[f"in_{name}"] = v
        args[name] = nc.dram_tensor(f"in_{name}", v.shape, _mybir.dt.from_np(v.dtype), kind="ExternalInput").ap()
    out = nc.dram_tensor("out", (1, T, D), F32, kind="ExternalOutput").ap()
    build(nc, args, out)
    r = _run(nc, [arrays], core_ids=[0])
    return r.results[0]["out"]
```

```python
import math
from contextlib import ExitStack

import numpy as np
import concourse.bass as bass
from concourse import mybir

F32 = mybir.dt.float32
I32 = mybir.dt.int32
ALU = mybir.AluOpType
ACT = mybir.ActivationFunctionType
X = mybir.AxisListType.X
MUL, ADD, SUB, MAX = ALU.mult, ALU.add, ALU.subtract, ALU.max

P = 128
T, D = 256, 1024
TILES = T // P
K8 = D // P
DEPTH = 2
SLOTS, SLOT = 12, 2048
HALF = 512

HEADS, HN = 16, 64
CH = 64
RMS_EPS, GN_EPS, LN_EPS = 1e-6, 64e-5, 1e-5

GROUPS = ((128, 1), (512, 4), (2048, 16))
AH, ADH = 8, 128

N_GROUPS, PER_GROUP = 4, 8
EXPERTS = N_GROUPS * PER_GROUP
F = 256
PAIRS = EXPERTS // 2
CAP = P // 2
UNROLL = 2
FAR = 1e4

SEG = dict(dq=0, dk=512, dv=1024, sq=1536, sk=2048, sv=2560, iq=3072, ik=3584, iw=3648, ga=3656, gb=4680)
W_IN = 5704
DH, SH = 4, 8
TOPK = min(256, T // 4)
ROT = 16
THETA = 500000.0
ALPHA = (2 * DEPTH) ** 0.25
BIG = 1e30


class Signal:

    def __init__(self, sem):
        self.sem, self.base = sem, 0

    def at(self, n):
        return self.base + n

    def close(self, n):
        self.base += n


class Chain:

    def __init__(self, sem):
        self.sem, self.n = sem, 0

    def mark(self, ins):
        self.n += 1
        ins.then_inc(self.sem, 1)

    def link(self, eng, ins):
        self.mark(ins)
        eng.wait_ge(self.sem, self.n)


class Carver:

    def __init__(self, buf, width, start=0):
        self.buf, self.width, self.at = buf, width, start

    def take(self, n):
        assert self.at + n <= self.width, (self.at + n, self.width)
        v = self.buf[:, self.at:self.at + n]
        self.at += n
        return v


class Core:
    pass


def plan_streams(a):

    def jobs(w, spans, per=2):
        rows = w.shape[0] // P
        v = w.rearrange("(p k) n -> p k n", k=rows)
        return [v[:, per * u:per * (u + 1), c0:c0 + n] for c0, n in spans for u in range(rows // per)]

    def wide(n):
        return [(c, min(D, n - c)) for c in range(0, n, D)]

    def moe(i, gate, up, down):
        g = gate[i].rearrange("g e (p k) f -> (g e) p (k f)", k=K8)
        u = up[i].rearrange("g e (p k) f -> (g e) p (k f)", k=K8)
        d = down[i].rearrange("g e (p j) n -> (g e) p (j n)", j=2)
        order = [g[0], u[0], g[1], u[1]]
        for e in range(0, EXPERTS - 2, 2):
            order += [g[e + 2], u[e + 2], g[e + 3], u[e + 3], d[e], d[e + 1]]
        return order + [d[EXPERTS - 2], d[EXPERTS - 1]]

    plan = []
    for i in range(DEPTH):
        plan.append((f"ada{i}", jobs(a["ada_w"][i], wide(6 * D))))
        if i == 0:
            for j in range(3):
                plan.append((f"rkv{j}", jobs(a["rw_w_rkv"][0, j], wide(D))))
            plan.append(("scratch", []))
            plan.append(("rwo", jobs(a["rw_w_o"][0], wide(D))))
        else:
            plan.append(("qkv", jobs(a["at_w_qkv"][0], wide(9 * D))))
            plan.append(("scratch", []))
            plan.append(("awo", jobs(a["at_w_o"][0], wide(D))))
        plan.append((f"moe{i}", moe(i, a["moe_w_gate"], a["moe_w_up"], a["moe_w_down"])))
    for i in range(DEPTH):
        spans = [(0, D), (D, D), (2 * D, D), (3 * D, SEG["ga"] - 3 * D), (SEG["ga"], D), (SEG["gb"], D)]
        plan.append((f"win{i}", jobs(a["w_in_2"][i], spans)))
        plan.append(("scratch", []))
        plan.append((f"wbd{i}", jobs(a["w_branch_diff_2"][i], wide(D))))
        plan.append((f"wbs{i}", jobs(a["w_branch_dsa_2"][i], wide(D))))
        plan.append((f"wout{i}", jobs(a["w_out_2"][i], wide(D))))
        plan.append((f"pleg{i}", jobs(a["w_ple_gate_2"][i], wide(D))))
        plan.append((f"ple{i}", jobs(a["w_ple_2"][i], wide(D), per=1)))
        plan.append((f"moe{DEPTH + i}", moe(i, a["w_exp_gate_2"], a["w_exp_up_2"], a["w_exp_down_2"])))
    return plan


def make_core(nc, ctx, a):
    k = Core()
    k.nc, k.a = nc, a

    def sb(name, shape, dt=F32):
        return ctx.enter_context(nc.sbuf_tensor(name, shape, dt))

    k.arena = sb("arena", [P, SLOTS * SLOT])
    k.region_w = 21248
    k.region = sb("region", [P, k.region_w])
    k.x = sb("x_tokens", [P, TILES, D])
    k.xT = sb("x_features", [P, K8, T])
    k.gate_row = sb("gate_rows", [P, 2, D])
    k.mod = sb("mod_columns", [P, 6, K8])
    k.scale_col = sb("scale_columns", [P, 2, K8])
    k.ident = sb("identity", [P, P])
    k.router = sb("router", [P, K8, N_GROUPS + EXPERTS])
    k.router_bias = sb("router_bias", [P, N_GROUPS + EXPERTS])
    k.cond = sb("condition", [P, K8])
    k.desc = sb("descending", [P, PER_GROUP])
    k.stat = sb("statistics", [P, 64])
    k.cos = sb("cos", [P, TILES, ROT // 2])
    k.sin = sb("sin", [P, TILES, ROT // 2])
    k.ps = ctx.enter_context(nc.psum_tensor("ps", [P, 8, HALF], F32))

    def sem(name):
        return ctx.enter_context(nc.semaphore(name))

    k.landed = [sem(f"slot_landed{s}") for s in range(SLOTS)]
    k.used = sem("units_used")
    k.vec_chain = Chain(sem("vector_chain"))
    k.act_chain = Chain(sem("scalar_chain"))
    k.pool_chain = Chain(sem("gpsimd_chain"))
    k.small_landed, k.early_landed, k.router_landed, k.stored = (
        Signal(sem(n)) for n in ("small_landed", "early_landed", "router_landed", "stored"))
    k.pe_done, k.vec_done = Signal(sem("pe_done")), Signal(sem("vec_done"))
    k.act_done, k.pool_done = Signal(sem("act_done")), Signal(sem("pool_done"))
    (k.slots_built, k.gated_built, k.gathered, k.tokens_half0, k.tokens_half1, k.turned, k.hidden_moved,
     k.gated_moved, k.silu_ready, k.hidden_ready, k.out_half, k.out_moved0, k.out_moved1) = (
        Signal(sem(name)) for name in (
            "slots_built", "gated_built", "gathered", "tokens_half0", "tokens_half1", "turned", "hidden_moved",
            "gated_moved", "silu_ready", "hidden_ready", "out_half", "out_moved0", "out_moved1"))
    k.over_landed = [sem(f"overflow_landed{i}") for i in range(2 * DEPTH)]
    k.over_turn = [sem(f"overflow_turn{i}") for i in range(2 * DEPTH)]
    k.raw_copied, k.masked = ([Signal(sem(f"{n}_tile{t}")) for t in range(TILES)] for n in ("raw_copied", "masked"))
    k.turn_prep, k.turn_joint, k.turn_tile0, k.turn_tile1 = (
        Signal(sem(f"turn_{n}")) for n in ("prepare", "joint", "tile0", "tile1"))
    k.plan, k.starts, k.stops, n = [], {}, [], 0
    for name, units in plan_streams(a):
        if name == "scratch":
            k.stops.append(n)
            continue
        k.starts[name] = n
        k.plan += units
        n += len(units)
        assert n % 2 == 0, "gate and up projections take neighbouring slots"
    k.issued = 0
    return k


def issue(k, sp, upto):
    for n in range(k.issued, min(upto, len(k.plan))):
        src = k.plan[n]
        size = int(np.prod(src.shape[1:]))
        at = (n % SLOTS) * SLOT
        dst = k.arena[:, at:at + size]
        if len(src.shape) == 3:
            dst = dst.rearrange("p (k n) -> p k n", k=src.shape[1])
        if n >= SLOTS:
            sp.wait_ge(k.used, n - SLOTS + 1)
        sp.dma_start(dst, src).then_inc(k.landed[n % SLOTS], 16)
    k.issued = max(k.issued, min(upto, len(k.plan)))


def ahead(k, sp, end):
    stop = min([s for s in k.stops if s >= end], default=len(k.plan))
    issue(k, sp, end)
    issue(k, sp, min(end + SLOTS, stop))


def landed(k, pe, n):
    pe.wait_ge(k.landed[n % SLOTS], 16 * (n // SLOTS + 1))


def used_up(k, eng, n):
    eng.wait_ge(k.used, n)


def unit(k, n, width, per=2):
    at = (n % SLOTS) * SLOT
    return k.arena[:, at:at + per * width].rearrange("p (k n) -> p k n", k=per)


def bank(k, b, n=1):
    return k.ps[:, b:b + n, :].rearrange("p b n -> p (b n)")


def project_tokens(k, pe, n0, xT, rows, width, set_, per=2, ready=None):
    halves = [(0, min(HALF, width))] + ([(HALF, width - HALF)] if width > HALF else [])
    for u in range(rows // per):
        landed(k, pe, n0 + u)
        if ready is not None:
            ready(u)
        w = unit(k, n0 + u, width, per)
        for kk in range(per):
            s = per * u + kk
            for tile in range(TILES):
                for h, (c0, n) in enumerate(halves):
                    mm = pe.matmul(k.ps[:, set_ * 4 + tile * 2 + h, 0:n], xT[:, s, tile * P:(tile + 1) * P],
                                   w[:, kk, c0:c0 + n], start=(s == 0), stop=(s == rows - 1))
        mm.then_inc(k.used, 1)


def project_features(k, pe, n0, xT, rows, set_):
    for u in range(rows // 2):
        landed(k, pe, n0 + u)
        w = unit(k, n0 + u, D)
        for kk in range(2):
            s = 2 * u + kk
            for m in range(K8):
                mm = pe.matmul(k.ps[:, set_ * 4 + m // 2, (m % 2) * T:(m % 2 + 1) * T],
                               w[:, kk, m * P:(m + 1) * P], xT[:, s, :],
                               start=(s == 0 and m % 2 == 0), stop=(s == rows - 1), skip_group_check=True)
        mm.then_inc(k.used, 1)


def setup_phase(k):
    a = k.a
    c = Carver(k.region, k.region_w)
    pos = c.take(TILES).bitcast(I32)
    posf = c.take(TILES)
    freq = c.take(ROT // 2)
    ang, turns, red = (c.take(TILES * ROT // 2).rearrange("p (t r) -> p t r", t=TILES) for _ in range(3))
    inv = (np.float32(1.0) / np.float32(THETA) ** (np.arange(0, ROT, 2, dtype=np.float32) / np.float32(ROT)))
    two_pi = 2 * math.pi
    hi = float(np.float32(6.28125))
    mid = float(np.float32(np.round((two_pi - hi) * 2 ** 18) / 2 ** 18))
    lo = float(np.float32(two_pi - hi - mid))
    ROUND = float(np.float32(1.5 * 2 ** 23))

    with k.nc.Block() as block:
        @block.sync
        def _(sp):
            sp.dma_start(k.cond[:, :], a["c"].rearrange("b (p k) -> p (b k)", k=K8)).then_inc(k.early_landed.sem, 16)
            sp.dma_start(k.x[:, :, :], a["x"].rearrange("b (t p) d -> p (b t) d", p=P)).then_inc(k.small_landed.sem, 16)
            sp.dma_start(pos, a["positions_2"].rearrange("b (t p) -> p (b t)", p=P),
                         allow_slow_non_contiguous=True).then_inc(k.small_landed.sem, 16)
            ahead(k, sp, 0)
            load_router(k, sp, 0)

        @block.gpsimd
        def _(pool):
            link = lambda ins: k.pool_chain.link(pool, ins)
            link(pool.memset(k.ident[:, :], 0.0))
            link(pool.affine_select(out=k.ident[:, :], in_=k.ident[:, :], pattern=[[-1, P]], compare_op=ALU.not_equal,
                                    fill=1.0, base=0, channel_multiplier=1))

        @block.vector
        def _(vec):
            link = lambda ins: k.vec_chain.link(vec, ins)
            for j in range(PER_GROUP):
                k.vec_chain.mark(vec.memset(k.desc[:, j:j + 1], float(PER_GROUP - j)))
            for j in range(ROT // 2):
                k.vec_chain.mark(vec.memset(freq[:, j:j + 1], float(inv[j])))
            vec.wait_ge(k.small_landed.sem, k.small_landed.at(32))
            link(vec.tensor_copy(posf, pos))
            f3 = freq.rearrange("p (a r) -> p a r", a=1).to_broadcast([P, TILES, ROT // 2])
            p3 = posf.rearrange("p (t a) -> p t a", a=1).to_broadcast([P, TILES, ROT // 2])
            link(vec.tensor_tensor(ang, p3, f3, MUL))
            link(vec.tensor_scalar(turns, ang, 1.0 / two_pi, None, MUL))
            link(vec.tensor_scalar(turns, turns, ROUND, -ROUND, ADD, ADD))
            link(vec.scalar_tensor_tensor(out=red, in0=turns, scalar=-hi, in1=ang, op0=MUL, op1=ADD))
            link(vec.scalar_tensor_tensor(out=red, in0=turns, scalar=-mid, in1=red, op0=MUL, op1=ADD))
            link(vec.scalar_tensor_tensor(out=red, in0=turns, scalar=-lo, in1=red, op0=MUL, op1=ADD))
            vec.sem_inc(k.vec_done.sem, 1)
            vec.wait_ge(k.act_done.sem, k.act_done.at(1))
            link(vec.tensor_tensor(k.cos[:, :, :], ang, ang, MUL))
            link(vec.tensor_scalar(k.cos[:, :, :], k.cos[:, :, :], -2.0, 1.0, MUL, ADD))

        @block.scalar
        def _(act):
            link = lambda ins: k.act_chain.link(act, ins)
            act.wait_ge(k.early_landed.sem, k.early_landed.at(16))
            k.act_chain.mark(act.activation(k.cond[:, :], k.cond[:, :], ACT.Silu))
            act.wait_ge(k.vec_done.sem, k.vec_done.at(1))
            link(act.activation(k.sin[:, :, :], red, ACT.Sin))
            link(act.activation(ang, red, ACT.Sin, scale=0.5))
            act.sem_inc(k.act_done.sem, 1)
    k.small_landed.close(32)
    k.early_landed.close(16)
    k.vec_done.close(1)
    k.act_done.close(1)


def ada_phase(k, i, early=()):
    a = k.a
    n0 = k.starts[f"ada{i}"]
    c = Carver(k.region, k.region_w)
    gain = c.take(2 * K8).rearrange("p (j k) -> p j k", j=2)
    part = v3(c.take(6 * HALF), 6, HALF)
    bias = v3(c.take(6 * HALF), 6, HALF)
    pick = c.take(2)
    rows = c.take(D)
    COLUMNS = (0, 1, 3, 4)
    small = (
        (gain[:, 0, :], a["norm_tm_g"][i].rearrange("(p k) -> p k", k=K8)),
        (gain[:, 1, :], a["norm_cm_g"][i].rearrange("(p k) -> p k", k=K8)),
    )
    with k.nc.Block() as block:
        @block.sync
        def _(sp):
            ahead(k, sp, n0 + 24)

        @block.scalar
        def _(act):
            for dst, src in small:
                act.dma_start(dst, src).then_inc(k.small_landed.sem, 16)
            for dst, src in early:
                act.dma_start(dst, src).then_inc(k.early_landed.sem, 16)
            act.wait_ge(k.pool_done.sem, k.pool_done.at(1))
            for h in range(2):
                src = a["ada_b"][i:i + 1].rearrange("a (j h n) -> a j h n", j=6, h=2)[:, :, h]
                act.dma_start(bias[32 * h:32 * h + 1], src).then_inc(k.small_landed.sem, 16)
            act.wait_ge(k.pe_done.sem, k.pe_done.at(2))
            k.act_chain.link(act, act.activation(k.gate_row[:, :, :], k.ps[:, 0:4, :].rearrange("p (g h) n -> p g (h n)", g=2),
                                                 ACT.Copy))

        @block.gpsimd
        def _(pool):
            k.pool_chain.link(pool, pool.memset(bias, 0.0))
            pool.sem_inc(k.pool_done.sem, 1)

        @block.tensor
        def _(pe):
            for j in range(6):
                for u in range(4):
                    landed(k, pe, n0 + 4 * j + u)
                    w = unit(k, n0 + 4 * j + u, D)
                    for kk in range(2):
                        s = 2 * u + kk
                        for h in range(2):
                            quarter = 32 * (2 * kk + h)
                            mm = pe.matmul(k.ps[quarter:quarter + 32, j, :], k.cond[:, s:s + 1].to_broadcast([P, 32]),
                                           w[:, kk, h * HALF:(h + 1) * HALF], start=(u == 0), stop=(u == 3),
                                           skip_group_check=True)
                    mm.then_inc(k.used, 1)
            pe.wait_ge(k.vec_done.sem, k.vec_done.at(1))
            for h in range(2):
                for m, j in enumerate(COLUMNS):
                    mm = pe.matmul(k.ps[32 * m:32 * m + 32, 6 + h, :], pick[:, h:h + 1].to_broadcast([P, 32]), part[:, j],
                                   start=True, stop=True, skip_group_check=True)
            mm.then_inc(k.pe_done.sem, 1)
            for g in range(2):
                for h in range(2):
                    mm = pe.matmul(k.ps[:, 2 * g + h, :], pick[:, h:h + 1].to_broadcast([P, P]), part[:, 3 * g + 2],
                                   start=True, stop=True)
            mm.then_inc(k.pe_done.sem, 1)
            pe.wait_ge(k.vec_done.sem, k.vec_done.at(2))
            for s in range(K8):
                mm = pe.transpose(k.ps[:, 4 + s // 4, (s % 4) * P:(s % 4 + 1) * P], rows[:, s:D:K8], k.ident[:, :])
            mm.then_inc(k.pe_done.sem, 1)

        @block.vector
        def _(vec):
            link = lambda ins: k.vec_chain.link(vec, ins)
            for h in range(2):
                k.vec_chain.mark(vec.tensor_tensor(pick[:, h:h + 1], k.ident[:, 32 * h:32 * h + 1],
                                                   k.ident[:, 64 + 32 * h:65 + 32 * h], ADD))
            vec.wait_ge(k.small_landed.sem, k.small_landed.at(64))
            for j in range(6):
                used_up(k, vec, n0 + 4 * (j + 1))
                k.vec_chain.mark(vec.tensor_tensor(part[:, j], k.ps[:, j, :], bias[:, j], ADD))
            vec.wait_ge(k.vec_chain.sem, k.vec_chain.n)
            vec.sem_inc(k.vec_done.sem, 1)
            vec.wait_ge(k.pe_done.sem, k.pe_done.at(1))
            link(vec.tensor_copy(rows, bank(k, 6, 2)))
            vec.sem_inc(k.vec_done.sem, 1)
            vec.wait_ge(k.pe_done.sem, k.pe_done.at(3))
            for m, j in enumerate(COLUMNS):
                link(vec.tensor_copy(k.mod[:, j, :], bank(k, 4, 2)[:, 32 * m:K8 * P:P]))
            for g in range(2):
                link(vec.scalar_tensor_tensor(out=k.scale_col[:, g, :], in0=k.mod[:, 3 * g + 1, :], scalar=1.0,
                                              in1=gain[:, g, :], op0=ADD, op1=MUL))
    k.small_landed.close(64)
    k.pe_done.close(3)
    k.vec_done.close(2)
    k.pool_done.close(1)


def transposes(k, pe, src, rows, bank0, cols=None):
    for s in range(rows):
        for tile in range(TILES):
            mm = pe.transpose(k.ps[:, bank0 + s // 2, (s % 2) * T + tile * P:(s % 2) * T + (tile + 1) * P],
                              src[:, tile, s:rows * P:rows], k.ident[:, :])
    return mm


def to_features_phase(k, src, dst, rows, end, norm=None, loaded=0):
    xn = k.region[:, 0:TILES * D].rearrange("p (t d) -> p t d", t=TILES)
    ss = k.stat[:, 0:TILES]
    rms = k.stat[:, TILES:2 * TILES]
    shared = rows // 2 if rows >= 4 else rows
    with k.nc.Block() as block:
        @block.sync
        def _(sp):
            ahead(k, sp, end)

        @block.scalar
        def _(act):
            if norm is not None:
                act.wait_ge(k.vec_done.sem, k.vec_done.at(1))
                act.activation(rms, rms, ACT.Sqrt).then_inc(k.act_done.sem, 1)
            act.wait_ge(k.pe_done.sem, k.pe_done.at(1))
            for s in range(shared, rows):
                t = k.ps[:, s // 2, (s % 2) * T:(s % 2 + 1) * T]
                if norm is None:
                    k.act_chain.mark(act.activation(dst[:, s, :], t, ACT.Copy))
                else:
                    k.act_chain.mark(act.activation(dst[:, s, :], t, ACT.Identity, scale=k.scale_col[:, norm, s:s + 1],
                                                    bias=k.mod[:, 3 * norm, s:s + 1]))
            act.wait_ge(k.act_chain.sem, k.act_chain.n)

        @block.tensor
        def _(pe):
            if norm is not None:
                pe.wait_ge(k.vec_done.sem, k.vec_done.at(2))
            if loaded:
                pe.wait_ge(k.early_landed.sem, k.early_landed.at(loaded))
            transposes(k, pe, src if norm is None else xn, rows, 0).then_inc(k.pe_done.sem, 1)

        @block.vector
        def _(vec):
            link = lambda ins: k.vec_chain.link(vec, ins)
            if norm is not None:
                for tile in range(TILES):
                    k.vec_chain.mark(vec.tensor_tensor_reduce(xn[:, tile], src[:, tile], src[:, tile], 1.0, 0.0, MUL,
                                                              ADD, ss[:, tile:tile + 1]))
                vec.wait_ge(k.vec_chain.sem, k.vec_chain.n)
                link(vec.tensor_scalar(rms, ss, 1.0 / D, RMS_EPS, MUL, ADD))
                vec.sem_inc(k.vec_done.sem, 1)
                vec.wait_ge(k.act_done.sem, k.act_done.at(1))
                link(vec.reciprocal(rms, rms))
                for tile in range(TILES):
                    link(vec.tensor_scalar(xn[:, tile], src[:, tile], rms[:, tile:tile + 1], None, MUL))
                vec.sem_inc(k.vec_done.sem, 1)
            vec.wait_ge(k.pe_done.sem, k.pe_done.at(1))
            for s in range(shared):
                t = k.ps[:, s // 2, (s % 2) * T:(s % 2 + 1) * T]
                if norm is None:
                    k.vec_chain.mark(vec.tensor_copy(dst[:, s, :], t))
                else:
                    k.vec_chain.mark(vec.tensor_scalar(dst[:, s, :], t, k.scale_col[:, norm, s:s + 1],
                                                       k.mod[:, 3 * norm, s:s + 1], MUL, ADD))
            vec.wait_ge(k.vec_chain.sem, k.vec_chain.n)
    k.pe_done.close(1)
    k.early_landed.close(loaded)
    if norm is not None:
        k.vec_done.close(2)
        k.act_done.close(1)


def residual_phase(k, name, xT, which):
    n0 = k.starts[name]
    with k.nc.Block() as block:
        @block.sync
        def _(sp):
            ahead(k, sp, n0 + 4)

        @block.tensor
        def _(pe):
            project_tokens(k, pe, n0, xT, K8, D, 0)

        @block.vector
        def _(vec):
            link = lambda ins: k.vec_chain.link(vec, ins)
            used_up(k, vec, n0 + 4)
            add_gated(k, vec, link, which, k.region[:, 0:TILES * D])


def add_gated(k, vec, link, which, scratch):
    tmp = scratch.rearrange("p (t d) -> p t d", t=TILES)
    link(vec.tensor_tensor(tmp, bank(k, 0, 4).rearrange("p (t d) -> p t d", t=TILES),
                           k.gate_row[:, which:which + 1, :].to_broadcast([P, TILES, D]), MUL))
    link(vec.tensor_tensor(k.x[:, :, :], k.x[:, :, :], tmp, ADD))


def v3(ap, a, n):
    return ap.rearrange("p (a n) -> p a n", a=a)


STAGES = tuple(2 ** s for s in range(1, int(math.log2(CH)) + 1))
FS = 256
ORDER = [(par, hp) for par in range(2) for hp in range(2)]


def rwkv_buffers(k):
    a = k.a
    c = Carver(k.region, k.region_w)
    b = Core()
    b.r, b.k, b.v = (v3(c.take(TILES * D), TILES, D) for _ in range(3))
    b.tw, b.ta = v3(c.take(2 * T), 2, T), v3(c.take(2 * T), 2, T)
    b.tg = v3(c.take(2 * T), 2, T)
    b.stage = c.take(2 * len(STAGES) * P).rearrange("p (z s n) -> p z s n", z=2, s=len(STAGES))
    b.tri = c.take(2 * 2 * P).rearrange("p (z w n) -> p z w n", z=2, w=2)
    b.blk = c.take(P)
    b.end = c.at
    b.xx = v3(c.take(K8 * T), K8, T)
    b.xs = c.take(2 * K8 * T).rearrange("p (b k t) -> p b k t", b=2, k=K8)
    b.mu = v3(c.take(6 * K8), 6, K8)
    b.w1 = c.take(K8 * P).rearrange("p (k z r) -> p k z r", k=K8, z=2)
    b.a1 = c.take(K8 * P).rearrange("p (k z r) -> p k z r", k=K8, z=2)
    b.g1 = c.take(K8 * 2 * P).rearrange("p (k z r) -> p k z r", k=K8, z=2)
    b.early = [(b.mu, a["rw_mu"][0].rearrange("j (p k) -> p j k", k=K8))]
    for z in range(2):
        b.early += [(b.w1[:, :, z, :], a["rw_w1"][0, z].rearrange("(p k) r -> p k r", k=K8)),
                    (b.a1[:, :, z, :], a["rw_a1"][0, z].rearrange("(p k) r -> p k r", k=K8)),
                    (b.g1[:, :, z, :], a["rw_g1"][0, z].rearrange("(p k) r -> p k r", k=K8))]
    s = Carver(k.arena, SLOTS * SLOT)
    b.vecs = s.take(9 * D).rearrange("p (j d) -> p j d", j=9)
    b.w2, b.a2 = s.take(D), s.take(D)
    b.g2 = v3(s.take(2 * D), 2, D)
    b.arena_at = s.at
    rows = [a["rw_w0"][0, 0], a["rw_a0"][0, 0], a["rw_w0"][0, 1], a["rw_a0"][0, 1], a["rw_k_k"][0], a["rw_k_a"][0],
            a["rw_r_k"][0].rearrange("h n -> (h n)"), a["rw_ln_w"][0], a["rw_ln_b"][0]]
    b.later = [(b.vecs[:, j, :], r.partition_broadcast(P)) for j, r in enumerate(rows)]
    b.later += [(b.w2, a["rw_w2"][0].rearrange("z r d -> (z r) d")), (b.a2, a["rw_a2"][0].rearrange("z r d -> (z r) d")),
                (b.g2, a["rw_g2"][0].rearrange("z r d -> r z d"))]
    return b


def rwkv_project_phase(k, b):
    a = k.a
    n0 = k.starts["rkv0"]
    xx, xs, mu, w1, a1, g1 = b.xx, b.xs, b.mu, b.w1, b.a1, b.g1
    n_early = 16 * len(b.early)
    freed = -(-b.arena_at // SLOT)
    assert n0 % SLOTS == 0 and freed <= 8
    with k.nc.Block() as block:
        @block.sync
        def _(sp):
            ahead(k, sp, n0 + 12)
            used_up(k, sp, n0 + freed)
            for dst, src in b.later:
                sp.dma_start(dst, src).then_inc(k.small_landed.sem, 16)

        @block.scalar
        def _(act):
            for j, dst in enumerate((b.r, b.k, b.v)):
                used_up(k, act, n0 + 4 * (j + 1))
                act.activation(dst, bank(k, 4 * (j % 2), 4).rearrange("p (t d) -> p t d", t=TILES),
                               ACT.Copy).then_inc(k.act_done.sem, 1)
            act.wait_ge(k.pe_done.sem, k.pe_done.at(1))
            act.wait_ge(k.pool_done.sem, k.pool_done.at(1))
            for z in range(2):
                half = slice(z * 64, z * 64 + 64)
                act.activation(b.tw[half, z], k.ps[half, 4, 0:T], ACT.Tanh).then_inc(k.act_done.sem, 1)
            act.wait_ge(k.pe_done.sem, k.pe_done.at(2))
            for z in range(2):
                half = slice(z * 64, z * 64 + 64)
                act.activation(b.ta[half, z], k.ps[half, 5, 0:T], ACT.Copy).then_inc(k.act_done.sem, 1)
            act.wait_ge(k.pe_done.sem, k.pe_done.at(3))
            act.activation(b.tg, v3(k.ps[:, 6, :], 2, T), ACT.Sigmoid).then_inc(k.act_done.sem, 1)

        @block.gpsimd
        def _(pool):
            link = lambda ins: k.pool_chain.link(pool, ins)

            def keep(v, pattern, base, mult):
                link(pool.affine_select(out=v, in_=v, pattern=pattern, compare_op=ALU.is_ge, fill=0.0, base=base,
                                        channel_multiplier=mult))

            for t in (b.tw, b.ta):
                link(pool.memset(t, 0.0))
            pool.sem_inc(k.pool_done.sem, 1)
            link(pool.memset(b.blk, 1.0))
            v = b.blk.rearrange("p (b m) -> p b m", m=CH)
            keep(v, [[-CH, P // CH], [0, CH]], 0, 1)
            keep(v, [[CH, P // CH], [0, CH]], CH - 1, -1)
            link(pool.memset(b.stage, 1.0))
            for z in range(2):
                for w in range(2):
                    link(pool.tensor_copy(b.tri[:, z, w], b.blk))
                    keep(b.tri[:, z, w], [[1 - 2 * z, P]], w - 1, 2 * z - 1)
                for i, m in enumerate(STAGES):
                    v = b.stage[:, z, i].rearrange("p (b q m) -> p b q m", q=2, m=m // 2)
                    if z == 0:
                        keep(v, [[-m, P // m], [-1000, 2], [0, m // 2]], -(m // 2), 1)
                        keep(v, [[m, P // m], [0, 2], [0, m // 2]], m - 1, -1)
                    else:
                        keep(v, [[-m, P // m], [1000, 2], [0, m // 2]], -1000, 1)
                        keep(v, [[m, P // m], [0, 2], [0, m // 2]], m // 2 - 1, -1)

        @block.vector
        def _(vec):
            link = lambda ins: k.vec_chain.link(vec, ins)
            mark = k.vec_chain.mark
            h = k.xT
            vec.wait_ge(k.early_landed.sem, k.early_landed.at(n_early))
            for j in range(6):
                if 2 <= j < 5:
                    used_up(k, vec, n0 + 4 * (j - 1))
                elif j == 5:
                    vec.wait_ge(k.pe_done.sem, k.pe_done.at(1))
                for u in range(K8 // 2):
                    two = slice(2 * u, 2 * u + 2)
                    if j == 0:
                        mark(vec.tensor_copy(xx[:, two, 0:1], h[:, two, 1:2]))
                        mark(vec.tensor_copy(xx[:, two, T - 1:T], h[:, two, T - 2:T - 1]))
                        link(vec.tensor_tensor(xx[:, two, 1:T - 1], h[:, two, 0:T - 2], h[:, two, 2:T], ADD))
                        link(vec.scalar_tensor_tensor(out=xx[:, two], in0=xx[:, two], scalar=0.5, in1=h[:, two], op0=MUL,
                                                      op1=SUB))
                    for s in (2 * u, 2 * u + 1):
                        mark(vec.scalar_tensor_tensor(out=xs[:, j % 2, s], in0=xx[:, s], scalar=mu[:, j, s:s + 1],
                                                      in1=h[:, s], op0=MUL, op1=ADD))
                    vec.wait_ge(k.vec_chain.sem, k.vec_chain.n)
                    vec.sem_inc(k.vec_done.sem, 1)

        @block.tensor
        def _(pe):
            for j in range(3):
                if j == 2:
                    pe.wait_ge(k.act_done.sem, k.act_done.at(1))
                project_tokens(k, pe, n0 + 4 * j, xs[:, j % 2], K8, D, j % 2,
                               ready=lambda u, j=j: pe.wait_ge(k.vec_done.sem, k.vec_done.at(4 * j + u + 1)))
            pe.wait_ge(k.act_done.sem, k.act_done.at(2))
            pe.wait_ge(k.early_landed.sem, k.early_landed.at(n_early))
            for j, w in ((3, w1), (4, a1)):
                pe.wait_ge(k.vec_done.sem, k.vec_done.at(4 * j + 4))
                for s in range(K8):
                    mm = pe.matmul(k.ps[:, 1 + j, 0:T], w[:, s].rearrange("p z r -> p (z r)"), xs[:, j % 2, s],
                                   start=(s == 0), stop=(s == K8 - 1))
                mm.then_inc(k.pe_done.sem, 1)
            pe.wait_ge(k.vec_done.sem, k.vec_done.at(24))
            for z in range(2):
                for s in range(K8):
                    mm = pe.matmul(k.ps[:, 6, z * T:(z + 1) * T], g1[:, s, z], xs[:, 1, s],
                                   start=(s == 0), stop=(s == K8 - 1))
            mm.then_inc(k.pe_done.sem, 1)
    k.early_landed.close(n_early)
    k.act_done.close(8)
    k.pool_done.close(1)
    k.vec_done.close(24)
    k.pe_done.close(3)


def rwkv_mix_phase(k, b):
    c = Carver(k.region, k.region_w, b.end)
    vecs, w2, a2, g2, blk, stage, tri = b.vecs, b.w2, b.a2, b.g2, b.blk, b.stage, b.tri
    pcs, norms, bonus, var, mean = v3(c.take(16), 2, 8), c.take(8), v3(c.take(24), 3, 8), c.take(8), c.take(8)
    s = Carver(k.arena, SLOTS * SLOT, b.arena_at)
    full = lambda: v3(c.take(TILES * FS), TILES, FS)
    two = lambda: c.take(2 * TILES * FS).rearrange("p (b t f) -> p b t f", b=2, t=TILES)
    cum, ein, eneg, ex, eh, lw, ar, bd, kk, at_ = (full() for _ in range(10))
    rt, bt, kt, kd = ein, cum, eneg, ar
    bhs, khs, gsbs = two(), two(), two()
    yb = full()
    aws = s.take(2 * TILES * 4 * P).rearrange("p (b t o w n) -> p b t o w n", b=2, t=TILES, o=4, w=2)
    arts = s.take(16 * P).rearrange("p (b h t w n) -> p b h t w n", b=2, h=2, t=TILES, w=2)
    btT, ktT = (c.take(8 * P).rearrange("p (q h t n) -> p q h t n", q=2, h=2, t=TILES) for _ in range(2))
    lq = s.take(TILES * 12 * P).rearrange("p (t o w n) -> p t o w n", t=TILES, o=4, w=3)
    mq = s.take(TILES * 8 * P).rearrange("p (t o w n) -> p t o w n", t=TILES, o=4, w=2)
    inv = s.take(TILES * 8 * P).rearrange("p (t o w n) -> p t o w n", t=TILES, o=4, w=2)
    xb = gu = lq[:, :, :, 0]
    ght = lambda tile, w: mq[:, tile, 2 * w:2 * w + 2, 0]
    us = v3(c.take(4 * HN), 4, HN)
    st = v3(c.take(2 * HN), 2, HN)
    og = v3(k.xT[:, :, :].rearrange("p k t -> p (k t)"), TILES, D)
    n_small = 16 * len(b.later)

    batches = [(q, z) for q in range(HEADS // 4) for z in range(2)]
    chunks = T // CH
    PREP, TILE_STEPS = 15, 4 + 4 * (len(STAGES) - 1) + 6
    LAST = TILE_STEPS - 6
    FINISH = 2 + 4 * (chunks - 2) + 2
    JOINT = FINISH + 4
    turn_tile = (k.turn_tile0, k.turn_tile1)

    def prep(eng, n, done):
        eng.wait_ge(k.turn_prep.sem, k.turn_prep.at(n * PREP + done))

    def prep_end(eng):
        eng.sem_inc(k.turn_prep.sem, 1)

    def joint(eng, n, done):
        eng.wait_ge(k.turn_joint.sem, k.turn_joint.at(n * JOINT + done))

    def joint_end(eng):
        eng.sem_inc(k.turn_joint.sem, 1)

    def tile_turn(eng, n, tile, done):
        eng.wait_ge(turn_tile[tile].sem, turn_tile[tile].at(n * TILE_STEPS + done))

    def tile_end(eng, tile):
        eng.sem_inc(turn_tile[tile].sem, 1)

    def of_batch(eng, sig, n):
        eng.wait_ge(sig.sem, sig.at(n + 1))

    def by_parity(ap):
        return ap.rearrange("p (h q n) -> p q h n", h=2, q=2)

    def features(q):
        return slice(q * FS, (q + 1) * FS)

    def finish_output(eng, link, n):
        q, z = batches[n]
        fs = features(q)
        joint(eng, n, FINISH + 3)
        yh = yb.rearrange("p t (h n) -> p (t h) n", n=HN)
        extra, gate = bhs[:, n % 2], gsbs[:, n % 2]
        row = lambda j: vecs[:, j:j + 1, fs].to_broadcast([P, TILES, FS])
        link(eng.tensor_tensor(yh, yh, var.rearrange("p (h a) -> p h a", a=1).to_broadcast([P, 8, HN]), MUL))
        link(eng.tensor_tensor(yb, yb, row(7), MUL))
        link(eng.tensor_tensor(yb, yb, row(8), ADD))
        link(eng.tensor_tensor(extra.rearrange("p t (h n) -> p t h n", n=HN),
                                b.v[:, :, fs].rearrange("p t (h n) -> p t h n", n=HN),
                                bonus[:, n % 3].rearrange("p (t h a) -> p t h a", t=TILES, a=1)
                                .to_broadcast([P, TILES, 4, HN]), MUL))
        link(eng.tensor_tensor(yb, yb, extra, ADD))
        if z == 0:
            link(eng.tensor_tensor(og[:, :, fs], gate, yb, MUL))
        else:
            link(eng.tensor_tensor(yb, gate, yb, MUL))
            link(eng.tensor_tensor(og[:, :, fs], og[:, :, fs], yb, ADD))
        joint_end(eng)

    with k.nc.Block() as block:
        @block.gpsimd
        def _(pool):
            for t in (btT, ktT):
                k.pool_chain.link(pool, pool.memset(t, 0.0))
            pool.sem_inc(k.pool_done.sem, 1)
            link = lambda ins: k.pool_chain.link(pool, ins)

            for n, (q, z) in enumerate(batches):
                for tile in range(TILES):
                    of_batch(pool, k.raw_copied[tile], n)
                    v = mq[:, tile].rearrange("p o w n -> p o (w n)")
                    link(pool.tensor_tensor(v, v, tri[:, z].rearrange("p w n -> p (w n)").rearrange("p (a m) -> p a m", a=1)
                                            .to_broadcast([P, 4, 2 * P]), MUL))
                    pool.sem_inc(k.masked[tile].sem, 1)
                if n:
                    finish_output(pool, link, n - 1)

        @block.tensor
        def _(pe):
            def prep_lora(n):
                q, z = batches[n]
                prep(pe, n, 1)
                for bank_, t1, t2 in ((3, b.tw, w2), (7, b.ta, a2)):
                    for tile in range(TILES):
                        mm = pe.matmul(k.ps[:, bank_, tile * FS:(tile + 1) * FS], t1[:, z, tile * P:(tile + 1) * P],
                                       t2[:, features(q)], start=True, stop=True)
                mm.then_inc(k.turn_prep.sem, 1)

            def prep_sums(n):
                prep(pe, n, 5)
                for tile in range(TILES):
                    pe.matmul(k.ps[:, 3, tile * FS:(tile + 1) * FS], tri[:, batches[n][1], 1], lw[:, tile], start=True, stop=True)
                    mm = pe.matmul(k.ps[:, 7, tile * FS:(tile + 1) * FS], blk, lw[:, tile], start=True, stop=True)
                mm.then_inc(k.turn_prep.sem, 1)

            def prep_totals(n):
                q, z = batches[n]
                prep(pe, n, 8)
                for hp in range(2):
                    for tile in range(TILES):
                        at = (hp * TILES + tile) * P
                        pe.matmul(k.ps[:, 3, at:at + P], lw[:, tile, hp * P:(hp + 1) * P], blk, start=True, stop=True)
                for tile in range(TILES):
                    mm = pe.matmul(k.ps[:, 7, tile * FS:(tile + 1) * FS], b.tg[:, z, tile * P:(tile + 1) * P],
                                   g2[:, z, features(q)], start=True, stop=True)
                mm.then_inc(k.turn_prep.sem, 1)

            def prep_transpose(n, turn, pair_):
                prep(pe, n, turn)
                for bank_, src in zip((3, 7), pair_):
                    for hp in range(2):
                        for tile in range(TILES):
                            at = (hp * TILES + tile) * P
                            mm = pe.transpose(k.ps[:, bank_, at:at + P], src[:, tile, hp * P:(hp + 1) * P], k.ident[:, :])
                mm.then_inc(k.turn_prep.sem, 1)

            def prep_at(n, step):
                if step == 8:
                    prep_lora(n)
                elif step == 12:
                    prep_sums(n)
                elif step == 16:
                    prep_totals(n)
                elif step == 20:
                    prep_transpose(n, 11, (at_, rt))
                elif step == 24:
                    prep_transpose(n, 13, (bt, kt))

            pe.wait_ge(k.small_landed.sem, k.small_landed.at(n_small))
            for step in (8, 12, 16, 20, 24):
                prep_at(0, step)
            for n, (q, z) in enumerate(batches):
                art, btT_, ktT_, aw = arts[:, n % 2], btT, ktT, aws[:, n % 2]
                bh, kh = bhs[:, n % 2], khs[:, n % 2]
                prep(pe, n + 1, 0)
                if n:
                    joint(pe, n - 1, FINISH)
                for step in range(0, TILE_STEPS, 2):
                    if n + 1 < len(batches):
                        prep_at(n + 1, step)
                    if step == TILE_STEPS - 2:
                        prep(pe, min(n + 2, len(batches)), 0)
                    for tile in range(TILES):
                        if step:
                            tile_turn(pe, n, tile, step)
                        if step == 4:
                            of_batch(pe, k.raw_copied[tile], n)
                        if step == LAST:
                            of_batch(pe, k.masked[tile], n)
                        pb = lambda i: k.ps[:, 4 * tile + i, :]
                        L, LT, QT = (lq[:, tile, :, w] for w in range(3))
                        MT, KT = (mq[:, tile, :, w] for w in range(2))
                        for o, (par, hp) in enumerate(ORDER):
                            half = slice(par * 64, par * 64 + 64)
                            v_pair = b.v[:, tile, q * FS + hp * P:q * FS + (hp + 1) * P]
                            if step == 0:
                                for m, side in enumerate((btT_, ktT_)):
                                    mm = pe.matmul(pb(2 * m + par)[:, hp * 256:(hp + 1) * 256], side[:, par, hp, tile],
                                                   art[:, hp, tile].rearrange("p w n -> p (w n)"),
                                                   start=True, stop=True)
                            elif step == 2:
                                mm = pe.matmul(pb(par)[:, hp * P:(hp + 1) * P], art[:, hp, tile, 0],
                                               btT_[:, par, hp, tile], start=True, stop=True)
                            elif step < LAST:
                                if step % 4 == 0:
                                    mm = pe.matmul(pb(2)[:, o * P:(o + 1) * P], LT[:, o], inv[:, tile, o, 0],
                                                   start=True, stop=True)
                                else:
                                    w = pb(o // 2)[:, (o % 2) * 256:(o % 2 + 1) * 256]
                                    if step < LAST - 2:
                                        pe.matmul(w[:, 0:P], inv[:, tile, o, 1], xb[:, tile, o], start=True, stop=True)
                                    mm = pe.matmul(w[:, P:2 * P], xb[:, tile, o], inv[:, tile, o, 1],
                                                   start=True, stop=True)
                            elif step == LAST:
                                mm = pe.matmul(pb(2)[:, o * P:(o + 1) * P], MT[:, o], v_pair, start=True, stop=True)
                            elif step == LAST + 2:
                                pe.matmul(pb(0)[:, o * P:(o + 1) * P], inv[:, tile, o, 1],
                                          aw[:, tile, o].rearrange("p w n -> p (w n)"), start=True, stop=True)
                                mm = pe.matmul(pb(1)[half, hp * P:(hp + 1) * P], aw[:, tile, o, 1 - par],
                                               inv[:, tile, o, 1], start=True, stop=True)
                            else:
                                pe.matmul(pb(2)[half, hp * P:(hp + 1) * P], gu[:, tile, o, (1 - par) * HN:(2 - par) * HN],
                                          QT[:, o], start=True, stop=True)
                                pe.matmul(pb(3)[:, o * P:(o + 1) * P], QT[:, o], gu[:, tile, o], start=True, stop=False)
                                mm = pe.matmul(pb(3)[:, o * P:(o + 1) * P], KT[:, o], v_pair, start=False, stop=True)
                        mm.then_inc(turn_tile[tile].sem, 1)

                at = 0
                for tile in range(TILES):
                    tile_turn(pe, n, tile, TILE_STEPS)
                for i, ch in enumerate(range(chunks) if z == 0 else reversed(range(chunks))):
                    tile, rows_ = ch // 2, slice((ch % 2) * CH, (ch % 2 + 1) * CH)
                    if i:
                        joint(pe, n, at)
                        for o, (par, hp) in enumerate(ORDER):
                            half = slice(par * 64, par * 64 + 64)
                            mm = pe.matmul(k.ps[rows_, 4 + par, hp * HN:(hp + 1) * HN], ght(tile, 1)[half, hp, rows_],
                                           st[half, hp], start=True, stop=True)
                            if i < chunks - 1:
                                mm = pe.matmul(k.ps[rows_, par, hp * HN:(hp + 1) * HN], ght(tile, 0)[half, hp, rows_],
                                               st[half, hp], start=True, stop=True)
                        mm.then_inc(k.turn_joint.sem, 1)
                        at += 2
                    if i < chunks - 1:
                        if i:
                            joint(pe, n, at)
                        for o, (par, hp) in enumerate(ORDER):
                            j = 2 * hp + par
                            half = slice(par * 64, par * 64 + 64)
                            u = us[rows_, o] if i else gu[rows_, tile, o, par * HN:(par + 1) * HN]
                            out = k.ps[half, 6, hp * HN:(hp + 1) * HN]
                            pe.matmul(out, bh[rows_, tile, j * HN:(j + 1) * HN], u, start=True, stop=False)
                            mm = pe.matmul(out, kh[rows_, tile, j * HN:(j + 1) * HN],
                                           b.v[rows_, tile, q * FS + j * HN:q * FS + (j + 1) * HN],
                                           start=False, stop=True)
                        mm.then_inc(k.turn_joint.sem, 1)
                        at += 2
                assert at == FINISH

        @block.scalar
        def _(act):
            mark = k.act_chain.mark
            ps3 = lambda i: v3(k.ps[:, i, :], TILES, FS)

            def done():
                act.wait_ge(k.act_chain.sem, k.act_chain.n)
                prep_end(act)

            def prepare(n):
                q, z = batches[n]
                if z == 0:
                    act.wait_ge(k.vec_done.sem, k.vec_done.at(q + 1))
                    act.activation(norms, norms, ACT.Sqrt).then_inc(k.act_done.sem, 1)
                prep(act, n, 3)
                mark(act.activation(lw, lw, ACT.Sigmoid))
                mark(act.activation(ar, ar, ACT.Sigmoid))
                done()
                prep(act, n, 6)
                mark(act.activation(cum, ps3(3), ACT.Copy))
                mark(act.activation(ein, ps3(3), ACT.Exp))
                mark(act.activation(eneg, ps3(3), ACT.Exp, scale=-1.0))
                done()
                prep(act, n, 9)
                if n >= 2:
                    joint(act, n - 2, JOINT)
                mark(act.activation(ex, ex, ACT.Exp))
                mark(act.activation(eh, eh, ACT.Exp))
                mark(act.activation(pcs[:, n % 2], k.ps[:, 3, 0:HALF:CH], ACT.Exp))
                mark(act.activation(gsbs[:, n % 2], ps3(7), ACT.Copy))
                done()
                prep(act, n, 12)
                for m in range(2):
                    mark(act.activation(arts[:, n % 2, :, :, m], k.ps[:, (3, 7)[m], :].rearrange("p (h t n) -> p h t n", h=2, t=TILES),
                                        ACT.Copy))
                for par in range(2):
                    for tile in range(TILES):
                        mark(act.activation(aws[:, n % 2, tile, 2 * par:2 * par + 2, 1 - par],
                                            by_parity(at_[:, tile])[:, par], ACT.Copy))
                done()
                prep(act, n, 14)
                act.wait_ge(k.pool_done.sem, k.pool_done.at(1))
                for m, dst in enumerate((btT, ktT)):
                    for par in range(2):
                        half = slice(par * 64, par * 64 + 64)
                        mark(act.activation(dst[half, par], k.ps[half, (3, 7)[m], :].rearrange("p (h t n) -> p h t n", h=2, t=TILES),
                                            ACT.Copy))
                done()

            def finish_roots(n):
                joint(act, n, FINISH + 1)
                act.activation(var, var, ACT.Sqrt).then_inc(k.turn_joint.sem, 1)

            prepare(0)
            for n in range(len(batches)):
                for tile in range(TILES):
                    tile_turn(act, n, tile, 1)
                    act.activation(mq[:, tile].rearrange("p o w n -> p (o w n)"), bank(k, 4 * tile + 2, 2),
                                   ACT.Copy).then_inc(k.raw_copied[tile].sem, 1)
                if n:
                    finish_roots(n - 1)
                if n + 1 < len(batches):
                    prepare(n + 1)
            finish_roots(len(batches) - 1)

        @block.vector
        def _(vec):
            link = lambda ins: k.vec_chain.link(vec, ins)
            mark = k.vec_chain.mark

            def settle():
                vec.wait_ge(k.vec_chain.sem, k.vec_chain.n)

            def done():
                settle()
                joint_end(vec)

            def bc_tiles(j, fs):
                return vecs[:, j:j + 1, fs].to_broadcast([P, TILES, FS])

            def per_head(ap):
                return ap.rearrange("p t (h n) -> p (t h) n", n=HN)

            def bc_head(cols):
                return cols.rearrange("p (h a) -> p h a", a=1).to_broadcast([P, 8, HN])

            ps3 = lambda i: v3(k.ps[:, i, :], TILES, FS)

            def prep_keys(n):
                q, z = batches[n]
                if z == 0:
                    fs = features(q)
                    link(vec.tensor_tensor(kk, b.k[:, :, fs], bc_tiles(4, fs), MUL))
                    link(vec.tensor_tensor(ex, kk, kk, MUL))
                    link(vec.tensor_reduce(norms, per_head(ex), X, ADD))
                    vec.sem_inc(k.vec_done.sem, 1)
                    vec.wait_ge(k.act_done.sem, k.act_done.at(q + 1))
                    link(vec.tensor_scalar(norms, norms, 1e-12, None, MAX))
                    link(vec.reciprocal(norms, norms))
                    link(vec.tensor_tensor(per_head(kk), per_head(kk), bc_head(norms), MUL))
                prep_end(vec)

            def prep_bias(n):
                q, z = batches[n]
                prep(vec, n, 2)
                mark(vec.tensor_tensor(lw, ps3(3), bc_tiles(2 * z, features(q)), ADD))
                mark(vec.tensor_tensor(ar, ps3(7), bc_tiles(2 * z + 1, features(q)), ADD))
                settle()
                prep_end(vec)

            def prep_decay(n):
                q, z = batches[n]
                fs = features(q)
                prep(vec, n, 4)
                mark(vec.tensor_scalar(lw, lw, -math.exp(-0.5), None, MUL))
                link(vec.tensor_tensor(bd, kk, ar, MUL))
                prep_end(vec)
                link(vec.scalar_tensor_tensor(out=kd, in0=ar, scalar=-1.0, in1=bc_tiles(5, fs), op0=ADD, op1=MUL))
                link(vec.scalar_tensor_tensor(out=kd, in0=kd, scalar=1.0, in1=b.k[:, :, fs], op0=ADD, op1=MUL))

            def prep_bonus(n):
                fs = features(batches[n][0])
                link(vec.tensor_tensor(ex, b.r[:, :, fs], kd, MUL))
                link(vec.tensor_tensor(ex, ex, bc_tiles(6, fs), MUL))
                link(vec.tensor_reduce(bonus[:, n % 3], per_head(ex), X, ADD))

            def prep_remain(n):
                prep(vec, n, 7)
                mark(vec.tensor_tensor(ex, cum, lw, SUB))
                mark(vec.tensor_tensor(eh, ps3(7), cum, SUB))
                settle()
                prep_end(vec)

            def prep_factors(n):
                prep(vec, n, 10)
                mark(vec.scalar_tensor_tensor(out=at_, in0=kk, scalar=-1.0, in1=ex, op0=MUL, op1=MUL))
                mark(vec.tensor_tensor(rt, b.r[:, :, features(batches[n][0])], ein, MUL))
                mark(vec.tensor_tensor(bt, bd, eneg, MUL))
                link(vec.tensor_tensor(kt, kd, eneg, MUL))
                prep_end(vec)

            def prep_rest(n):
                if n >= 2:
                    joint(vec, n - 2, JOINT)
                mark(vec.tensor_tensor(bhs[:, n % 2], bd, eh, MUL))
                mark(vec.tensor_tensor(khs[:, n % 2], kd, eh, MUL))

            def prep_at(n, step):
                if step == 5:
                    prep_keys(n)
                elif step == 7:
                    prep_bias(n)
                elif step == 9:
                    prep_decay(n)
                elif step == 11:
                    prep_bonus(n)
                elif step == 13:
                    prep_remain(n)
                elif step == 17:
                    prep_factors(n)
                elif step == 19:
                    prep_rest(n)

            def finish_sums(n):
                yh, eh_ = per_head(yb), per_head(ex)
                link(vec.tensor_reduce(mean, yh, X, ADD))
                link(vec.tensor_scalar(mean, mean, 1.0 / HN, None, MUL))
                link(vec.tensor_tensor(yh, yh, bc_head(mean), SUB))
                link(vec.tensor_tensor(eh_, yh, yh, MUL))
                link(vec.tensor_reduce(var, eh_, X, ADD))
                link(vec.tensor_scalar(var, var, 1.0 / HN, GN_EPS, MUL, ADD))
                joint_end(vec)

            def finish_scale(n):
                joint(vec, n, FINISH + 2)
                link(vec.reciprocal(var, var))
                joint_end(vec)

            def add_identity(tile, w):
                v = inv[:, tile, :, w]
                link(vec.tensor_tensor(v, v, v3(k.ident[:, :], 1, P).to_broadcast([P, 4, P]), ADD))

            vec.wait_ge(k.small_landed.sem, k.small_landed.at(n_small))
            for step in (5, 7, 9, 11, 13, 17, 19):
                prep_at(0, step)
            for n, (q, z) in enumerate(batches):
                fs = features(q)
                art, aw, pc = arts[:, n % 2], aws[:, n % 2], pcs[:, n % 2]
                for step in range(1, TILE_STEPS, 2):
                    for tile in range(TILES):
                        tile_turn(vec, n, tile, step)
                        b0 = 4 * tile
                        inv_t = inv[:, tile].rearrange("p o w n -> p (o w n)")
                        if step == 1:
                            link(vec.tensor_tensor(
                                lq[:, tile, :, 1:3].rearrange("p o w n -> p o (w n)"), v3(bank(k, b0, 2), 4, 2 * P),
                                tri[:, z].rearrange("p w n -> p (w n)").rearrange("p (a m) -> p a m", a=1)
                                .to_broadcast([P, 4, 2 * P]), MUL))
                        elif step == 3:
                            for par in range(2):
                                mark(vec.tensor_tensor(inv[:, tile, 2 * par:2 * par + 2, 0], v3(k.ps[:, b0 + par, 0:256], 2, P),
                                                       stage[:, z, 0:1].to_broadcast([P, 2, P]), MUL))
                            settle()
                            add_identity(tile, 0)
                        elif step < LAST:
                            if step % 4 == 1:
                                i = (step - 1) // 4
                                link(vec.tensor_tensor(xb[:, tile], v3(k.ps[:, b0 + 2, :], 4, P),
                                                       stage[:, z, i:i + 1].to_broadcast([P, 4, P]), MUL))
                            elif step < LAST - 1:
                                link(vec.tensor_tensor(inv_t, inv_t, bank(k, b0, 2), ADD))
                            else:
                                link(vec.tensor_tensor(inv[:, tile, :, 1], inv[:, tile, :, 1],
                                                       v3(bank(k, b0, 2), 4, 2 * P)[:, :, P:2 * P], ADD))
                        elif step == LAST + 1:
                            for par in range(2):
                                o = slice(2 * par, 2 * par + 2)
                                mark(vec.tensor_copy(aw[:, tile, o, par],
                                                     v3(k.ps[:, b0 + 2, :], 4, P)[:, o, par * HN:(par + 1) * HN]))
                            settle()
                        elif step == LAST + 3:
                            mark(vec.tensor_copy(gu[:, tile], v3(k.ps[:, b0, :], 4, P)))
                            mark(vec.tensor_copy(ght(tile, 0), v3(k.ps[:, b0 + 1, 0:256], 2, P)))
                            settle()
                        else:
                            if n:
                                joint(vec, n - 1, JOINT)
                            mark(vec.tensor_tensor(ght(tile, 1), v3(k.ps[:, b0 + 2, 0:256], 2, P), art[:, :, tile, 1], ADD))
                            for par in range(2):
                                mark(vec.tensor_copy(by_parity(yb[:, tile])[:, par],
                                                     v3(k.ps[:, b0 + 3, par * 256:(par + 1) * 256], 2, P)[:, :, par * HN:(par + 1) * HN]))
                            settle()
                        tile_end(vec, tile)
                    if step == 1:
                        for tile in range(TILES):
                            link(vec.tensor_tensor(inv[:, tile, :, 1], lq[:, tile, :, 1],
                                                   stage[:, 1 - z, 0:1].to_broadcast([P, 4, P]), MUL))
                            add_identity(tile, 1)
                    if n and step == 3:
                        finish_sums(n - 1)
                    if n and step == 5:
                        finish_scale(n - 1)
                    if n + 1 < len(batches):
                        prep_at(n + 1, step)

                at = 0
                for i, ch in enumerate(range(chunks) if z == 0 else reversed(range(chunks))):
                    tile, rows_ = ch // 2, slice((ch % 2) * CH, (ch % 2 + 1) * CH)
                    if i:
                        joint(vec, n, at + 1)
                        if i < chunks - 1:
                            for par in range(2):
                                o = slice(2 * par, 2 * par + 2)
                                mark(vec.tensor_tensor(us[rows_, o], v3(k.ps[rows_, par, 0:P], 2, HN),
                                                       gu[rows_, tile, o, par * HN:(par + 1) * HN], ADD))
                            settle()
                        else:
                            y_ = by_parity(yb[rows_, tile])
                            link(vec.tensor_tensor(y_, k.ps[rows_, 4:6, 0:P].rearrange("p q (h n) -> p q h n", h=2), y_, ADD))
                        joint_end(vec)
                        at += 2
                    if i < chunks - 1:
                        if i:
                            y_ = by_parity(yb[rows_, tile])
                            mark(vec.tensor_tensor(y_, k.ps[rows_, 4:6, 0:P].rearrange("p q (h n) -> p q h n", h=2), y_, ADD))
                        joint(vec, n, at + 1)
                        for hp in range(2):
                            new = k.ps[:, 6, hp * HN:(hp + 1) * HN]
                            if i == 0:
                                mark(vec.tensor_copy(st[:, hp], new))
                            else:
                                col = hp * 4 + ch
                                mark(vec.scalar_tensor_tensor(out=st[:, hp], in0=st[:, hp], scalar=pc[:, col:col + 1],
                                                              in1=new, op0=MUL, op1=ADD))
                        done()
                        at += 2
            finish_sums(len(batches) - 1)
            finish_scale(len(batches) - 1)
            finish_output(vec, link, len(batches) - 1)
    k.small_landed.close(n_small)
    k.pool_done.close(1)
    k.vec_done.close(HEADS // 4)
    k.act_done.close(HEADS // 4)
    k.turn_prep.close(len(batches) * PREP)
    k.turn_joint.close(len(batches) * JOINT)
    for sig in turn_tile:
        sig.close(len(batches) * TILE_STEPS)
    for sig in k.raw_copied + k.masked:
        sig.close(len(batches))
    return og


def router_loads(k, i):
    a = k.a
    NR = N_GROUPS + EXPERTS
    rw, rb = k.router[:, :, :], k.router_bias[:, :]
    small = []
    if i < DEPTH:
        small.append((rw[:, :, 0:N_GROUPS], a["moe_router_g"][i].rearrange("(p k) g -> p k g", k=K8)))
        small.append((rb[:, 0:N_GROUPS], a["moe_router_g_b"][i].partition_broadcast(P)))
        for g in range(N_GROUPS):
            at = N_GROUPS + g * PER_GROUP
            small.append((rw[:, :, at:at + PER_GROUP], a["moe_router_e"][i, g].rearrange("(p k) e -> p k e", k=K8)))
            small.append((rb[:, at:at + PER_GROUP], a["moe_router_e_b"][i, g].partition_broadcast(P)))
    else:
        j = i - DEPTH
        small.append((rw[:, :, 0:N_GROUPS], a["w_route_group_2"][j].rearrange("(p k) g -> p k g", k=K8)))
        small.append((rb[:, 0:N_GROUPS], a["b_route_group_2"][j].partition_broadcast(P)))
        small.append((rw[:, :, N_GROUPS:NR], a["w_route_expert_2"][j].rearrange("(p k) e -> p k e", k=K8)))
        small.append((rb[:, N_GROUPS:NR], a["b_route_expert_2"][j].partition_broadcast(P)))
    return small


def load_router(k, eng, i):
    if i < 2 * DEPTH:
        for dst, src in router_loads(k, i):
            eng.dma_start(dst, src).then_inc(k.router_landed.sem, 16)


def route_phase(k, i, end):
    a = k.a
    first = i < DEPTH
    NR = N_GROUPS + EXPERTS
    c = Carver(k.region, k.region_w)
    k.key, k.gate = (c.take(TILES * EXPERTS).rearrange("p (q t w) -> p q t w", q=PAIRS, t=TILES) for _ in range(2))
    k.over = v3(c.take(TILES * EXPERTS), EXPERTS, TILES)
    k.count = c.take(1).bitcast(I32)
    k.slot_ids = c.take(CAP)
    k.xm = c.take(TILES * D).rearrange("p (t s m) -> p t s m", t=TILES, s=K8)
    k.moe_end = c.at
    before, ones = c.take(P), c.take(P)
    chosen, rank = (v3(c.take(TILES * EXPERTS), TILES, EXPERTS) for _ in range(2))
    peak = c.take(1)
    ids = c.take(CAP).bitcast(I32)
    lg = v3(c.take(TILES * NR), TILES, NR)
    gates = c.take(TILES * EXPERTS).rearrange("p (t g e) -> p t g e", t=TILES, g=N_GROUPS)
    tmp4 = c.take(TILES * EXPERTS).rearrange("p (t g e) -> p t g e", t=TILES, g=N_GROUPS)
    ohg, eg, s4 = (v3(c.take(TILES * N_GROUPS), TILES, N_GROUPS) for _ in range(3))
    sel, oh1, oh2, s8, e2 = (v3(c.take(TILES * PER_GROUP), TILES, PER_GROUP) for _ in range(5))
    cols = v3(c.take(8 * TILES), 8, TILES)
    m0, mm, pg, m1, m2, ex, w1, w2 = (cols[:, j, :] for j in range(8))
    rw, rb = k.router[:, :, :], k.router_bias[:, :]
    n_small = 16 * len(router_loads(k, i))

    def last(col, n):
        return col.rearrange("p (t a) -> p t a", a=1).to_broadcast([P, TILES, n])

    with k.nc.Block() as block:
        @block.sync
        def _(sp):
            ahead(k, sp, end)

        @block.tensor
        def _(pe):
            pe.wait_ge(k.router_landed.sem, k.router_landed.at(n_small))
            for tile in range(TILES):
                for s in range(K8):
                    mm_ = pe.matmul(k.ps[:, tile, 0:NR], k.xT[:, s, tile * P:(tile + 1) * P], rw[:, s],
                                    start=(s == 0), stop=(s == K8 - 1))
            mm_.then_inc(k.pe_done.sem, 1)
            if first:
                for tile in range(TILES):
                    for s in range(K8):
                        mm_ = pe.transpose(k.ps[:, 4 + 2 * tile + s // 4, (s % 4) * P:(s % 4 + 1) * P],
                                           k.xT[:, s, tile * P:(tile + 1) * P], k.ident[:, :])
                mm_.then_inc(k.pe_done.sem, 1)
            pe.wait_ge(k.vec_done.sem, k.vec_done.at(3))
            pe.wait_ge(k.pool_done.sem, k.pool_done.at(1))
            for n, terms in enumerate((((before, 0),), ((ones, 0), (before, 1)), ((ones, 0), (ones, 1)))):
                for m, (w, tile) in enumerate(terms):
                    mm_ = pe.matmul(k.ps[:, 3, n * EXPERTS:(n + 1) * EXPERTS], w, chosen[:, tile], start=(m == 0),
                                    stop=(m == len(terms) - 1))
            mm_.then_inc(k.pe_done.sem, 1)

        @block.scalar
        def _(act):
            act.wait_ge(k.vec_done.sem, k.vec_done.at(1))
            act.activation(eg, eg, ACT.Exp).then_inc(k.act_done.sem, 1)
            act.wait_ge(k.vec_done.sem, k.vec_done.at(2))
            act.activation(ex, ex, ACT.Exp).then_inc(k.act_done.sem, 1)
            if first:
                act.wait_ge(k.pe_done.sem, k.pe_done.at(2))
                act.activation(k.xm.rearrange("p t s m -> p (t s m)"), bank(k, 4, 4), ACT.Copy).then_inc(k.act_done.sem, 1)

        @block.gpsimd
        def _(pool):
            link = lambda ins: k.pool_chain.link(pool, ins)
            link(pool.memset(ones, 1.0))
            link(pool.memset(before, 1.0))
            link(pool.affine_select(out=before, in_=before, pattern=[[1, P]], compare_op=ALU.is_ge, fill=0.0, base=-1,
                                    channel_multiplier=-1))
            link(pool.iota(ids, pattern=[[1, CAP]], base=0, channel_multiplier=0))
            pool.sem_inc(k.pool_done.sem, 1)

        @block.vector
        def _(vec):
            link = lambda ins: k.vec_chain.link(vec, ins)

            def first_best(values, best, onehot, scratch, n):
                link(vec.tensor_reduce(best, values, X, MAX))
                link(vec.tensor_tensor(scratch, values, last(best, n), ALU.is_equal))
                link(vec.tensor_tensor(scratch, scratch, v3(k.desc[:, 0:n], 1, n).to_broadcast([P, TILES, n]), MUL))
                link(vec.tensor_reduce(mm, scratch, X, MAX))
                link(vec.tensor_tensor(onehot, scratch, last(mm, n), ALU.is_equal))

            vec.wait_ge(k.pe_done.sem, k.pe_done.at(1))
            vec.wait_ge(k.router_landed.sem, k.router_landed.at(n_small))
            link(vec.tensor_tensor(lg, k.ps[:, 0:TILES, 0:NR], v3(rb, 1, NR).to_broadcast([P, TILES, NR]), ADD))
            lgg = lg[:, :, 0:N_GROUPS]
            first_best(lgg, m0, ohg, s4, N_GROUPS)
            link(vec.tensor_tensor(eg, lgg, last(m0, N_GROUPS), SUB))
            vec.sem_inc(k.vec_done.sem, 1)
            link(vec.tensor_tensor(tmp4, lg[:, :, N_GROUPS:NR].rearrange("p t (g e) -> p t g e", g=N_GROUPS),
                                   ohg.rearrange("p t (g a) -> p t g a", a=1).to_broadcast([P, TILES, N_GROUPS, PER_GROUP]), MUL))
            link(vec.tensor_reduce(sel, tmp4.rearrange("p t g e -> p t e g"), X, ADD))
            first_best(sel, m1, oh1, s8, PER_GROUP)
            link(vec.scalar_tensor_tensor(out=e2, in0=oh1, scalar=-BIG, in1=sel, op0=MUL, op1=ADD))
            first_best(e2, m2, oh2, s8, PER_GROUP)
            link(vec.tensor_tensor(ex, m2, m1, SUB))
            vec.sem_inc(k.vec_done.sem, 1)
            vec.wait_ge(k.act_done.sem, k.act_done.at(1))
            link(vec.tensor_reduce(pg, eg, X, ADD))
            link(vec.reciprocal(pg, pg))
            vec.wait_ge(k.act_done.sem, k.act_done.at(2))
            link(vec.tensor_scalar(w1, ex, 1.0, None, ADD))
            link(vec.reciprocal(w1, w1))
            link(vec.tensor_tensor(w1, w1, pg, MUL))
            link(vec.tensor_tensor(w2, w1, ex, MUL))
            group = ohg.rearrange("p t (g a) -> p t g a", a=1)
            link(vec.tensor_tensor(s8, oh1, oh2, ADD))
            for tile in range(TILES):
                link(vec.tensor_tensor(v3(chosen[:, tile], N_GROUPS, PER_GROUP), group[:, tile].to_broadcast([P, N_GROUPS, PER_GROUP]),
                                       s8[:, tile:tile + 1].to_broadcast([P, N_GROUPS, PER_GROUP]), MUL))
            vec.sem_inc(k.vec_done.sem, 1)
            link(vec.tensor_tensor(oh1, oh1, last(w1, PER_GROUP), MUL))
            link(vec.tensor_tensor(oh2, oh2, last(w2, PER_GROUP), MUL))
            link(vec.tensor_tensor(oh1, oh1, oh2, ADD))
            for tile in range(TILES):
                link(vec.tensor_tensor(gates[:, tile], group[:, tile].to_broadcast([P, N_GROUPS, PER_GROUP]),
                                       oh1[:, tile:tile + 1].to_broadcast([P, N_GROUPS, PER_GROUP]), MUL))
            flat = gates.rearrange("p t g e -> p t (g e)")
            paired = lambda ap: ap.rearrange("p t (q w) -> p q t w", w=2)
            link(vec.tensor_copy(k.gate, paired(flat)))
            vec.wait_ge(k.pool_done.sem, k.pool_done.at(1))
            link(vec.tensor_copy(k.slot_ids, ids))
            n = 3 if first else 2
            vec.wait_ge(k.pe_done.sem, k.pe_done.at(n))
            link(vec.tensor_copy(rank, v3(k.ps[:, 3, 0:TILES * EXPERTS], TILES, EXPERTS)))
            link(vec.tensor_reduce(peak, k.ps[:, 3, TILES * EXPERTS:(TILES + 1) * EXPERTS], X, MAX))
            link(vec.tensor_copy(k.count, peak))
            link(vec.scalar_tensor_tensor(out=k.over.rearrange("p e t -> p t e"), in0=rank, scalar=float(CAP), in1=flat,
                                          op0=ALU.is_ge, op1=MUL))
            link(vec.tensor_scalar(chosen, chosen, -FAR, FAR, MUL, ADD))
            link(vec.tensor_tensor(k.key, paired(rank), paired(chosen), ADD))
    k.router_landed.close(n_small)
    k.pe_done.close(3 if first else 2)
    k.vec_done.close(3)
    k.act_done.close(3 if first else 2)
    k.pool_done.close(1)


def experts_phase(k, i):
    a = k.a
    j = i % DEPTH
    wg, wu, wd = ((a["moe_w_gate"], a["moe_w_up"], a["moe_w_down"]) if i < DEPTH else
                  (a["w_exp_gate_2"], a["w_exp_up_2"], a["w_exp_down_2"]))
    wg = wg[j].rearrange("g e (p k) f -> (g e) p (k f)", k=K8)
    wu = wu[j].rearrange("g e (p k) f -> (g e) p (k f)", k=K8)
    wd = wd[j].rearrange("g e (p r) n -> (g e) p (r n)", r=2)
    n0 = k.starts[f"moe{i}"]
    passes = (PAIRS - UNROLL) // UNROLL
    c = Carver(k.region, k.region_w, k.moe_end)
    zeros = c.take(HALF)
    slots, gated = (c.take(TILES * P).rearrange("p (t w n) -> p t w n", t=TILES, w=2) for _ in range(2))
    gatedT = v3(c.take(2 * T), 2, T)
    xe = v3(c.take(K8 * P), K8, P)
    silu_out, hid = c.take(F), c.take(F)
    hidT = v3(c.take(2 * P), 2, P)
    out = c.take(D)
    over_w = v3(c.take(3 * SLOT), 3, SLOT)
    over_silu, over_hid, over_hidT = (v3(c.take(TILES * F), TILES, F) for _ in range(3))
    landed_, turn_ = k.over_landed[i], k.over_turn[i]
    OVER_STEPS = 7
    gate_at = lambda q: 6 * q - 2 if q else 0
    down_at = lambda q: min(6 * q + 8, 3 * EXPERTS - 2)
    assert k.issued >= n0 + SLOTS, "the first units are loaded ahead"

    def slot(n, width=1):
        at = ((n0 + n) % SLOTS) * SLOT
        return k.arena[:, at:at + width * SLOT]

    def wait_slot(eng, n, p):
        eng.wait_ge(k.landed[(n0 + n) % SLOTS], 16 * ((n0 + n) // SLOTS + 1) + 16 * p)

    def wait_pair(eng, sig, q, p):
        eng.wait_ge(sig.sem, sig.at(q + 1) + UNROLL * p)

    def column(v, q, p):
        one = v[:, q] if isinstance(p, int) else v[:, bass.ds(p * UNROLL + q, 1)].rearrange("p a t w -> p (a t) w")
        return one.rearrange("p t (w n) -> p t w n", n=1).to_broadcast([P, TILES, 2, CAP])

    def overflow(eng, body):
        count = eng.value_load(k.count[0:1, 0:1], min_val=0, max_val=T)
        with eng.If(count > CAP):
            with eng.Fori(0, EXPERTS) as e:
                body(e)

    with k.nc.Block() as block:
        @block.sync
        def _(sp):
            def general(e):
                sp.wait_ge(turn_, OVER_STEPS * e + 1)
                for m, w in enumerate((wg, wu, wd)):
                    sp.dma_start(over_w[:, m], w[bass.ds(e, 1)].rearrange("a p n -> p (a n)")).then_inc(landed_, 16)

            def load(n, p, src):
                sp.wait_ge(k.used, n0 + n + 1 - SLOTS + SLOTS * p)
                sp.dma_start(slot(n), src).then_inc(k.landed[(n0 + n) % SLOTS], 16)

            load_router(k, sp, i + 1)
            overflow(sp, general)
            issue(k, sp, n0 + 4 + SLOTS)
            with sp.Fori(1, passes) as p:
                for s in range(UNROLL):
                    one = lambda w, e: w[bass.ds(p * 2 * UNROLL + e, 1)].rearrange("a p n -> p (a n)")
                    for e in range(2):
                        load(gate_at(s + 1) + 2 * e, p, one(wg, 2 * s + 2 + e))
                        load(gate_at(s + 1) + 2 * e + 1, p, one(wu, 2 * s + 2 + e))
                    for e in range(2):
                        load(down_at(s) + e, p, one(wd, 2 * s + e))
            k.issued = n0 + 4 + SLOTS * passes
            ahead(k, sp, n0 + 3 * EXPERTS)

        @block.tensor
        def _(pe):
            def general(e):
                pe.wait_ge(landed_, 48 * e + 48)
                pe.wait_ge(turn_, OVER_STEPS * e + 1)
                for m in range(2):
                    w = v3(over_w[:, m], K8, F)
                    for tile in range(TILES):
                        for s in range(K8):
                            mm = pe.matmul(k.ps[:, 4 + m, tile * F:(tile + 1) * F], k.xT[:, s, tile * P:(tile + 1) * P],
                                           w[:, s], start=(s == 0), stop=(s == K8 - 1))
                mm.then_inc(turn_, 1)
                pe.wait_ge(turn_, OVER_STEPS * e + 5)
                for tile in range(TILES):
                    for r in range(2):
                        mm = pe.transpose(k.ps[:, 6, r * T + tile * P:r * T + (tile + 1) * P], over_hid[:, tile, r:F:2],
                                          k.ident[:, :])
                mm.then_inc(turn_, 1)
                pe.wait_ge(turn_, OVER_STEPS * e + 7)
                w = v3(over_w[:, 2], 2, D)
                for r in range(2):
                    for tile in range(TILES):
                        for h in range(2):
                            mm = pe.matmul(k.ps[:, 2 * tile + h, :], over_hidT[:, r, tile * P:(tile + 1) * P],
                                           w[:, r, h * HALF:(h + 1) * HALF], start=False, stop=True, skip_group_check=True)
                mm.then_inc(turn_, 1)

            def gather(q, p):
                wait_pair(pe, k.slots_built, q, p)
                for s in range(K8):
                    for tile in range(TILES):
                        tokens = k.xm[:, tile, s] if i < DEPTH else k.x[:, tile, s:D:K8]
                        mm = pe.matmul(k.ps[:, 4 + s // 4, (s % 4) * P:(s % 4 + 1) * P], tokens,
                                       slots[:, tile].rearrange("p w n -> p (w n)"), start=(tile == 0), stop=(tile == 1))
                mm.then_inc(k.gathered.sem, 1)

            def turn(q, p, hidden, slots_):
                if hidden:
                    wait_pair(pe, k.hidden_ready, q, p)
                    for r in range(2):
                        mm = pe.transpose(k.ps[:, 7, r * P:(r + 1) * P], hid[:, r:F:2], k.ident[:, :])
                if slots_:
                    wait_pair(pe, k.gated_built, q + 1, p)
                    if q >= 0:
                        wait_pair(pe, k.gated_moved, q, p)
                    for tile in range(TILES):
                        mm = pe.transpose(k.ps[:, 7, T + tile * P:T + (tile + 1) * P],
                                          gated[:, tile].rearrange("p w n -> p (w n)"), k.ident[:, :])
                mm.then_inc(k.turned.sem, 1)

            def first_layer(q, p):
                wait_pair(pe, k.tokens_half0, q, p)
                wait_pair(pe, k.tokens_half1, q, p)
                for m in range(4):
                    wait_slot(pe, gate_at(q) + m, p)
                for s in range(K8):
                    for e in range(2):
                        w = v3(slot(gate_at(q) + 2 * e, 2), 2, SLOT)[:, :, s * F:(s + 1) * F]
                        mm = pe.matmul(v3(k.ps[e * CAP:(e + 1) * CAP, 6, :], 2, F), xe[:, s, e * CAP:(e + 1) * CAP], w,
                                       start=(s == 0), stop=(s == K8 - 1), skip_group_check=True)
                        if s == K8 - 1:
                            mm.then_inc(k.used, 2)

            def second_layer(q, p):
                wait_pair(pe, k.hidden_moved, q, p)
                for m in range(2):
                    wait_slot(pe, down_at(q) + m, p)
                for h in range(2):
                    for r in range(2):
                        for e in range(2):
                            w = v3(slot(down_at(q) + e), 2, D)
                            mm = pe.matmul(k.ps[e * CAP:(e + 1) * CAP, 4 + h, :], hidT[:, r, e * CAP:(e + 1) * CAP],
                                           w[:, r, h * HALF:(h + 1) * HALF], start=(r == 0), stop=(r == 1),
                                           skip_group_check=True)
                            if h and r:
                                mm.then_inc(k.used, 1)
                    if h == 0:
                        mm.then_inc(k.out_half.sem, 1)

            def scatter(q, p):
                for h, moved in enumerate((k.out_moved0, k.out_moved1)):
                    wait_pair(pe, moved, q, p)
                    for tile in range(TILES):
                        pe.matmul(k.ps[:, 2 * tile + h, :], gatedT[:, q % 2, tile * P:(tile + 1) * P],
                                  out[:, h * HALF:(h + 1) * HALF], start=False, stop=True, skip_group_check=True)

            pe.wait_ge(k.pool_done.sem, k.pool_done.at(1))
            for b in range(4):
                pe.matmul(k.ps[:, b, :], zeros[:, 0:P], zeros, start=True, stop=True)
            overflow(pe, general)
            gather(0, 0)
            turn(-1, 0, False, True)
            first_layer(0, 0)

            def pair(q, p, more):
                if more:
                    gather(q + 1, p)
                turn(q, p, True, more)
                if more:
                    first_layer(q + 1, p)
                second_layer(q, p)
                scatter(q, p)

            with pe.Fori(0, passes) as p:
                for s in range(UNROLL):
                    pair(s, p, True)
            for q in range(PAIRS - UNROLL, PAIRS):
                pair(q, 0, q + 1 < PAIRS)
            pe.transpose(k.ps[:, 7, 0:P], k.ident[:, :], k.ident[:, :]).then_inc(k.pe_done.sem, 1)

        @block.scalar
        def _(act):
            def general(e):
                act.wait_ge(turn_, OVER_STEPS * e + 2)
                act.activation(over_silu, v3(k.ps[:, 4, :], TILES, F), ACT.Silu).then_inc(turn_, 1)

            def move_tokens(q, p):
                wait_pair(act, k.gathered, q, p)
                act.activation(xe[:, 0:4].rearrange("p s n -> p (s n)"), k.ps[:, 4, :], ACT.Copy).then_inc(k.tokens_half0.sem, 1)

            def pair(q, p, more):
                act.wait_ge(k.used, n0 + gate_at(q) + 4 + SLOTS * p)
                act.activation(silu_out, k.ps[:, 6, 0:F], ACT.Silu).then_inc(k.silu_ready.sem, 1)
                if more:
                    move_tokens(q + 1, p)
                wait_pair(act, k.out_half, q, p)
                act.activation(out[:, 0:HALF], k.ps[:, 4, :], ACT.Copy).then_inc(k.out_moved0.sem, 1)

            overflow(act, general)
            move_tokens(0, 0)
            with act.Fori(0, passes) as p:
                for s in range(UNROLL):
                    pair(s, p, True)
            for q in range(PAIRS - UNROLL, PAIRS):
                pair(q, 0, q + 1 < PAIRS)

        @block.vector
        def _(vec):
            def general(e):
                vec.wait_ge(turn_, OVER_STEPS * e + 3)
                vec.tensor_tensor(over_hid, v3(k.ps[:, 5, :], TILES, F), over_silu, MUL).then_inc(turn_, 1)
                vec.wait_ge(turn_, OVER_STEPS * e + 4)
                gate = k.over[:, bass.ds(e, 1)].rearrange("p a (t n) -> p (a t) n", n=1)
                vec.tensor_tensor(over_hid, over_hid, gate.to_broadcast([P, TILES, F]), MUL).then_inc(turn_, 1)
                vec.wait_ge(turn_, OVER_STEPS * e + 6)
                vec.tensor_copy(over_hidT, v3(k.ps[:, 6, :], 2, T)).then_inc(turn_, 1)

            def build(q, p):
                ids = k.slot_ids.rearrange("p (a b n) -> p a b n", a=1, b=1).to_broadcast([P, TILES, 2, CAP])
                vec.tensor_tensor(slots, ids, column(k.key, q, p), ALU.is_equal).then_inc(k.slots_built.sem, 1)
                wait_pair(vec, k.slots_built, q, p)
                vec.tensor_tensor(gated, slots, column(k.gate, q, p), MUL).then_inc(k.gated_built.sem, 1)

            def move_tokens(q, p):
                wait_pair(vec, k.gathered, q, p)
                vec.tensor_copy(xe[:, 4:8].rearrange("p s n -> p (s n)"), k.ps[:, 5, :]).then_inc(k.tokens_half1.sem, 1)

            def move_gated(q, p):
                wait_pair(vec, k.turned, q, p)
                vec.tensor_copy(gatedT[:, q % 2], k.ps[:, 7, T:2 * T]).then_inc(k.gated_moved.sem, 1)

            def pair(q, p, left):
                wait_pair(vec, k.silu_ready, q, p)
                vec.tensor_tensor(hid, k.ps[:, 6, F:2 * F], silu_out, MUL).then_inc(k.hidden_ready.sem, 1)
                if left > 1:
                    move_tokens(q + 1, p)
                wait_pair(vec, k.turned, q + 1, p)
                vec.tensor_copy(hidT.rearrange("p r n -> p (r n)"), k.ps[:, 7, 0:T]).then_inc(k.hidden_moved.sem, 1)
                if left > 1:
                    move_gated(q + 1, p)
                if left > 2:
                    build(q + 2, p)
                vec.wait_ge(k.used, n0 + down_at(q) + 2 + SLOTS * p)
                vec.tensor_copy(out[:, HALF:D], k.ps[:, 5, :]).then_inc(k.out_moved1.sem, 1)

            vec.sem_inc(turn_, 1)
            overflow(vec, general)
            build(0, 0)
            move_tokens(0, 0)
            move_gated(0, 0)
            build(1, 0)
            with vec.Fori(0, passes) as p:
                for s in range(UNROLL):
                    pair(s, p, 3)
            for q in range(PAIRS - UNROLL, PAIRS):
                pair(q, 0, PAIRS - q)
            vec.wait_ge(k.pe_done.sem, k.pe_done.at(1))

        @block.gpsimd
        def _(pool):
            k.pool_chain.link(pool, pool.memset(zeros, 0.0))
            pool.sem_inc(k.pool_done.sem, 1)
    for sig in (k.slots_built, k.gated_built, k.gathered, k.tokens_half0, k.tokens_half1, k.hidden_moved, k.gated_moved,
                k.silu_ready, k.hidden_ready, k.out_half, k.out_moved0, k.out_moved1):
        sig.close(PAIRS)
    k.turned.close(PAIRS + 1)
    k.pe_done.close(1)
    k.pool_done.close(1)


def moe_residual_phase(k, i):
    with k.nc.Block() as block:
        @block.vector
        def _(vec):
            link = lambda ins: k.vec_chain.link(vec, ins)
            add_gated(k, vec, link, 1, k.region[:, 0:TILES * D])


def qkv_phase(k, b):
    n0 = k.starts["qkv"]
    c = Carver(k.region, k.region_w)
    b.q, b.k = (c.take(len(GROUPS) * AH * T).rearrange("p (g h t) -> p g h t", g=len(GROUPS), h=AH) for _ in range(2))
    b.v = c.take(len(GROUPS) * TILES * D).rearrange("p (g t d) -> p g t d", g=len(GROUPS), t=TILES)
    b.o = v3(c.take(TILES * D), TILES, D)
    jobs = [(g, j) for g in range(len(GROUPS)) for j in range(3)]
    with k.nc.Block() as block:
        @block.sync
        def _(sp):
            ahead(k, sp, n0 + 4 * len(jobs))

        @block.tensor
        def _(pe):
            for n, (g, j) in enumerate(jobs):
                if n >= 2:
                    pe.wait_ge(k.act_done.sem, k.act_done.at(n - 1))
                if j < 2:
                    project_features(k, pe, n0 + 4 * n, k.xT, K8, n % 2)
                else:
                    project_tokens(k, pe, n0 + 4 * n, k.xT, K8, D, n % 2)

        @block.scalar
        def _(act):
            for n, (g, j) in enumerate(jobs):
                used_up(k, act, n0 + 4 * (n + 1))
                src = bank(k, 4 * (n % 2), 4)
                dst = (b.q[:, g], b.k[:, g], b.v[:, g])[j]
                act.activation(dst, v3(src, dst.shape[1], dst.shape[2]), ACT.Copy,
                               scale=ADH ** -0.5 if j == 0 else 1.0).then_inc(k.act_done.sem, 1)
    k.act_done.close(len(jobs))


def dilated_phase(k, b):
    G = len(GROUPS)
    s = Carver(k.arena, SLOTS * SLOT)
    away = s.take(G * TILES * T).rearrange("p (g t n) -> p g t n", g=G, t=TILES)
    diff = v3(s.take(TILES * T), TILES, T).bitcast(I32)
    rem = v3(s.take(TILES * T), TILES, T).bitcast(I32)
    tmp = v3(s.take(TILES * T), TILES, T)
    sc = s.take(TILES * G * T).rearrange("p (t g n) -> p t g n", t=TILES, g=G)
    pT = s.take(TILES * G * T).rearrange("p (t g n) -> p t g n", t=TILES, g=G)
    neg_max, den = s.take(TILES), s.take(TILES)
    slopes = [2.0 ** (-8.0 * (j + 1) / (G * AH)) for j in range(G * AH)]
    STEPS = 7
    turn_tile = (k.turn_tile0, k.turn_tile1)

    def turn(eng, tile, h, done):
        if h * STEPS + done:
            eng.wait_ge(turn_tile[tile].sem, turn_tile[tile].at(h * STEPS + done))

    with k.nc.Block() as block:
        @block.gpsimd
        def _(pool):
            k.pool_chain.link(pool, pool.iota(diff, pattern=[[-P, TILES], [1, T]], base=0, channel_multiplier=-1))
            pool.sem_inc(k.pool_done.sem, 1)

        @block.tensor
        def _(pe):
            for h in range(AH):
                for tile in range(TILES):
                    turn(pe, tile, h, 0)
                    for g in range(G):
                        mm = pe.matmul(k.ps[:, 4 * tile + g // 2, (g % 2) * T:(g % 2 + 1) * T],
                                       b.q[:, g, h, tile * P:(tile + 1) * P], b.k[:, g, h], start=True, stop=True)
                    mm.then_inc(turn_tile[tile].sem, 1)
                for tile in range(TILES):
                    turn(pe, tile, h, 3)
                    for g in range(G):
                        for n in range(TILES):
                            at = (g % 2) * T + n * P
                            mm = pe.transpose(k.ps[:, 4 * tile + 2 + g // 2, at:at + P], sc[:, tile, g, n * P:(n + 1) * P],
                                              k.ident[:, :])
                    mm.then_inc(turn_tile[tile].sem, 1)
                for tile in range(TILES):
                    turn(pe, tile, h, 5)
                    for g in range(G):
                        for n in range(TILES):
                            mm = pe.matmul(k.ps[:, 4 * tile, 0:ADH], pT[:, tile, g, n * P:(n + 1) * P],
                                           b.v[:, g, n, h * ADH:(h + 1) * ADH], start=(g == 0 and n == 0),
                                           stop=(g == G - 1 and n == TILES - 1))
                    mm.then_inc(turn_tile[tile].sem, 1)

        @block.scalar
        def _(act):
            for h in range(AH):
                for tile in range(TILES):
                    turn(act, tile, h, 2)
                    act.activation(sc[:, tile], sc[:, tile], ACT.Exp, bias=neg_max[:, tile:tile + 1],
                                   accum_out=den[:, tile:tile + 1]).then_inc(turn_tile[tile].sem, 1)
                for tile in range(TILES):
                    turn(act, tile, h, 4)
                    act.activation(pT[:, tile].rearrange("p g n -> p (g n)"), bank(k, 4 * tile + 2, 2)[:, 0:G * T],
                                   ACT.Copy).then_inc(turn_tile[tile].sem, 1)

        @block.vector
        def _(vec):
            link = lambda ins: k.vec_chain.link(vec, ins)
            mark = k.vec_chain.mark
            vec.wait_ge(k.pool_done.sem, k.pool_done.at(1))
            link(vec.tensor_copy(tmp, diff))
            link(vec.scalar_tensor_tensor(out=tmp, in0=tmp, scalar=-1.0, in1=tmp, op0=MUL, op1=MAX))
            for g, (window, dil) in enumerate(GROUPS):
                link(vec.tensor_scalar(away[:, g], tmp, float(window // 2), BIG * 100, ALU.is_gt, MUL))
                if dil > 1:
                    link(vec.tensor_scalar(rem, diff, dil - 1, None, ALU.bitwise_and))
                    link(vec.tensor_copy(sc[:, :, 0], rem))
                    link(vec.tensor_scalar(sc[:, :, 0], sc[:, :, 0], 0.0, BIG * 100, ALU.is_gt, MUL))
                    link(vec.tensor_tensor(away[:, g], away[:, g], sc[:, :, 0], ADD))
                link(vec.tensor_tensor(away[:, g], away[:, g], tmp, ADD))
            for h in range(AH):
                for tile in range(TILES):
                    turn(vec, tile, h, 1)
                    for g in range(G):
                        mark(vec.scalar_tensor_tensor(out=sc[:, tile, g], in0=away[:, g, tile], scalar=-slopes[g * AH + h],
                                                      in1=k.ps[:, 4 * tile + g // 2, (g % 2) * T:(g % 2 + 1) * T],
                                                      op0=MUL, op1=ADD))
                    vec.wait_ge(k.vec_chain.sem, k.vec_chain.n)
                    vec.tensor_reduce(neg_max[:, tile:tile + 1], sc[:, tile].rearrange("p g n -> p (g n)"), X, MAX,
                                      negate=True).then_inc(turn_tile[tile].sem, 1)
                for tile in range(TILES):
                    turn(vec, tile, h, 6)
                    link(vec.reciprocal(den[:, tile:tile + 1], den[:, tile:tile + 1]))
                    vec.tensor_scalar(b.o[:, tile, h * ADH:(h + 1) * ADH], k.ps[:, 4 * tile, 0:ADH], den[:, tile:tile + 1],
                                      None, MUL).then_inc(turn_tile[tile].sem, 1)
            for tile in range(TILES):
                turn(vec, tile, AH, 0)
    k.pool_done.close(1)
    for sig in turn_tile:
        sig.close(AH * STEPS)


def rms_rows_phase(k, gain):
    c = Carver(k.region, k.region_w)
    row, sq = c.take(D), c.take(D)
    ss = k.stat[:, 0:TILES]
    with k.nc.Block() as block:
        @block.sync
        def _(sp):
            sp.dma_start(row, gain.partition_broadcast(P)).then_inc(k.small_landed.sem, 16)

        @block.scalar
        def _(act):
            act.wait_ge(k.vec_done.sem, k.vec_done.at(1))
            act.activation(ss, ss, ACT.Sqrt).then_inc(k.act_done.sem, 1)

        @block.vector
        def _(vec):
            link = lambda ins: k.vec_chain.link(vec, ins)
            for tile in range(TILES):
                link(vec.tensor_tensor_reduce(sq, k.x[:, tile], k.x[:, tile], 1.0, 0.0, MUL, ADD, ss[:, tile:tile + 1]))
            link(vec.tensor_scalar(ss, ss, 1.0 / D, RMS_EPS, MUL, ADD))
            vec.sem_inc(k.vec_done.sem, 1)
            vec.wait_ge(k.small_landed.sem, k.small_landed.at(16))
            vec.wait_ge(k.act_done.sem, k.act_done.at(1))
            link(vec.reciprocal(ss, ss))
            for tile in range(TILES):
                link(vec.scalar_tensor_tensor(out=k.x[:, tile], in0=k.x[:, tile], scalar=ss[:, tile:tile + 1], in1=row,
                                              op0=MUL, op1=MUL))
    k.small_landed.close(16)
    k.vec_done.close(1)
    k.act_done.close(1)


def layer_norm_phase(k, gain, bias, n_used, extra=None):
    c = Carver(k.region, k.region_w)
    row, off, sq = c.take(D), c.take(D), c.take(D)
    sq1 = c.take(D)
    mean, var, minus = k.stat[:, 0:TILES], k.stat[:, TILES:2 * TILES], k.stat[:, 2 * TILES:2 * TILES + 1]
    with k.nc.Block() as block:
        @block.sync
        def _(sp):
            sp.dma_start(row, gain.partition_broadcast(P)).then_inc(k.small_landed.sem, 16)
            sp.dma_start(off, bias.partition_broadcast(P)).then_inc(k.small_landed.sem, 16)
            ahead(k, sp, n_used)

        @block.scalar
        def _(act):
            link = lambda ins: k.act_chain.link(act, ins)
            act.wait_ge(k.vec_done.sem, k.vec_done.at(1))
            link(act.activation(sq1, k.x[:, 1], ACT.Copy, accum_out=minus))
            link(act.activation(minus, minus, ACT.Copy, scale=-1.0 / D))
            link(act.activation(k.x[:, 1], k.x[:, 1], ACT.Identity, bias=minus))
            act.activation(sq1, k.x[:, 1], ACT.Square, accum_out=var[:, 1:2]).then_inc(k.act_done.sem, 1)
            act.wait_ge(k.vec_done.sem, k.vec_done.at(2))
            act.activation(var, var, ACT.Sqrt).then_inc(k.act_done.sem, 1)

        @block.vector
        def _(vec):
            link = lambda ins: k.vec_chain.link(vec, ins)
            mark = k.vec_chain.mark
            used_up(k, vec, n_used)
            for tile in reversed(range(TILES)):
                link(vec.scalar_tensor_tensor(out=k.x[:, tile], in0=k.x[:, tile], scalar=ALPHA, in1=bank(k, 2 * tile, 2),
                                              op0=MUL, op1=ADD))
                if extra is not None:
                    link(vec.tensor_tensor(k.x[:, tile], k.x[:, tile], extra[:, tile], ADD))
                if tile == 1:
                    vec.sem_inc(k.vec_done.sem, 1)
            link(vec.tensor_reduce(mean[:, 0:1], k.x[:, 0], X, ADD))
            link(vec.tensor_scalar(mean[:, 0:1], mean[:, 0:1], 1.0 / D, None, MUL))
            link(vec.tensor_scalar(k.x[:, 0], k.x[:, 0], mean[:, 0:1], None, SUB))
            link(vec.tensor_tensor_reduce(sq, k.x[:, 0], k.x[:, 0], 1.0, 0.0, MUL, ADD, var[:, 0:1]))
            vec.wait_ge(k.act_done.sem, k.act_done.at(1))
            link(vec.tensor_scalar(var, var, 1.0 / D, LN_EPS, MUL, ADD))
            vec.sem_inc(k.vec_done.sem, 1)
            vec.wait_ge(k.small_landed.sem, k.small_landed.at(32))
            vec.wait_ge(k.act_done.sem, k.act_done.at(2))
            link(vec.reciprocal(var, var))
            for tile in range(TILES):
                link(vec.scalar_tensor_tensor(out=k.x[:, tile], in0=k.x[:, tile], scalar=var[:, tile:tile + 1], in1=row,
                                              op0=MUL, op1=MUL))
            link(vec.tensor_tensor(k.x[:, :, :], k.x[:, :, :], v3(off, 1, D).to_broadcast([P, TILES, D]), ADD))
    k.small_landed.close(32)
    k.vec_done.close(2)
    k.act_done.close(2)


SLICES = ("dq", "dk", "sq", "sk", "iq")
SLOT_OF = {name: 4 * j for j, name in enumerate(SLICES)}
IK_SLOT = 4 * len(SLICES)


def second_buffers(k):
    c = Carver(k.region, k.region_w)
    b = Core()
    b.h = v3(c.take(TILES * SEG["ga"]), TILES, SEG["ga"])
    b.sg = c.take(2 * TILES * D).rearrange("p (j t d) -> p j t d", j=2, t=TILES)
    b.f = v3(c.take((IK_SLOT + 1) * T), IK_SLOT + 1, T)
    b.ya, b.yb = (v3(c.take(TILES * 4 * P), TILES, 4 * P) for _ in range(2))
    b.ik2 = v3(c.take(TILES * P), TILES, P)
    b.lam = c.take(4)
    b.end = c.at
    return b


def w_in_phase(k, b, i):
    n0 = k.starts[f"win{i}"]
    spans = [(0, D), (D, D), (2 * D, D), (3 * D, SEG["ga"] - 3 * D), (SEG["ga"], D), (SEG["gb"], D)]
    with k.nc.Block() as block:
        @block.sync
        def _(sp):
            ahead(k, sp, n0 + 4 * len(spans))

        @block.tensor
        def _(pe):
            for n, (c0, width) in enumerate(spans):
                if n >= 2:
                    pe.wait_ge(k.act_done.sem, k.act_done.at(n - 1))
                project_tokens(k, pe, n0 + 4 * n, k.xT, K8, width, n % 2)

        @block.scalar
        def _(act):
            for n, (c0, width) in enumerate(spans):
                used_up(k, act, n0 + 4 * (n + 1))
                src = v3(bank(k, 4 * (n % 2), 4), TILES, D)[:, :, 0:width]
                if n < 4:
                    ins = act.activation(b.h[:, :, c0:c0 + width], src, ACT.Copy)
                else:
                    ins = act.activation(b.sg[:, n - 4], src, ACT.Sigmoid)
                ins.then_inc(k.act_done.sem, 1)
    k.act_done.close(len(spans))


def rotary_phase(k, b, i):
    R2 = ROT // 2
    s = Carver(k.arena, SLOTS * SLOT)
    t1, t2, t3, t4 = (s.take(TILES * 16 * R2).rearrange("p (t h r) -> p t h r", t=TILES, r=R2) for _ in range(4))
    lp = v3(s.take(4 * HN), 4, HN)
    lt = v3(s.take(2 * HN), 2, HN)
    lam_init = 0.8 - 0.6 * math.exp(-0.3 * i)
    groups = [[(seg, j) for seg in SLICES for j in range(4)][g:g + 2] for g in range(0, IK_SLOT, 2)] + [[("ik", 0)]]
    with k.nc.Block() as block:
        @block.sync
        def _(sp):
            sp.dma_start(lp.rearrange("p j n -> p (j n)"),
                         k.a["diff_lambda_2"][i].rearrange("j n -> (j n)").partition_broadcast(P)).then_inc(k.small_landed.sem, 16)

        @block.vector
        def _(vec):
            link = lambda ins: k.vec_chain.link(vec, ins)
            mark = k.vec_chain.mark
            for c0, heads in ((SEG["dq"], 16), (SEG["sq"], 16), (SEG["iq"], 9)):
                v = b.h[:, :, c0:c0 + heads * HN].rearrange("p t (h n) -> p t h n", n=HN)
                x1, x2 = v[:, :, :, 0:R2], v[:, :, :, R2:ROT]
                cos, sin = (tab[:, :, :].rearrange("p t (a r) -> p t a r", a=1).to_broadcast([P, TILES, heads, R2])
                            for tab in (k.cos, k.sin))
                a1, a2, a3, a4 = (t[:, :, 0:heads] for t in (t1, t2, t3, t4))
                mark(vec.tensor_tensor(a1, x1, cos, MUL))
                mark(vec.tensor_tensor(a2, x2, sin, MUL))
                mark(vec.tensor_tensor(a3, x2, cos, MUL))
                link(vec.tensor_tensor(a4, x1, sin, MUL))
                mark(vec.tensor_tensor(x1, a1, a2, SUB))
                link(vec.tensor_tensor(x2, a3, a4, ADD))
            for r in range(2):
                mark(vec.tensor_copy(b.ik2[:, :, r * HN:(r + 1) * HN], b.h[:, :, SEG["ik"]:SEG["ik"] + HN]))
            vec.wait_ge(k.vec_chain.sem, k.vec_chain.n)
            vec.sem_inc(k.vec_done.sem, 1)
            vec.wait_ge(k.small_landed.sem, k.small_landed.at(16))
            l4 = lp.rearrange("p (a b) n -> p a b n", b=2)
            link(vec.tensor_tensor(lt, l4[:, :, 0], l4[:, :, 1], MUL))
            link(vec.tensor_reduce(b.lam[:, 0:2], lt, X, ADD))
            vec.sem_inc(k.vec_done.sem, 1)
            vec.wait_ge(k.act_done.sem, k.act_done.at(1))
            link(vec.tensor_tensor(b.lam[:, 2:3], b.lam[:, 1:2], b.lam[:, 0:1], SUB))
            link(vec.tensor_scalar(b.lam[:, 2:3], b.lam[:, 2:3], -lam_init, None, ADD))

        @block.tensor
        def _(pe):
            pe.wait_ge(k.vec_done.sem, k.vec_done.at(1))
            for g, members in enumerate(groups):
                if g >= 8:
                    pe.wait_ge(k.act_done.sem, k.act_done.at(1 + g - 7))
                for m, (seg, j) in enumerate(members):
                    for tile in range(TILES):
                        src = b.ik2[:, tile] if seg == "ik" else b.h[:, tile, SEG[seg] + j * P:SEG[seg] + (j + 1) * P]
                        at = m * T + tile * P
                        mm = pe.transpose(k.ps[:, g % 8, at:at + P], src, k.ident[:, :])
                mm.then_inc(k.pe_done.sem, 1)

        @block.scalar
        def _(act):
            act.wait_ge(k.vec_done.sem, k.vec_done.at(2))
            act.activation(b.lam[:, 0:2], b.lam[:, 0:2], ACT.Exp).then_inc(k.act_done.sem, 1)
            for g, members in enumerate(groups):
                act.wait_ge(k.pe_done.sem, k.pe_done.at(g + 1))
                n = len(members)
                act.activation(b.f[:, 2 * g:2 * g + n], v3(k.ps[:, g % 8, 0:n * T], n, T), ACT.Copy).then_inc(k.act_done.sem, 1)
    k.small_landed.close(16)
    k.vec_done.close(2)
    k.pe_done.close(len(groups))
    k.act_done.close(1 + len(groups))


def pair_attention_phase(k, b, i):
    s = Carver(k.arena, SLOTS * SLOT)
    causal = v3(s.take(TILES * T), TILES, T)
    mask = v3(s.take(TILES * T), TILES, T)
    work, best = v3(s.take(TILES * T), TILES, T), v3(s.take(TILES * 8), TILES, 8)
    relu = s.take(TILES * 8 * T).rearrange("p (t h n) -> p t h n", t=TILES, h=8)
    iw = v3(s.take(TILES * SH), TILES, SH)
    sc = s.take(TILES * 2 * T).rearrange("p (t w n) -> p t w n", t=TILES, w=2)
    pT = s.take(TILES * 2 * T).rearrange("p (t w n) -> p t w n", t=TILES, w=2)
    neg_max, den = v3(s.take(TILES * 2), TILES, 2), v3(s.take(TILES * 2), TILES, 2)
    scale = HN ** -0.5
    IDX, STEPS = 2, 8
    PIECES = 6
    assert 3 * DH == TILES * PIECES
    turn_tile = (k.turn_tile0, k.turn_tile1)

    def turn(eng, tile, unit_, done):
        n = IDX + unit_ * STEPS + done
        eng.wait_ge(turn_tile[tile].sem, turn_tile[tile].at(n))

    def end(ins, tile):
        ins.then_inc(turn_tile[tile].sem, 1)

    def keys(tile):
        return (tile + 1) * P

    with k.nc.Block() as block:
        @block.gpsimd
        def _(pool):
            k.pool_chain.link(pool, pool.memset(causal, 0.0))
            for tile in range(TILES):
                k.pool_chain.link(pool, pool.affine_select(out=causal[:, tile], in_=causal[:, tile], pattern=[[-1, T]],
                                                           compare_op=ALU.is_ge, fill=-BIG, base=tile * P,
                                                           channel_multiplier=1))
            pool.sem_inc(k.pool_done.sem, 1)

        @block.tensor
        def _(pe):
            for tile in range(TILES):
                for hd in range(SH):
                    par, pair = hd % 2, hd // 2
                    half = slice(par * HN, (par + 1) * HN)
                    mm = pe.matmul(k.ps[:, 4 * tile + 2 * par + pair // 2, (pair % 2) * T:(pair % 2) * T + keys(tile)],
                                   b.f[half, SLOT_OF["iq"] + pair, tile * P:(tile + 1) * P], b.f[half, IK_SLOT, 0:keys(tile)],
                                   start=True, stop=True)
                end(mm, tile)
            for u in range(DH + SH // 2):
                qs, ks = (SLOT_OF["dq"] + u, SLOT_OF["dk"] + u) if u < DH else (SLOT_OF["sq"] + u - DH, SLOT_OF["sk"] + u - DH)
                for tile in range(TILES):
                    turn(pe, tile, u, 0)
                    for w in range(2):
                        half = slice(w * HN, (w + 1) * HN)
                        mm = pe.matmul(k.ps[:, 4 * tile + w, 0:keys(tile)], b.f[half, qs, tile * P:(tile + 1) * P],
                                       b.f[half, ks, 0:keys(tile)], start=True, stop=True)
                    end(mm, tile)
                for tile in range(TILES):
                    turn(pe, tile, u, 4)
                    for w in range(1 if u < DH else 2):
                        for n in range(tile + 1):
                            at = w * T + n * P
                            mm = pe.transpose(k.ps[:, 4 * tile + 2, at:at + P], sc[:, tile, w, n * P:(n + 1) * P], k.ident[:, :])
                    end(mm, tile)
                for tile in range(TILES):
                    turn(pe, tile, u, 6)
                    for w in range(1 if u < DH else 2):
                        width = P if u < DH else HN
                        c0 = SEG["dv"] + u * P if u < DH else SEG["sv"] + ((u - DH) * 2 + w) * HN
                        for n in range(tile + 1):
                            mm = pe.matmul(k.ps[:, 4 * tile + 3, w * HN:w * HN + width], pT[:, tile, w, n * P:(n + 1) * P],
                                           b.h[:, n, c0:c0 + width], start=(n == 0), stop=(n == tile))
                    end(mm, tile)

        @block.scalar
        def _(act):
            for tile in range(TILES):
                act.wait_ge(turn_tile[tile].sem, turn_tile[tile].at(1))
                end(act.activation(relu[:, tile, :, 0:keys(tile)], v3(bank(k, 4 * tile, 4), 8, T)[:, :, 0:keys(tile)],
                                   ACT.Relu, scale=scale), tile)
            for u in range(DH + SH // 2):
                for tile in range(TILES):
                    turn(act, tile, u, 2)
                    for w in range(2):
                        k.act_chain.mark(act.activation(sc[:, tile, w, 0:keys(tile)], sc[:, tile, w, 0:keys(tile)], ACT.Exp,
                                                        bias=neg_max[:, tile, w:w + 1], accum_out=den[:, tile, w:w + 1]))
                    act.wait_ge(k.act_chain.sem, k.act_chain.n)
                    act.sem_inc(turn_tile[tile].sem, 1)
                for tile in range(TILES):
                    turn(act, tile, u, 5)
                    n = 1 if u < DH else 2
                    end(act.activation(pT[:, tile, 0:n, 0:keys(tile)], v3(k.ps[:, 4 * tile + 2, 0:n * T], n, T)[:, :, 0:keys(tile)],
                                       ACT.Copy), tile)

        @block.vector
        def _(vec):
            link = lambda ins: k.vec_chain.link(vec, ins)
            mark = k.vec_chain.mark
            link(vec.tensor_scalar(iw, b.h[:, :, SEG["iw"]:SEG["iw"] + SH], SH ** -0.5, None, MUL))
            vec.wait_ge(k.pool_done.sem, k.pool_done.at(1))

            def select(piece):
                tile, m = piece // PIECES, piece % PIECES
                n = keys(tile)
                wk = work[:, tile, 0:n]
                if m == 0:
                    vec.wait_ge(turn_tile[tile].sem, turn_tile[tile].at(2))
                if m < 2:
                    for hd in range(m * SH // 2, (m + 1) * SH // 2):
                        r = relu[:, tile, (hd % 2) * 4 + hd // 2, 0:n]
                        if hd == 0:
                            link(vec.tensor_scalar(wk, r, iw[:, tile, 0:1], None, MUL))
                        else:
                            link(vec.scalar_tensor_tensor(out=wk, in0=r, scalar=iw[:, tile, hd:hd + 1], in1=wk, op0=MUL, op1=ADD))
                    if m == 1:
                        link(vec.tensor_tensor(wk, wk, causal[:, tile, 0:n], ADD))
                else:
                    for _ in range(TOPK // 8 // (PIECES - 2)):
                        link(vec.max(best[:, tile], wk))
                        link(vec.match_replace(wk, best[:, tile], wk, -3e38))
                if m == PIECES - 1:
                    link(vec.tensor_scalar(mask[:, tile, 0:n], wk, -2e38, -BIG, ALU.is_gt, MUL))
                    link(vec.tensor_tensor(mask[:, tile, 0:n], mask[:, tile, 0:n], causal[:, tile, 0:n], ADD))

            for u in range(DH + SH // 2):
                hide = causal if u < DH else mask
                for tile in range(TILES):
                    turn(vec, tile, u, 1)
                    n = keys(tile)
                    link(vec.scalar_tensor_tensor(out=sc[:, tile, :, 0:n], in0=k.ps[:, 4 * tile:4 * tile + 2, 0:n], scalar=scale,
                                                  in1=hide[:, tile:tile + 1, 0:n].to_broadcast([P, 2, n]), op0=MUL, op1=ADD))
                    end(vec.tensor_reduce(neg_max[:, tile], sc[:, tile, :, 0:n], X, MAX, negate=True), tile)
                if u < DH:
                    select(3 * u)
                for tile in range(TILES):
                    turn(vec, tile, u, 3)
                    n = keys(tile)
                    link(vec.reciprocal(den[:, tile], den[:, tile]))
                    if u < DH:
                        link(vec.tensor_tensor(den[:, tile, 1:2], den[:, tile, 1:2], b.lam[:, 2:3], MUL))
                        link(vec.tensor_scalar(sc[:, tile, 0, 0:n], sc[:, tile, 0, 0:n], den[:, tile, 0:1], None, MUL))
                        end(vec.scalar_tensor_tensor(out=sc[:, tile, 0, 0:n], in0=sc[:, tile, 1, 0:n], scalar=den[:, tile, 1:2],
                                                     in1=sc[:, tile, 0, 0:n], op0=MUL, op1=ADD), tile)
                    else:
                        vec.sem_inc(turn_tile[tile].sem, 1)
                if u < DH:
                    select(3 * u + 1)
                for tile in range(TILES):
                    turn(vec, tile, u, 7)
                    src = k.ps[:, 4 * tile + 3, 0:P]
                    if u < DH:
                        end(vec.tensor_copy(b.ya[:, tile, u * P:(u + 1) * P], src), tile)
                    else:
                        end(vec.tensor_tensor(v3(b.yb[:, tile, (u - DH) * P:(u - DH + 1) * P], 2, HN), v3(src, 2, HN),
                                              den[:, tile].rearrange("p (w a) -> p w a", a=1).to_broadcast([P, 2, HN]), MUL), tile)
                if u < DH:
                    select(3 * u + 2)
    k.pool_done.close(1)
    for sig in turn_tile:
        sig.close(IDX + (DH + SH // 2) * STEPS)


def subnorm_phase(k, b, i, end):
    lam_init = 0.8 - 0.6 * math.exp(-0.3 * i)
    c = Carver(k.region, k.region_w, b.end)
    gain = c.take(P)
    rms = c.take(TILES * DH)
    sq = v3(b.f[:, 0:4].rearrange("p s t -> p (s t)"), TILES * DH, P)
    y = b.ya.rearrange("p t (h n) -> p (t h) n", n=P)
    with k.nc.Block() as block:
        @block.sync
        def _(sp):
            sp.dma_start(gain, k.a["diff_subln_g_2"][i].partition_broadcast(P)).then_inc(k.small_landed.sem, 16)
            ahead(k, sp, end)

        @block.scalar
        def _(act):
            act.wait_ge(k.vec_done.sem, k.vec_done.at(1))
            act.activation(rms, rms, ACT.Sqrt).then_inc(k.act_done.sem, 1)

        @block.vector
        def _(vec):
            link = lambda ins: k.vec_chain.link(vec, ins)
            link(vec.tensor_tensor(sq, y, y, MUL))
            link(vec.tensor_reduce(rms, sq, X, ADD))
            link(vec.tensor_scalar(rms, rms, 1.0 / P, LN_EPS, MUL, ADD))
            vec.sem_inc(k.vec_done.sem, 1)
            vec.wait_ge(k.act_done.sem, k.act_done.at(1))
            link(vec.reciprocal(rms, rms))
            link(vec.tensor_scalar(rms, rms, 1.0 - lam_init, None, MUL))
            link(vec.tensor_tensor(y, y, rms.rearrange("p (h a) -> p h a", a=1).to_broadcast([P, TILES * DH, P]), MUL))
            vec.wait_ge(k.small_landed.sem, k.small_landed.at(16))
            link(vec.tensor_tensor(y, y, v3(gain, 1, P).to_broadcast([P, TILES * DH, P]), MUL))
    k.small_landed.close(16)
    k.vec_done.close(1)
    k.act_done.close(1)


def two_products_phase(k, names, lhs, rows, finish):
    n0, n1 = (k.starts[n] for n in names)
    per = min(2, rows[1] // 2)
    end = n1 + rows[1] // per
    with k.nc.Block() as block:
        @block.sync
        def _(sp):
            ahead(k, sp, end)

        @block.tensor
        def _(pe):
            project_tokens(k, pe, n0, lhs[0], rows[0], D, 0)
            project_tokens(k, pe, n1, lhs[1], rows[1], D, 1, per)

        finish(block, n1, end)


def second_layer_phases(k, i):
    a = k.a
    b = second_buffers(k)
    w_in_phase(k, b, i)
    rotary_phase(k, b, i)
    pair_attention_phase(k, b, i)
    subnorm_phase(k, b, i, k.starts[f"wbd{i}"])
    yaT, ybT = b.f[:, 0:4], b.f[:, 4:8]
    to_features_phase(k, b.ya, yaT, 4, k.starts[f"wbd{i}"])
    to_features_phase(k, b.yb, ybT, 4, k.starts[f"wbd{i}"])
    merged = v3(k.region[:, 0:TILES * D], TILES, D)
    mergedT = v3(k.region[:, TILES * D:2 * TILES * D], K8, T)

    def merge(block, first, end):
        @block.vector
        def _(vec):
            link = lambda ins: k.vec_chain.link(vec, ins)
            used_up(k, vec, first)
            link(vec.tensor_tensor(merged, v3(bank(k, 0, 4), TILES, D), b.sg[:, 0], MUL))
            used_up(k, vec, end)
            link(vec.tensor_tensor(b.sg[:, 1], v3(bank(k, 4, 4), TILES, D), b.sg[:, 1], MUL))
            link(vec.tensor_tensor(merged, merged, b.sg[:, 1], ADD))

    two_products_phase(k, (f"wbd{i}", f"wbs{i}"), (yaT, ybT), (4, 4), merge)
    to_features_phase(k, merged, mergedT, K8, k.starts[f"wout{i}"])
    n0 = k.starts[f"wout{i}"]
    c = Carver(k.region, k.region_w, k.region_w - 2 * TILES * D)
    ple = v3(c.take(TILES * D), TILES, D)
    p_tok, pT = v3(c.take(TILES * T), TILES, T), v3(c.take(2 * T), 2, T)
    with k.nc.Block() as block:
        @block.sync
        def _(sp):
            sp.dma_start(p_tok, a["p_2"][i, 0].rearrange("(t p) d -> p t d", p=P)).then_inc(k.early_landed.sem, 16)
            ahead(k, sp, n0 + 4)

        @block.tensor
        def _(pe):
            project_tokens(k, pe, n0, mergedT, K8, D, 0)
    layer_norm_phase(k, a["ln1_g_2"][i], a["ln1_b_2"][i], n0 + 4)
    to_features_phase(k, k.x, k.xT, K8, k.starts[f"pleg{i}"])

    to_features_phase(k, p_tok, pT, 2, k.starts[f"pleg{i}"], loaded=16)

    def embed(block, first, end):
        @block.scalar
        def _(act):
            used_up(k, act, first)
            act.activation(ple, v3(bank(k, 0, 4), TILES, D), ACT.Sigmoid).then_inc(k.act_done.sem, 1)

        @block.vector
        def _(vec):
            vec.wait_ge(k.act_done.sem, k.act_done.at(1))
            used_up(k, vec, end)
            k.vec_chain.link(vec, vec.tensor_tensor(ple, ple, v3(bank(k, 4, 4), TILES, D), MUL))

    two_products_phase(k, (f"pleg{i}", f"ple{i}"), (k.xT, pT), (K8, 2), embed)
    k.act_done.close(1)
    route_phase(k, DEPTH + i, k.starts[f"moe{DEPTH + i}"])
    experts_phase(k, DEPTH + i)
    layer_norm_phase(k, a["ln2_g_2"][i], a["ln2_b_2"][i], k.starts[f"moe{DEPTH + i}"] + 3 * EXPERTS, extra=ple)


def build(nc, a, out, upto=None):
    with ExitStack() as ctx:
        k = make_core(nc, ctx, a)
        phases = []
        rwkv = rwkv_buffers(k)

        def phase(name, f):
            phases.append((name, f))

        for i in range(DEPTH):
            phase(f"ada{i}", lambda i=i: ada_phase(k, i, early=rwkv.early if i == 0 else ()))
            first = "rkv0" if i == 0 else "qkv"
            phase(f"norm_tm{i}", lambda i=i, f=first: to_features_phase(k, k.x, k.xT, K8, k.starts[f], norm=0))
            if i == 0:
                def mix():
                    b = rwkv
                    rwkv_project_phase(k, b)
                    og = rwkv_mix_phase(k, b)
                    k.mixT = v3(k.region[:, b.end:b.end + T * K8], K8, T)
                    to_features_phase(k, og, k.mixT, K8, k.starts["rwo"])
                    residual_phase(k, "rwo", k.mixT, 0)
                phase("rwkv", mix)

            else:
                def mix():
                    b = Core()
                    qkv_phase(k, b)
                    dilated_phase(k, b)
                    mixT = v3(k.region[:, 0:T * K8], K8, T)
                    to_features_phase(k, b.o, mixT, K8, k.starts["awo"])
                    residual_phase(k, "awo", mixT, 0)
                phase("dilated", mix)

            def moe(i=i):
                to_features_phase(k, k.x, k.xT, K8, k.starts[f"moe{i}"], norm=1)
                route_phase(k, i, k.starts[f"moe{i}"])
                experts_phase(k, i)
                moe_residual_phase(k, i)
            phase(f"moe{i}", moe)
        phase("final", lambda: rms_rows_phase(k, a["final_g"]))
        for i in range(DEPTH):
            phase(f"second_x{i}", lambda i=i: to_features_phase(k, k.x, k.xT, K8, k.starts[f"win{i}"]))
            phase(f"second{i}", lambda i=i: second_layer_phases(k, i))
        setup_phase(k)
        for name, f in phases:
            f()
            if name == upto:
                break
        src = k.x
        with nc.Block() as block:
            @block.sync
            def _(sp):
                sp.dma_start(out.rearrange("b (t p) d -> p (b t) d", p=P), src[:, :, :]).then_inc(k.stored.sem, 16)
                sp.wait_ge(k.stored.sem, k.stored.at(16))


def kernel(**inputs):
    import numpy as _np
    import concourse.bacc as _bacc
    from concourse import mybir as _mybir
    from concourse.bass_utils import run_bass_kernel_spmd as _run

    nc = _bacc.Bacc("TRN2", target_bir_lowering=False, num_devices=1)
    arrays, args = {}, {}
    for name, value in inputs.items():
        v = _np.ascontiguousarray(value)
        arrays[f"in_{name}"] = v
        args[name] = nc.dram_tensor(f"in_{name}", v.shape, _mybir.dt.from_np(v.dtype), kind="ExternalInput").ap()
    out = nc.dram_tensor("out", (1, T, D), F32, kind="ExternalOutput").ap()
    build(nc, args, out)
    r = _run(nc, [arrays], core_ids=[0])
    return r.results[0]["out"]
```
